# Optimizing a Trainium2 kernel written in Bass

```python
import math
import jax
import jax.numpy as jnp
from jax import lax
import numpy as np

D_MODEL = 1024
BATCH = 1
SEQ = 256
DEPTH = 1

CHUNK = 64
EPS = 1e-6

ATTN_HEAD_DIM = 64
ATTN_WIDTH = D_MODEL // 2
ATTN_HEADS = ATTN_WIDTH // ATTN_HEAD_DIM
LEFT_CHUNKS = 8
BAND = (LEFT_CHUNKS + 1) * CHUNK
REL_CLIP = 128
N_REL = 2 * REL_CLIP + 1

DN_HEAD_DIM = 128
DN_WIDTH = D_MODEL - ATTN_WIDTH
DN_HEADS = DN_WIDTH // DN_HEAD_DIM
CONV_WIDTH = 4

MIX_WIDTH = ATTN_WIDTH + DN_WIDTH
IN_PROJ_WIDTH = 3 * ATTN_WIDTH + 4 * DN_WIDTH + 2 * DN_HEADS

PEER_HEADS = 8
PEER_KEY_DIM = 256
PEER_HALF = PEER_KEY_DIM // 2
N_KEYS = 128
N_EXPERTS = N_KEYS * N_KEYS
PEER_TOPK = 16
PEER_BLOCK = 128


def rms_norm(x, gain):
    xf = x.astype(jnp.float32)
    y = xf * lax.rsqrt(jnp.mean(xf * xf, axis=-1, keepdims=True) + EPS)
    return (y * gain.astype(jnp.float32)).astype(x.dtype)

def l2_norm(x):
    xf = x.astype(jnp.float32)
    return xf * lax.rsqrt(jnp.sum(xf * xf, axis=-1, keepdims=True) + EPS)

def modulate(h, shift, scale):
    return h * (1.0 + scale) + shift

def chunked_band_attention(q, k, v, q_gain, k_gain, rel_bias):
    B, S = q.shape[:2]
    nc = S // CHUNK
    shp = (B, nc, CHUNK, ATTN_HEADS, ATTN_HEAD_DIM)
    pad = ((0, 0), (LEFT_CHUNKS, 0), (0, 0), (0, 0), (0, 0))
    q = rms_norm(q, q_gain).reshape(shp)
    k = jnp.pad(rms_norm(k, k_gain).reshape(shp), pad)
    v = jnp.pad(v.reshape(shp), pad)
    band_idx = np.arange(nc)[:, None] + np.arange(LEFT_CHUNKS + 1)[None, :]
    kb = k[:, band_idx].reshape(B, nc, BAND, ATTN_HEADS, ATTN_HEAD_DIM)
    vb = v[:, band_idx].reshape(B, nc, BAND, ATTN_HEADS, ATTN_HEAD_DIM)
    scores = jnp.einsum("bnqhd,bnkhd->bhnqk", q, kb,
                        preferred_element_type=jnp.float32) * (ATTN_HEAD_DIM ** -0.5)
    rel = np.arange(CHUNK)[:, None] + LEFT_CHUNKS * CHUNK - np.arange(BAND)[None, :]
    rel_idx = np.clip(rel, -REL_CLIP, REL_CLIP) + REL_CLIP
    bias = rel_bias.astype(jnp.float32)[:, rel_idx]
    valid = (np.arange(nc)[:, None] + np.arange(BAND)[None, :] // CHUNK) >= LEFT_CHUNKS
    scores = jnp.where(valid[None, None, :, None, :], scores + bias[None, :, None], -jnp.inf)
    p = jax.nn.softmax(scores, axis=-1).astype(vb.dtype)
    o = jnp.einsum("bhnqk,bnkhd->bnqhd", p, vb)
    return o.reshape(B, S, ATTN_WIDTH)

def causal_depthwise_conv(x, w):
    S = x.shape[1]
    xp = jnp.pad(x, ((0, 0), (CONV_WIDTH - 1, 0), (0, 0)))
    y = xp[:, 0:S] * w[0]
    for i in range(1, CONV_WIDTH):
        y = y + xp[:, i:i + S] * w[i]
    return jax.nn.silu(y)

def gated_delta_rule(q, k, v, g, beta):
    B, S, H, Dk = q.shape
    Dv = v.shape[-1]
    nc = S // CHUNK

    def to_chunks(t):
        return t.astype(jnp.float32).reshape(B, nc, CHUNK, H, -1).transpose(1, 0, 3, 2, 4)

    q = to_chunks(q) * (Dk ** -0.5)
    k = to_chunks(k)
    v = to_chunks(v)
    g = g.astype(jnp.float32).reshape(B, nc, CHUNK, H).transpose(1, 0, 3, 2)
    beta = beta.astype(jnp.float32).reshape(B, nc, CHUNK, H).transpose(1, 0, 3, 2)
    gc = jnp.cumsum(g, axis=-1)
    tri = np.tril(np.ones((CHUNK, CHUNK), dtype=bool))
    strict = np.tril(np.ones((CHUNK, CHUNK), dtype=bool), -1)
    decay = jnp.exp(jnp.where(tri, gc[..., :, None] - gc[..., None, :], -jnp.inf))
    k_beta = k * beta[..., None]
    v_beta = v * beta[..., None]
    lower = jnp.where(strict, jnp.einsum("nbhid,nbhjd->nbhij", k_beta, k) * decay, 0.0)
    rhs = jnp.concatenate([v_beta, k_beta * jnp.exp(gc)[..., None]], axis=-1)
    sol = lax.linalg.triangular_solve(jnp.eye(CHUNK, dtype=jnp.float32) + lower, rhs,
                                      left_side=True, lower=True, unit_diagonal=True)
    u = sol[..., :Dv]
    w = sol[..., Dv:]
    intra = jnp.einsum("nbhid,nbhjd->nbhij", q, k) * decay

    def step(state, xs):
        q_c, k_c, u_c, w_c, a_c, g_c = xs
        v_new = u_c - jnp.einsum("bhcd,bhde->bhce", w_c, state)
        o = (jnp.einsum("bhcd,bhde->bhce", q_c * jnp.exp(g_c)[..., None], state)
             + jnp.einsum("bhij,bhje->bhie", a_c, v_new))
        g_last = g_c[..., -1]
        k_dec = k_c * jnp.exp(g_last[..., None] - g_c)[..., None]
        state = state * jnp.exp(g_last)[..., None, None] + jnp.einsum("bhcd,bhce->bhde", k_dec, v_new)
        return state, o

    state0 = jnp.zeros((B, H, Dk, Dv), jnp.float32)
    _, o = lax.scan(step, state0, (q, k, u, w, intra, gc))
    return o.transpose(1, 0, 3, 2, 4).reshape(B, S, H, Dv)

def peer(h, w_query, query_gain, sub_keys_1, sub_keys_2, expert_down, expert_up):
    B, S, D = h.shape
    n_blocks = (B * S) // PEER_BLOCK

    def block(hb):
        qry = (hb @ w_query).reshape(PEER_BLOCK, PEER_HEADS, PEER_KEY_DIM)
        qry = rms_norm(qry, query_gain)
        s1 = jnp.einsum("thd,nd->thn", qry[..., :PEER_HALF], sub_keys_1, preferred_element_type=jnp.float32)
        s2 = jnp.einsum("thd,nd->thn", qry[..., PEER_HALF:], sub_keys_2, preferred_element_type=jnp.float32)
        v1, i1 = lax.top_k(s1, PEER_TOPK)
        v2, i2 = lax.top_k(s2, PEER_TOPK)
        cand_s = (v1[..., :, None] + v2[..., None, :]).reshape(PEER_BLOCK, PEER_HEADS, PEER_TOPK * PEER_TOPK)
        cand_i = (i1[..., :, None] * N_KEYS + i2[..., None, :]).reshape(PEER_BLOCK, PEER_HEADS, PEER_TOPK * PEER_TOPK)
        top_s, pos = lax.top_k(cand_s, PEER_TOPK)
        experts = jnp.take_along_axis(cand_i, pos, axis=-1)
        gates = jax.nn.softmax(top_s, axis=-1)
        u = expert_down[experts]
        vv = expert_up[experts]
        act = jax.nn.gelu(jnp.einsum("thkd,td->thk", u, hb, preferred_element_type=jnp.float32),
                          approximate=False)
        return jnp.einsum("thk,thkd->td", (gates * act).astype(vv.dtype), vv)

    out = lax.map(block, h.reshape(n_blocks, PEER_BLOCK, D))
    return out.reshape(B, S, D)

def hybrid_layer(x, c, w_ada, b_ada, norm1_gain, w_in, attn_q_gain, attn_k_gain, attn_rel_bias,
                 attn_out_gain, dn_conv_w, dn_a_log, dn_dt_bias, dn_out_gain, w_out, norm2_gain,
                 peer_w_query, peer_query_gain, peer_sub_keys_1, peer_sub_keys_2,
                 peer_expert_down, peer_expert_up):
    B, S, _ = x.shape
    mod = jax.nn.silu(c) @ w_ada + b_ada
    shift1, scale1, gate1, shift2, scale2, gate2 = [m[:, None, :] for m in jnp.split(mod, 6, axis=-1)]

    h = modulate(rms_norm(x, norm1_gain), shift1, scale1)
    proj = h @ w_in
    cuts = [ATTN_WIDTH, 2 * ATTN_WIDTH, 3 * ATTN_WIDTH, 3 * ATTN_WIDTH + 3 * DN_WIDTH,
            3 * ATTN_WIDTH + 4 * DN_WIDTH, 3 * ATTN_WIDTH + 4 * DN_WIDTH + DN_HEADS]
    qa, ka, va, qkv_b, z_b, b_raw, a_raw = jnp.split(proj, cuts, axis=-1)

    hd_a = (B, S, ATTN_HEADS, ATTN_HEAD_DIM)
    o_a = chunked_band_attention(qa.reshape(hd_a), ka.reshape(hd_a), va.reshape(hd_a),
                                 attn_q_gain, attn_k_gain, attn_rel_bias)
    o_a = rms_norm(o_a, attn_out_gain)

    qkv_b = causal_depthwise_conv(qkv_b, dn_conv_w)
    q_b, k_b, v_b = jnp.split(qkv_b, 3, axis=-1)
    hd_b = (B, S, DN_HEADS, DN_HEAD_DIM)
    q_b = l2_norm(q_b.reshape(hd_b))
    k_b = l2_norm(k_b.reshape(hd_b))
    beta = jax.nn.sigmoid(b_raw.astype(jnp.float32))
    g = -jnp.exp(dn_a_log.astype(jnp.float32)) * jax.nn.softplus(
        a_raw.astype(jnp.float32) + dn_dt_bias.astype(jnp.float32))
    o_b = gated_delta_rule(q_b, k_b, v_b.reshape(hd_b), g, beta)
    o_b = rms_norm(o_b, dn_out_gain) * jax.nn.silu(z_b.reshape(hd_b).astype(jnp.float32))
    o_b = o_b.reshape(B, S, DN_WIDTH).astype(x.dtype)

    mix = jnp.concatenate([o_a, o_b], axis=-1) @ w_out
    x = x + gate1 * mix

    h2 = modulate(rms_norm(x, norm2_gain), shift2, scale2)
    y = peer(h2, peer_w_query, peer_query_gain, peer_sub_keys_1, peer_sub_keys_2,
             peer_expert_down, peer_expert_up)
    return x + gate2 * y

def first_inputs(seed: int = 0) -> dict:
    key = jax.random.key(seed)
    ks = iter(jax.random.split(key, 32))
    L = DEPTH

    def nrm(shape, scale):
        return scale * jax.random.normal(next(ks), shape, jnp.float32)

    def gain(shape):
        return 1.0 + nrm(shape, 0.02)

    x = nrm((BATCH, SEQ, D_MODEL), 1.0)
    c = nrm((BATCH, D_MODEL), 1.0)
    w_ada = nrm((L, D_MODEL, 6 * D_MODEL), 0.5 * D_MODEL ** -0.5)
    b_ada = nrm((L, 6 * D_MODEL), 0.02)
    norm1_gain = gain((L, D_MODEL))
    w_in = nrm((L, D_MODEL, IN_PROJ_WIDTH), D_MODEL ** -0.5)
    attn_q_gain = gain((L, ATTN_HEAD_DIM))
    attn_k_gain = gain((L, ATTN_HEAD_DIM))
    attn_rel_bias = nrm((L, ATTN_HEADS, N_REL), 0.5)
    attn_out_gain = gain((L, ATTN_WIDTH))
    dn_conv_w = nrm((L, CONV_WIDTH, 3 * DN_WIDTH), CONV_WIDTH ** -0.5)
    dn_a_log = jnp.log(jax.random.uniform(next(ks), (L, DN_HEADS), jnp.float32, 1.0, 16.0))
    dt = jnp.exp(jax.random.uniform(next(ks), (L, DN_HEADS), jnp.float32,
                                    math.log(1e-3), math.log(1e-1)))
    dn_dt_bias = dt + jnp.log(-jnp.expm1(-dt))
    dn_out_gain = gain((L, DN_HEAD_DIM))
    w_out = nrm((L, MIX_WIDTH, D_MODEL), MIX_WIDTH ** -0.5)
    norm2_gain = gain((L, D_MODEL))
    peer_w_query = nrm((L, D_MODEL, PEER_HEADS * PEER_KEY_DIM), D_MODEL ** -0.5)
    peer_query_gain = gain((L, PEER_KEY_DIM))
    peer_sub_keys_1 = nrm((L, N_KEYS, PEER_HALF), PEER_HALF ** -0.5)
    peer_sub_keys_2 = nrm((L, N_KEYS, PEER_HALF), PEER_HALF ** -0.5)
    peer_expert_down = nrm((L, N_EXPERTS, D_MODEL), D_MODEL ** -0.5)
    peer_expert_up = nrm((L, N_EXPERTS, D_MODEL), 0.5)
    return {"x": x, "c": c, "w_ada": w_ada, "b_ada": b_ada, "norm1_gain": norm1_gain,
            "w_in": w_in, "attn_q_gain": attn_q_gain, "attn_k_gain": attn_k_gain,
            "attn_rel_bias": attn_rel_bias, "attn_out_gain": attn_out_gain,
            "dn_conv_w": dn_conv_w, "dn_a_log": dn_a_log, "dn_dt_bias": dn_dt_bias,
            "dn_out_gain": dn_out_gain, "w_out": w_out, "norm2_gain": norm2_gain,
            "peer_w_query": peer_w_query, "peer_query_gain": peer_query_gain,
            "peer_sub_keys_1": peer_sub_keys_1, "peer_sub_keys_2": peer_sub_keys_2,
            "peer_expert_down": peer_expert_down, "peer_expert_up": peer_expert_up}

def first_block(x, c, w_ada, b_ada, norm1_gain, w_in, attn_q_gain, attn_k_gain, attn_rel_bias,
              attn_out_gain, dn_conv_w, dn_a_log, dn_dt_bias, dn_out_gain, w_out, norm2_gain,
              peer_w_query, peer_query_gain, peer_sub_keys_1, peer_sub_keys_2,
              peer_expert_down, peer_expert_up):
    for layer in range(DEPTH):
        x = hybrid_layer(x, c, w_ada[layer], b_ada[layer], norm1_gain[layer], w_in[layer],
                         attn_q_gain[layer], attn_k_gain[layer], attn_rel_bias[layer],
                         attn_out_gain[layer], dn_conv_w[layer], dn_a_log[layer], dn_dt_bias[layer],
                         dn_out_gain[layer], w_out[layer], norm2_gain[layer], peer_w_query[layer],
                         peer_query_gain[layer], peer_sub_keys_1[layer], peer_sub_keys_2[layer],
                         peer_expert_down[layer], peer_expert_up[layer])
    return x


HG_HEADS = 8
HG_DK = 128
HG_DV = 128
HG_KEY_WIDTH = HG_HEADS * HG_DK
HG_WIDTH = HG_HEADS * HG_DV
SB_HEADS = 16
SB_DH = 64
SB_WIDTH = SB_HEADS * SB_DH
SB_BLOCK = 128
FF_HIDDEN = (8 * D_MODEL + 3 * 256 - 1) // (3 * 256) * 256
IN_SPLITS = (HG_KEY_WIDTH, HG_KEY_WIDTH, HG_WIDTH, HG_WIDTH, SB_WIDTH, SB_WIDTH, SB_WIDTH, D_MODEL, D_MODEL)
IN_WIDTH = sum(IN_SPLITS)


def rms_norm_2(x, gain):
    x32 = x.astype(jnp.float32)
    y = x32 * lax.rsqrt(jnp.mean(x32 * x32, axis=-1, keepdims=True) + EPS) * gain.astype(jnp.float32)
    return y.astype(x.dtype)

def split_cols(t, widths):
    outs, start = [], 0
    for w in widths:
        outs.append(t[..., start:start + w])
        start += w
    return outs

def hgrn2_mixer(q, f_raw, i, lb):
    b, s, _ = q.shape
    n = s // CHUNK
    lb = lb.astype(jnp.float32)
    f = lb + (1.0 - lb) * jax.nn.sigmoid(f_raw.astype(jnp.float32))
    log_f = jnp.log(f)
    k = 1.0 - f

    def chunks(t, d):
        return t.astype(jnp.float32).reshape(b, n, CHUNK, HG_HEADS, d).transpose(1, 0, 3, 2, 4)

    qc, kc, gc = chunks(q, HG_DK), chunks(k, HG_DK), chunks(log_f, HG_DK)
    vc = chunks(i, HG_DV)
    causal = jnp.tril(jnp.ones((CHUNK, CHUNK), dtype=bool))[:, :, None]

    def step(state, inp):
        q_c, k_c, v_c, g_c = inp
        cum = jnp.cumsum(g_c, axis=-2)
        diff = cum[:, :, :, None, :] - cum[:, :, None, :, :]
        decay = jnp.exp(jnp.where(causal, diff, -jnp.inf))
        scores = jnp.einsum('bhtd,bhtsd,bhsd->bhts', q_c, decay, k_c)
        o = (jnp.einsum('bhts,bhsv->bhtv', scores, v_c)
             + jnp.einsum('bhtd,bhdv->bhtv', q_c * jnp.exp(cum), state))
        last = cum[:, :, -1:, :]
        state = (jnp.exp(last[:, :, 0, :, None]) * state
                 + jnp.einsum('bhsd,bhsv->bhdv', k_c * jnp.exp(last - cum), v_c))
        return state, o

    s0 = jnp.zeros((b, HG_HEADS, HG_DK, HG_DV), jnp.float32)
    _, o = lax.scan(step, s0, (qc, kc, vc, gc))
    return o.transpose(1, 0, 3, 2, 4).reshape(b, s, HG_HEADS, HG_DV)

def stick_breaking(q, k, v):
    s_len = q.shape[2]
    scale = 1.0 / float(np.sqrt(SB_DH))
    outs = []
    for blk in range(s_len // SB_BLOCK):
        q0 = blk * SB_BLOCK
        end = q0 + SB_BLOCK
        z = jnp.einsum('bhqd,bhkd->bhqk', q[:, :, q0:end], k[:, :, :end]) * scale
        qpos = q0 + jnp.arange(SB_BLOCK)
        kpos = jnp.arange(end)
        mask = kpos[None, :] < qpos[:, None]
        log_keep = jnp.where(mask, jax.nn.log_sigmoid(-z), 0.0)
        log_w = jax.nn.log_sigmoid(z) + lax.cumsum(log_keep, axis=3, reverse=True) - log_keep
        a = jnp.where(mask, jnp.exp(log_w), 0.0)
        outs.append(jnp.einsum('bhqk,bhkd->bhqd', a, v[:, :, :end]))
    return jnp.concatenate(outs, axis=2)

def second_inputs(seed: int = 0) -> dict:
    key = jax.random.key(seed)
    ks = jax.random.split(key, 14)
    f32 = jnp.float32
    nrm = lambda k, shape, fan: jax.random.normal(k, shape, f32) * (fan ** -0.5)
    gain = lambda k, shape: 1.0 + 0.02 * jax.random.normal(k, shape, f32)
    return {
        'x': jax.random.normal(ks[0], (BATCH, SEQ, D_MODEL), f32),
        'norm1_gain': gain(ks[1], (DEPTH, D_MODEL)),
        'w_in': nrm(ks[2], (DEPTH, D_MODEL, IN_WIDTH), D_MODEL),
        'lb_logits': 0.5 * jax.random.normal(ks[3], (DEPTH + 1, HG_KEY_WIDTH), f32),
        'hg_out_norm': gain(ks[4], (DEPTH, HG_HEADS, HG_DV)),
        'sb_q_norm': gain(ks[5], (DEPTH, SB_HEADS, SB_DH)),
        'sb_k_norm': gain(ks[6], (DEPTH, SB_HEADS, SB_DH)),
        'w_hg_out': nrm(ks[7], (DEPTH, HG_WIDTH, D_MODEL), HG_WIDTH),
        'w_sb_out': nrm(ks[8], (DEPTH, SB_WIDTH, D_MODEL), SB_WIDTH),
        'w_o': nrm(ks[9], (DEPTH, D_MODEL, D_MODEL), D_MODEL),
        'norm2_gain': gain(ks[10], (DEPTH, D_MODEL)),
        'w_ffn_in': nrm(ks[11], (DEPTH, D_MODEL, 2 * FF_HIDDEN), D_MODEL),
        'w_ffn_out': nrm(ks[12], (DEPTH, FF_HIDDEN, D_MODEL), FF_HIDDEN),
    }

def second_block(x, norm1_gain, w_in, lb_logits, hg_out_norm, sb_q_norm, sb_k_norm,
              w_hg_out, w_sb_out, w_o, norm2_gain, w_ffn_in, w_ffn_out):
    b, s, _ = x.shape
    lower_bounds = jnp.cumsum(jax.nn.softmax(lb_logits.astype(jnp.float32), axis=0), axis=0)
    for layer in range(DEPTH):
        h = rms_norm_2(x, norm1_gain[layer])
        proj = h @ w_in[layer]
        hq, hf, hi, hg, sq, sk, sv, ga, gb = split_cols(proj, IN_SPLITS)

        o_hg = hgrn2_mixer(hq, hf, hi, lower_bounds[layer])
        o_hg = rms_norm_2(o_hg, hg_out_norm[layer]).reshape(b, s, HG_WIDTH)
        o_hg = o_hg * jax.nn.sigmoid(hg.astype(jnp.float32))
        y_hg = o_hg.astype(x.dtype) @ w_hg_out[layer]

        def heads(t):
            return t.astype(jnp.float32).reshape(b, s, SB_HEADS, SB_DH)
        q = rms_norm_2(heads(sq), sb_q_norm[layer]).transpose(0, 2, 1, 3)
        k = rms_norm_2(heads(sk), sb_k_norm[layer]).transpose(0, 2, 1, 3)
        v = heads(sv).transpose(0, 2, 1, 3)
        o_sb = stick_breaking(q, k, v).transpose(0, 2, 1, 3).reshape(b, s, SB_WIDTH)
        y_sb = o_sb.astype(x.dtype) @ w_sb_out[layer]

        mixed = jax.nn.sigmoid(ga) * y_hg + jax.nn.sigmoid(gb) * y_sb
        x = x + mixed @ w_o[layer]

        h2 = rms_norm_2(x, norm2_gain[layer])
        gate, up = split_cols(h2 @ w_ffn_in[layer], (FF_HIDDEN, FF_HIDDEN))
        x = x + (jax.nn.silu(gate) * up) @ w_ffn_out[layer]
    return x


def setup_inputs(seed=0):
    out = dict(first_inputs(seed))
    for name, value in second_inputs(seed + 1).items():
        if name != "x":
            out[name + "_2"] = value
    return out


def reference(
    x, c, w_ada, b_ada, norm1_gain, w_in, attn_q_gain, attn_k_gain, attn_rel_bias,
    attn_out_gain, dn_conv_w, dn_a_log, dn_dt_bias, dn_out_gain, w_out, norm2_gain,
    peer_w_query, peer_query_gain, peer_sub_keys_1, peer_sub_keys_2, peer_expert_down,
    peer_expert_up, norm1_gain_2, w_in_2, lb_logits_2, hg_out_norm_2, sb_q_norm_2, sb_k_norm_2,
    w_hg_out_2, w_sb_out_2, w_o_2, norm2_gain_2, w_ffn_in_2, w_ffn_out_2,
):
    x = first_block(
        x, c, w_ada, b_ada, norm1_gain, w_in, attn_q_gain, attn_k_gain, attn_rel_bias,
        attn_out_gain, dn_conv_w, dn_a_log, dn_dt_bias, dn_out_gain, w_out, norm2_gain,
        peer_w_query, peer_query_gain, peer_sub_keys_1, peer_sub_keys_2, peer_expert_down,
        peer_expert_up,
    )
    return second_block(
        x, norm1_gain_2, w_in_2, lb_logits_2, hg_out_norm_2, sb_q_norm_2, sb_k_norm_2,
        w_hg_out_2, w_sb_out_2, w_o_2, norm2_gain_2, w_ffn_in_2, w_ffn_out_2,
    )


_drawn_inputs = setup_inputs


def setup_inputs(seed=0):
    import zlib

    import numpy as np

    out = dict(_drawn_inputs(seed))
    spreads = {}
    factors = {'norm1_gain': 5.356,
     'attn_q_gain': 8.0,
     'attn_k_gain': 8.0,
     'attn_out_gain': 23.629,
     'dn_a_log': 3.118,
     'dn_out_gain': 7.685,
     'norm2_gain': 10.959,
     'peer_query_gain': 13.057,
     'norm1_gain_2': 3.928,
     'hg_out_norm_2': 107.8,
     'sb_q_norm_2': 40.235,
     'sb_k_norm_2': 36.854,
     'norm2_gain_2': 14.806}
    for name, (base, spread) in spreads.items():
        noise = np.random.default_rng([zlib.crc32(name.encode()), seed]).standard_normal(out[name].shape)
        drawn = base * np.exp(spread * noise) if base else spread * noise
        out[name] = jnp.asarray(drawn.astype(out[name].dtype))
    for name, factor in factors.items():
        out[name] = (out[name] * factor).astype(out[name].dtype)
    return out
```

```python
from contextlib import ExitStack

import concourse.bass as bass
from concourse import mybir

F32 = mybir.dt.float32
F32R = mybir.dt.float32r
U32 = mybir.dt.uint32
ALU = mybir.AluOpType
ACT = mybir.ActivationFunctionType
AX = mybir.AxisListType.X

P = 128
D = 1024
KT = D // P
S = 256
TT = S // P
EPS = 1e-6
NEG = -1e30
SLOTS = 4
SLOT = 2048
UNIT = 512
UPC = SLOT // UNIT
BUFFERS = 4

O_CONST = 0
O_GATE2 = 1536
O_X_HI = O_GATE2 + D
O_X_LO = O_X_HI + KT * S
O_W_HI = O_X_LO + KT * S
O_W_LO = O_W_HI + BUFFERS * UNIT
O_RING = O_W_LO + BUFFERS * UNIT
O_R = O_RING + SLOTS * SLOT
O_PICKS = O_R + P * S
WORDS = O_PICKS + 3 * S + 640


class Stream:

    def __init__(self, ring, landed, lo_ready, turned):
        self.ring, self.landed, self.lo_ready, self.turned = ring, landed, lo_ready, turned
        self.segments, self.count, self.issued, self.units = [], 0, 0, 0

    def add(self, count, source, cols, turned=False):
        unit0 = 0 if turned else self.units
        self.segments.append((self.count, count, source, cols, self.turned if turned else self.lo_ready,
                              2 if turned else UPC, unit0))
        self.count += count
        if not turned:
            self.units += UPC * count
        return self.count - count, unit0

    def words(self, n, first, count):
        o = (n % SLOTS) * SLOT + first
        return self.ring[:, o:o + count]

    def landed_value(self, n):
        return 16 * (n // SLOTS + 1)

    def load(self, sp, n, rounds, j, seg):
        start, _, source, cols, _, _, _ = seg
        if n >= SLOTS:
            for s0, count, _, _, used, per, unit0 in self.segments:
                if s0 <= n - SLOTS < s0 + count:
                    sp.wait_ge(used, rounds * (per * SLOTS) + (unit0 + per * (n - SLOTS - s0 + 1)))
        dst = self.ring[:, (n % SLOTS) * SLOT:(n % SLOTS + 1) * SLOT].rearrange("p (k n) -> p k n", n=cols)
        sp.dma_start(dst, source(rounds, j)).then_inc(self.landed[n % SLOTS], 16)

    def issue(self, sp, upto):
        for seg in self.segments:
            start, count = seg[0], seg[1]
            lo, hi = max(self.issued, start), min(upto, start + count)
            if lo >= hi:
                continue
            n = lo
            while n < hi and (n < start + SLOTS or (n - start) % SLOTS):
                self.load(sp, n, 0, n - start, seg)
                n += 1
            rounds = (hi - n) // SLOTS
            if rounds > 1:
                with sp.Fori(0, rounds) as r:
                    for j in range(SLOTS):
                        self.load(sp, n + j, r, n + j - start, seg)
                n += SLOTS * rounds
            for m in range(n, hi):
                self.load(sp, m, 0, m - start, seg)
            self.issued = hi


class Steps:

    def __init__(self, eng, sem, done=0):
        self.eng, self.sem, self.done = eng, sem, done

    def __call__(self, ins):
        self.done += 1
        ins.then_inc(self.sem, 1)
        self.eng.wait_ge(self.sem, self.done)


class Pieces:

    def __init__(self, pieces):
        self.pieces = pieces

    def piece(self, t):
        return self.pieces[(t + 2) // 4]

    def __getitem__(self, key):
        _, k, tokens = key
        return self.piece(k)[:, k if k < 2 else (k + 2) % 4, tokens]


def build(nc, A, out):
    with ExitStack() as ctx:
        mem = ctx.enter_context(nc.sbuf_tensor("mem", [P, WORDS], F32))
        mem_base = nc.sbuf_base - 4 * WORDS
        ps = ctx.enter_context(nc.psum_tensor("ps", [P, 8, 512], F32))
        psf = ps[:, :, :].rearrange("p b n -> p (b n)")
        ctx.enter_context(nc.allow_non_contiguous_dma(reason="short rows of small parameters"))
        x_spill = nc.dram_tensor("x_spill", (P, TT * D), F32, kind="Internal").ap()
        rel_ext = nc.dram_tensor("rel_ext", (8, 384), F32, kind="Internal").ap()

        stage_sems = []

        def lasting_sem(name):
            return ctx.enter_context(nc.semaphore(name))

        def sem(name):
            stage_sems.append(nc.alloc_semaphore(name))
            return stage_sems[-1]

        def renew_semaphores():
            with nc.Block() as block:
                @block.gpsimd
                def _(pool):
                    nc.clear_and_free_semaphores(stage_sems)
            stage_sems.clear()

        def at(off, *shape):
            n = 1
            for s in shape:
                n *= s
            v = mem[:, off:off + n]
            if len(shape) == 2:
                v = v.rearrange("p (a b) -> p a b", b=shape[1])
            elif len(shape) == 3:
                v = v.rearrange("p (a b c) -> p a b c", b=shape[1], c=shape[2])
            return v

        def wide(ap, n):
            return ap.unsqueeze(2).to_broadcast([ap.shape[0], ap.shape[1], n])

        ident = at(O_CONST, P)
        ones = at(O_CONST + 128, P)
        anti = at(O_CONST + 256, P)
        upper = at(O_CONST + 384, P)
        strict_low = at(O_CONST + 512, P)
        strict_up = at(O_CONST + 640, P)
        low = at(O_CONST + 768, P)
        iota = at(O_CONST + 896, P)
        zeros = at(O_CONST + 1024, P)
        eps = at(O_CONST + 1152, 1)
        tiny = at(O_CONST + 1160, 160)
        gate2 = at(O_GATE2, D)

        views = []

        def atr(off, *shape):
            n = shape[0] * (shape[1] if len(shape) > 1 else 1)
            for o, size, tensor in views:
                if o <= off and off + n <= o + size:
                    break
            else:
                o, tensor = off, nc.alloc_sbuf_tensor_at(f"parts{len(views)}", [P, n], F32R, offset=mem_base + 4 * off)
                views.append((off, n, tensor))
            v = tensor[:, off - o:off - o + n]
            return v.rearrange("p (a b) -> p a b", b=shape[1]) if len(shape) == 2 else v

        x_hi, x_lo = atr(O_X_HI, KT, S), atr(O_X_LO, KT, S)
        w_hi, w_lo = ([atr(o, BUFFERS, UNIT)[:, i, :] for i in range(BUFFERS)] for o in (O_W_HI, O_W_LO))

        landed = [lasting_sem(f"landed{i}") for i in range(SLOTS)]
        hi_ready, lo_ready = lasting_sem("hi_ready"), lasting_sem("lo_ready")
        unit_used, turned = lasting_sem("unit_used"), lasting_sem("down_turned")
        st = Stream(at(O_RING, SLOTS * SLOT), landed, lo_ready, turned)

        def column_chunks(w, first):
            v = w.rearrange("(k p) n -> p k n", p=P)
            return lambda r, j: v[:, j % 2 * 4:j % 2 * 4 + 4, bass.ds(r * 1024 + (first + j // 2 * 512), 512)]

        def row_chunks(w):
            v = w.rearrange("(k p) n -> p k n", p=P)
            return lambda r, j: v[:, bass.ds(r * 8 + j * 2, 2), :]

        def expert_chunks(w):
            v = w.rearrange("(a b) d -> a b d", a=P)
            return lambda r, j: v[:, bass.ds(r * 8 + j * 2, 2), :]

        w_in, w_in2 = A["w_in"][0], A["w_in_2"][0]
        FF = A["w_ffn_out_2"].shape[1]
        FT = FF // P
        n_ada = st.add(24, column_chunks(A["w_ada"][0], 0), 512)
        n_in = st.add(14, column_chunks(w_in, 0), 512)
        n_wout = st.add(4, row_chunks(A["w_out"][0]), D)
        n_query = st.add(8, column_chunks(A["peer_w_query"][0], 0), 512)
        n_down = st.add(64, expert_chunks(A["peer_expert_down"][0]), D, turned=True)
        n_up = st.add(64, expert_chunks(A["peer_expert_up"][0]), D)
        n_in2a = st.add(8, column_chunks(w_in2, 0), 512)
        n_in2b = st.add(28, column_chunks(w_in2, 4 * 512), 512)
        n_hgo = st.add(4, row_chunks(A["w_hg_out_2"][0]), D)
        n_sbo = st.add(4, row_chunks(A["w_sb_out_2"][0]), D)
        n_wo = st.add(4, row_chunks(A["w_o_2"][0]), D)
        n_ffi = st.add(22, column_chunks(A["w_ffn_in_2"][0], 0), 512)
        n_ffo = st.add(11, row_chunks(A["w_ffn_out_2"][0]), D)

        def split_hi(act, n, g, u, rounds):
            if u == 0:
                act.wait_ge(landed[n % SLOTS], rounds * 16 + st.landed_value(n))
            act.wait_ge(unit_used, rounds * (UPC * SLOTS) + (g + 1))
            act.copy(w_hi[g % BUFFERS], st.words(n, u * UNIT, UNIT)).then_inc(hi_ready, 1)

        def split_lo(dve, n, g, u, rounds):
            dve.wait_ge(hi_ready, rounds * (UPC * SLOTS) + (g + 1))
            dve.tensor_tensor(w_lo[g % BUFFERS], st.words(n, u * UNIT, UNIT), w_hi[g % BUFFERS].bitcast(F32),
                              ALU.subtract).then_inc(lo_ready, 1)

        def await_unit(pe, g, rounds):
            pe.wait_ge(lo_ready, rounds * (UPC * SLOTS) + (g + 1))

        def three(pe, o, lhs, rhs, start, stop, **kw):
            for i, (a, b) in enumerate(((0, 0), (0, 1), (1, 0))):
                mm = pe.matmul(o, lhs[a], rhs[b], start=start and i == 0, stop=stop and i == 2,
                               skip_group_check=True, **kw)
            return mm

        def product_group(pe, c, g, rounds, kind, left):
            for k in range(KT):
                await_unit(pe, g + k, rounds)
                parts = [w[(g + k) % BUFFERS] for w in (w_hi, w_lo)]
                if kind == "t":
                    for tt in range(TT):
                        ts = slice(tt * P, (tt + 1) * P)
                        mm = three(pe, ps[:, c % 2 * 4 + tt, :], [a[:, k, ts] for a in left], parts,
                                   k == 0, k == KT - 1)
                else:
                    for m in range(4):
                        ms = slice(m * P, (m + 1) * P)
                        mm = three(pe, ps[:, c % 2 * 4 + m, 0:S], [w[:, ms] for w in parts],
                                   [a[:, k, :] for a in left], k == 0, k == KT - 1)
                mm.then_inc(unit_used, 1)

        def split_groups(eng, split, at_unit, seg, groups, evacuate):
            n0, g0 = seg
            for c in range(groups):
                for u in range(KT):
                    split(eng, n0 + 2 * c + u // UPC, g0 + KT * c + u, u % UPC, 0)
                    if u == at_unit and c:
                        eng.wait_ge(unit_used, used_value(g0 + KT * c - 1))
                        evacuate(c - 1)
            eng.wait_ge(unit_used, used_value(g0 + KT * groups - 1))
            evacuate(groups - 1)

        def hi_groups(act, seg, groups, evacuate):
            split_groups(act, split_hi, 4, seg, groups, evacuate)

        def lo_groups(dve, seg, groups, evacuate):
            split_groups(dve, split_lo, 3, seg, groups, evacuate)

        def used_value(g):
            return g + 1 + BUFFERS

        def transposes(pe, pairs):
            for o, i in pairs:
                last = pe.transpose(o, i, ident[0:i.shape[0], 0:i.shape[0]])
            return last

        def turn_rows(pe, rows, s_t):
            for q in range(4):
                transposes(pe, [(psf[:, (k * TT + tt) * P:(k * TT + tt + 1) * P], rows[:, tt, k * P:(k + 1) * P])
                                for k in (2 * q, 2 * q + 1) for tt in range(TT)]).then_inc(s_t, 1)

        def turned_hi(act, s_t, s_hi):
            for q in range(4):
                act.wait_ge(s_t, q + 1)
                act.copy(atr(O_X_HI + q * 512, 512), ps[:, q, :]).then_inc(s_hi, 1)

        def turned_lo(dve, s_hi, s_lo):
            for q in range(4):
                dve.wait_ge(s_hi, q + 1)
                dve.tensor_tensor(atr(O_X_LO + q * 512, 512), ps[:, q, :], atr(O_X_HI + q * 512, 512).bitcast(F32),
                                  ALU.subtract).then_inc(s_lo, 1)

        x = at(O_R, TT, D)
        O_MODS = O_R + TT * D
        mods = at(O_MODS, 6, D)
        shift1, scale1, gate1, shift2, scale2 = (mods[:, i, :] for i in range(5))
        O_S = O_MODS + 6 * D
        gain = at(O_S, D)
        h = at(O_S + D, TT, D)
        O_P1 = O_S + 3 * D
        N_P1 = 3 * 512 + 512
        p1 = at(O_P1, TT, N_P1)
        O_BA = O_P1 + TT * N_P1
        ba = at(O_BA, TT, 8)
        w_ba = at(O_BA + 16, KT, 8)
        O_CV = O_BA + 96
        LEAD = 3
        conv_in = at(O_CV, 12, S + LEAD)
        O_A = O_CV + 12 * (S + LEAD) + 4

        c_col = at(O_P1, KT)
        c_hi, c_lo = atr(O_X_HI, KT, P), atr(O_X_LO, KT, P)
        b_ada = mem[0:1, O_A:O_A + 6 * D]

        s_c, s_x, s_csil, s_crow, s_clo = sem("c_loaded"), sem("x_loaded"), sem("c_silu"), sem("c_hi"), sem("c_lo")
        s_ada, s_ada_out, s_const, s_pool = sem("ada_done"), sem("ada_bank_free"), lasting_sem("constants"), sem("pool_steps")
        with nc.Block() as block:
            @block.sync
            def _(sp):
                sp.dma_start(c_col, A["c"][0].rearrange("(k p) -> p k", p=P)).then_inc(s_c, 16)
                sp.dma_start(b_ada, A["b_ada"]).then_inc(s_c, 16)
                sp.dma_start(x, A["x"][0].rearrange("(t p) d -> p t d", p=P)).then_inc(s_x, 16)
                sp.dma_start(w_ba, w_in.rearrange("(k p) n -> p k n", p=P)[:, :, 3584:3592]).then_inc(s_x, 16)
                sp.dma_start(gain, A["norm1_gain"].to_broadcast([P, D])).then_inc(s_x, 16)
                st.issue(sp, n_in[0] + SLOTS)

            @block.gpsimd
            def _(pool):
                step = Steps(pool, s_pool)
                for m, v in ((ident, 0.0), (anti, 0.0), (ones, 1.0), (upper, 1.0), (strict_low, 1.0),
                             (strict_up, 1.0), (low, 1.0), (zeros, 0.0), (eps, EPS)):
                    step(pool.memset(m, v))
                for m, op, fill, base, pattern, mult in (
                        (ident, ALU.not_equal, 1.0, 0, -1, 1), (anti, ALU.not_equal, 1.0, -(P - 1), 1, 1),
                        (upper, ALU.is_ge, 0.0, 0, 1, -1), (strict_low, ALU.is_gt, 0.0, 0, -1, 1),
                        (strict_up, ALU.is_gt, 0.0, 0, 1, -1), (low, ALU.is_ge, 0.0, 0, -1, 1)):
                    step(pool.affine_select(out=m, in_=m, compare_op=op, fill=fill, base=base,
                                            pattern=[[pattern, P]], channel_multiplier=mult))
                pool.iota(iota, pattern=[[1, P]], base=0, channel_multiplier=0,
                          allow_small_or_imprecise_dtypes=True).then_inc(s_const, 1)

            n, g = n_ada

            @block.scalar
            def _(act):
                act.wait_ge(s_c, 32)
                act.activation(c_col, c_col, ACT.Silu).then_inc(s_csil, 1)
                act.wait_ge(s_csil, 1)
                act.copy(c_hi, wide(c_col, P)).then_inc(s_crow, 1)
                with act.Fori(0, 6) as r:
                    for u in range(16):
                        split_hi(act, n + u // UPC, g + u, u % UPC, r)

            @block.vector
            def _(dve):
                dve.wait_ge(s_crow, 1)
                dve.tensor_tensor(c_lo, wide(c_col, P), c_hi.bitcast(F32), ALU.subtract).then_inc(s_clo, 1)

                def out_row(c, rounds):
                    dve.wait_ge(s_ada, rounds * 2 + (c + 1))
                    dve.wait_ge(s_const, 1)
                    dve.tensor_copy(mem[:, bass.ds(rounds * 1024 + (O_MODS + 512 * c), 512)],
                                    ps[:, c % 2, :]).then_inc(s_ada_out, 1)
                for u in range(16):
                    split_lo(dve, n + u // UPC, g + u, u % UPC, 0)
                    if u == 11:
                        out_row(0, 0)
                with dve.Fori(0, 5) as r:
                    for u in range(16, 32):
                        split_lo(dve, n + u // UPC, g + u, u % UPC, r)
                        if u % 8 == 3:
                            out_row(u // 8 - 1, r)
                out_row(11, 0)

            @block.tensor
            def _(pe):
                pe.sem_inc(unit_used, BUFFERS)
                pe.sem_inc(s_ada_out, 2)
                pe.wait_ge(s_clo, 1)
                pe.wait_ge(s_const, 1)
                with pe.Fori(0, 6) as r:
                    for c in range(2):
                        pe.wait_ge(s_ada_out, r * 2 + (c + 1))
                        for k in range(KT):
                            await_unit(pe, g + KT * c + k, r)
                            three(pe, ps[:, c, :], [c_hi[:, k, :], c_lo[:, k, :]],
                                  [w[k % BUFFERS] for w in (w_hi, w_lo)], k == 0, False).then_inc(unit_used, 1)
                        pe.matmul(ps[:, c, :], ones[0:1, :],
                                  mem[0:1, bass.ds(r * 1024 + (O_A + 512 * c), 512)],
                                  start=False, stop=True, skip_group_check=True).then_inc(s_ada, 1)

        def norm_stage(tag, rows, src, s_gain, gain_value, shift=None, scale=None, before=None, extra=None):
            s_sq, s_std, s_h, s_t, s_hi, s_lo = (sem(f"{tag}_{n}") for n in (
                "squares", "std", "rows", "transposed", "hi", "lo"))
            s_v = sem(f"{tag}_steps")
            with nc.Block() as block:
                @block.scalar
                def _(act):
                    for tt in range(TT):
                        act.activation(rows[:, tt, :], src[:, tt, :], ACT.Square,
                                       accum_out=tiny[:, tt:tt + 1]).then_inc(s_sq, 1)
                    act.wait_ge(s_sq, TT)
                    act.activation(tiny[:, 2:4], tiny[:, 0:2], ACT.Sqrt, bias=eps, scale=1.0 / D).then_inc(s_std, 1)
                    turned_hi(act, s_t, s_hi)

                @block.vector
                def _(dve):
                    step = Steps(dve, s_v)
                    dve.wait_ge(s_std, 1)
                    step(dve.reciprocal(tiny[:, 4:6], tiny[:, 2:4]))
                    dve.wait_ge(s_gain, gain_value)
                    for tt in range(TT):
                        one = dve.scalar_tensor_tensor(out=rows[:, tt, :], in0=src[:, tt, :],
                                                       scalar=tiny[:, 4 + tt:5 + tt], in1=gain,
                                                       op0=ALU.mult, op1=ALU.mult)
                        if scale is not None:
                            step(one)
                            step(dve.scalar_tensor_tensor(out=rows[:, tt, :], in0=scale, scalar=1.0,
                                                          in1=rows[:, tt, :], op0=ALU.add, op1=ALU.mult))
                            one = dve.tensor_tensor(rows[:, tt, :], rows[:, tt, :], shift, ALU.add)
                        one.then_inc(s_h, 1)
                    turned_lo(dve, s_hi, s_lo)

                @block.tensor
                def _(pe):
                    pe.wait_ge(s_h, TT)
                    turn_rows(pe, rows, s_t)

        norm_stage("norm1", h, x, s_x, 48, shift1, scale1)

        s_ba, s_bank_v, s_bank_a = sem("proj1_ba_done"), sem("proj1_bank_out_dve"), sem("proj1_bank_out_act")
        s_z3, s_bah = sem("conv_lead_zero"), sem("ba_hi")
        ba_hi, ba_lo = (atr(O_A + 64 * i, KT * 8).rearrange("p (k n) -> p k n", n=8) for i in range(2))

        with nc.Block() as block:
            n0, g0 = n_in

            @block.sync
            def _(sp):
                st.issue(sp, n_wout[0] + SLOTS)

            @block.gpsimd
            def _(pool):
                pool.memset(conv_in[:, :, 0:LEAD], 0.0).then_inc(s_z3, 1)

            @block.tensor
            def _(pe):
                for c in range(7):
                    if c >= 2:
                        pe.wait_ge(s_bank_v, c - 1)
                        pe.wait_ge(s_bank_a, c - 1)
                    product_group(pe, c, g0 + KT * c, 0, "f" if 3 <= c < 6 else "t", (x_hi, x_lo))
                for tt in range(TT):
                    for k in range(KT):
                        ts = slice(tt * P, (tt + 1) * P)
                        mm = three(pe, ps[:, 7, tt * 8:tt * 8 + 8], [x_hi[:, k, ts], x_lo[:, k, ts]],
                                   [ba_hi[:, k, :], ba_lo[:, k, :]], k == 0, k == KT - 1)
                mm.then_inc(s_ba, 1)

            def out_of(b, c):
                if 3 <= c < 6:
                    t = (c - 3) * 4 + b * 2
                    return conv_in[:, t:t + 2, LEAD:LEAD + S], ps[:, c % 2 * 4 + 2 * b:c % 2 * 4 + 2 * b + 2, 0:S]
                col = 512 * (c if c < 3 else 3)
                return p1[:, b, col:col + 512], ps[:, c % 2 * 4 + b, :]

            @block.vector
            def _(dve):
                dve.wait_ge(s_bah, 1)
                dve.tensor_tensor(ba_lo, w_ba, ba_hi.bitcast(F32), ALU.subtract)
                lo_groups(dve, n_in, 7, lambda c: dve.tensor_copy(*out_of(0, c)).then_inc(s_bank_v, 1))
                dve.wait_ge(s_ba, 1)
                dve.tensor_copy(ba, ps[:, 7, 0:16].rearrange("p (t n) -> p t n", n=8)).then_inc(s_bank_v, 1)

            @block.scalar
            def _(act):
                act.copy(ba_hi, w_ba).then_inc(s_bah, 1)
                hi_groups(act, n_in, 7, lambda c: act.copy(*out_of(1, c)).then_inc(s_bank_a, 1))

        HA, DA = 8, 64
        mix = at(O_A, TT, D)
        O_B = O_A + TT * D
        qkT = at(O_B, 2 * HA, S)[0:DA]
        prob = at(O_B + 4096, HA, 384)
        probT = at(O_B + 4096 + 3072, 3 * HA, P)
        O_BT = O_B + 4096 + 6144
        bias_r = at(O_BT, HA, 2 * P)
        qk_gain = at(O_BT + 2048, 2, DA)
        att_gain = at(O_BT + 2048 + 128, 512)
        ext = mem[0:HA, O_B + 4096:O_B + 4096 + 384]
        squares = at(O_B + 4096, TT, D)
        NREL = A["attn_rel_bias"].shape[2]
        s_par, s_ext, s_ext_out, s_bias, s_bneg = (sem("att_" + n) for n in (
            "params", "rel_extended", "rel_stored", "bias_loaded", "bias_masked"))
        s_sum, s_std, s_qk, s_tr, s_ev_v, s_ev_a, s_sc, s_diff, s_exp, s_pt, s_ptv, s_pta, s_o, s_on, s_osq, s_ostd, s_dv = (
            sem("att_" + n) for n in (
                "sums", "std", "qk_normed", "qk_transposed", "qkT_dve", "qkT_act", "scores", "shifted", "exp",
                "probs_transposed", "probT_dve", "probT_act", "heads", "out_rows", "out_squares", "out_std", "steps"))
        with nc.Block() as block:
            @block.sync
            def _(sp):
                sp.dma_start(ext[:, 0:NREL], A["attn_rel_bias"][0]).then_inc(s_par, 16)
                sp.dma_start(qk_gain[:, 0, :], A["attn_q_gain"].to_broadcast([P, DA])).then_inc(s_par, 16)
                sp.dma_start(qk_gain[:, 1, :], A["attn_k_gain"].to_broadcast([P, DA])).then_inc(s_par, 16)
                sp.dma_start(att_gain, A["attn_out_gain"].to_broadcast([P, 512])).then_inc(s_par, 16)
                sp.wait_ge(s_ext, 1)
                sp.dma_start(rel_ext, ext).then_inc(s_ext_out, 16)
                sp.wait_ge(s_ext_out, 16)
                for blk in range(2):
                    src = bass.AP(rel_ext.tensor, 1 + P * blk, [[1, P], [384, HA], [1, P]])
                    sp.dma_start(bias_r[:, :, blk * P:(blk + 1) * P], src).then_inc(s_bias, 16)

            @block.gpsimd
            def _(pool):
                pool.wait_ge(s_bias, 32)
                pool.memset(bias_r[0:64, :, 0:64], NEG).then_inc(s_bneg, 1)

            @block.vector
            def _(dve):
                step = Steps(dve, s_dv)
                dve.wait_ge(s_par, 64)
                dve.tensor_scalar(ext[:, NREL:384], ones[0:HA, 0:384 - NREL], ext[:, NREL - 1:NREL], None, ALU.mult)\
                    .then_inc(s_ext, 1)
                dve.wait_ge(s_ext_out, 16)
                step(dve.tensor_tensor(squares, p1[:, :, 0:D], p1[:, :, 0:D], ALU.mult))
                dve.tensor_reduce(tiny[:, 0:32], squares.rearrange("p t (h d) -> p (t h) d", d=DA), AX, ALU.add)\
                    .then_inc(s_sum, 1)
                step(dve.tensor_scalar(qk_gain[:, 0, :], qk_gain[:, 0, :], DA ** -0.5, None, ALU.mult))
                dve.wait_ge(s_std, 1)
                step(dve.reciprocal(tiny[:, 64:96], tiny[:, 32:64]))
                for tt in range(TT):
                    v = p1[:, tt, 0:D].rearrange("p (h d) -> p h d", d=DA)
                    step(dve.tensor_tensor(v, v, wide(tiny[:, 64 + 16 * tt:80 + 16 * tt], DA), ALU.mult))
                    for q in range(2):
                        w = v[:, q * HA:(q + 1) * HA, :]
                        ins = dve.tensor_tensor(w, w, qk_gain[:, q:q + 1, :].to_broadcast([P, HA, DA]), ALU.mult)
                    ins.then_inc(s_qk, 1)
                for b in range(0, 8, 2):
                    dve.wait_ge(s_tr, b + 1)
                    dve.tensor_copy(qkT[:, 2 * b:2 * b + 2, :], ps[0:DA, b, :].rearrange("p (a t) -> p a t", t=S))\
                        .then_inc(s_ev_v, 1)
                for half in range(2):
                    hs = slice(half * 4, half * 4 + 4)
                    dve.wait_ge(s_sc, half * 4 + 4)
                    for i, (a, b) in enumerate(((0, P), (P, 384))):
                        m = tiny[:, 96 + i * 8 + half * 4:100 + i * 8 + half * 4]
                        step(dve.tensor_reduce(m, ps[:, hs, a:b], AX, ALU.max))
                        ins = dve.tensor_tensor(prob[:, hs, a:b], ps[:, hs, a:b], wide(m, b - a), ALU.subtract)
                    ins.then_inc(s_diff, 1)
                for half in range(2):
                    hs = slice(half * 4, half * 4 + 4)
                    dve.wait_ge(s_exp, half + 1)
                    step(dve.tensor_reduce(tiny[:, 112 + half * 4:116 + half * 4], prob[:, hs, 0:P], AX, ALU.add))
                    step(dve.tensor_reduce(tiny[:, 120 + half * 4:124 + half * 4], prob[:, hs, P:384], AX, ALU.add))
                step(dve.reciprocal(tiny[:, 112:128], tiny[:, 112:128]))
                for b in range(0, 6, 2):
                    dve.wait_ge(s_pt, b + 1)
                    dve.tensor_copy(probT[:, 4 * b:4 * b + 4, :], ps[:, b, :].rearrange("p (a t) -> p a t", t=P))\
                        .then_inc(s_ptv, 1)
                dve.wait_ge(s_o, 1)
                for tt in range(TT):
                    dve.tensor_tensor(mix[:, tt, 0:512].rearrange("p (h d) -> p h d", d=DA),
                                      ps[:, 6 + tt, :].rearrange("p (h d) -> p h d", d=DA),
                                      wide(tiny[:, 112 + 8 * tt:120 + 8 * tt], DA), ALU.mult).then_inc(s_on, 1)
                dve.wait_ge(s_ostd, 1)
                step(dve.reciprocal(tiny[:, 4:6], tiny[:, 2:4]))
                for tt in range(TT):
                    step(dve.scalar_tensor_tensor(out=mix[:, tt, 0:512], in0=mix[:, tt, 0:512],
                                                  scalar=tiny[:, 4 + tt:5 + tt], in1=att_gain,
                                                  op0=ALU.mult, op1=ALU.mult))

            @block.scalar
            def _(act):
                act.wait_ge(s_sum, 1)
                act.activation(tiny[:, 32:64], tiny[:, 0:32], ACT.Sqrt, bias=eps, scale=1.0 / DA).then_inc(s_std, 1)
                for b in range(1, 8, 2):
                    act.wait_ge(s_tr, b + 1)
                    act.copy(qkT[:, 2 * b:2 * b + 2, :], ps[0:DA, b, :].rearrange("p (a t) -> p a t", t=S))\
                        .then_inc(s_ev_a, 1)
                for half in range(2):
                    act.wait_ge(s_diff, half + 1)
                    act.activation(prob[:, half * 4:half * 4 + 4, :], prob[:, half * 4:half * 4 + 4, :], ACT.Exp)\
                        .then_inc(s_exp, 1)
                for b in range(1, 6, 2):
                    act.wait_ge(s_pt, b + 1)
                    act.copy(probT[:, 4 * b:4 * b + 4, :], ps[:, b, :].rearrange("p (a t) -> p a t", t=P))\
                        .then_inc(s_pta, 1)
                act.wait_ge(s_on, 2)
                act.wait_ge(s_pt, 6)
                for tt in range(TT):
                    act.activation(prob[:, 0:4, 0:P], mix[:, tt, 0:512].rearrange("p (a t) -> p a t", t=P), ACT.Square,
                                   accum_out=tiny[:, tt:tt + 1]).then_inc(s_osq, 1)
                    act.wait_ge(s_osq, tt + 1)
                act.activation(tiny[:, 2:4], tiny[:, 0:2], ACT.Sqrt, bias=eps, scale=1.0 / 512).then_inc(s_ostd, 1)

            @block.tensor
            def _(pe):
                pe.wait_ge(s_qk, 2)
                for b in range(8):
                    transposes(pe, [(ps[0:DA, b, (u % 2) * S + tt * P:(u % 2) * S + (tt + 1) * P],
                                     p1[:, tt, u * DA:(u + 1) * DA])
                                    for u in (2 * b, 2 * b + 1) for tt in range(TT)]).then_inc(s_tr, 1)
                pe.wait_ge(s_ev_v, 4)
                pe.wait_ge(s_ev_a, 4)
                pe.wait_ge(s_bneg, 1)
                for hd in range(HA):
                    q, k = qkT[:, hd, :], qkT[:, HA + hd, :]
                    b0, b1 = bias_r[:, hd, 0:P], bias_r[:, hd, P:2 * P]
                    pe.matmul(ps[:, hd, 0:P], q[:, 0:P], k[:, 0:P], start=True, stop=False)
                    pe.matmul(ps[:, hd, 0:P], b0, anti, start=False, stop=True)
                    pe.matmul(ps[:, hd, P:384], q[:, P:S], k, start=True, stop=False)
                    pe.matmul(ps[:, hd, P:S], b1, anti, start=False, stop=False)
                    pe.matmul(ps[:, hd, S:384], b0, anti, start=False, stop=True).then_inc(s_sc, 1)
                for b in range(6):
                    pe.wait_ge(s_exp, 2 if b >= 3 else 1)
                    if b == 3:
                        pe.wait_ge(s_diff, 2)
                    transposes(pe, [(ps[:, b, j * P:(j + 1) * P],
                                     prob[:, (4 * b + j) // 3, (4 * b + j) % 3 * P:(4 * b + j) % 3 * P + P])
                                    for j in range(4)]).then_inc(s_pt, 1)
                pe.wait_ge(s_ptv, 3)
                pe.wait_ge(s_pta, 3)
                for tt in range(TT):
                    for hd in range(HA):
                        o = ps[:, 6 + tt, hd * DA:(hd + 1) * DA]
                        for j in range(tt + 1):
                            mm = pe.matmul(o, probT[:, 3 * hd + tt + j, :],
                                           p1[:, j, 2 * 512 + hd * DA:2 * 512 + (hd + 1) * DA],
                                           start=j == 0, stop=j == tt)
                mm.then_inc(s_o, 1)

        HD = 4
        U = TT * HD
        O_H = O_S + D
        taps = at(O_B, 48)
        taps_rows = mem[0:48, O_B + 48:O_B + 48 + P]
        dn_par = at(O_B + 176, 16)
        dn_gain = at(O_B + 192, P)
        gb = at(O_B + 320, 12, U)
        conv = at(O_B + 512, 12, S)
        O_C = O_B + 512 + 12 * S
        kbg, vb, T, TI, X, L = (at(O_C + i * 1024, U, P) for i in range(6))
        AT = at(O_C + 6 * 1024, U, P)
        vnew = at(O_C + 7 * 1024, U, P)
        wT = at(O_X_LO, HD, P)
        kdec = at(O_X_LO + 512, HD, P)
        assert O_C + 8 * 1024 <= WORDS
        Cm = [at(O_H + i * 1024, U, P) for i in range(2)]
        O_CI = O_CV
        Dm, DT, gcB = (at(O_CI + i * 1024, U, P) for i in range(3))
        state = at(O_X_HI, HD, P)
        qgT = at(O_X_HI + 512, HD, P)
        lev = at(O_P1, 7, P)
        zsil = p1[:, :, 3 * 512:4 * 512]
        g_, beta_, gc_, eg_, egk_, tmp_, beg_ = (gb[:, i, :] for i in range(7))
        ab = ba.rearrange("p t (b h) -> p t b h", b=2)
        (s_par, s_lev, s_lv, s_tap, s_tapo, s_conv, s_silu, s_sq, s_ssum, s_sstd, s_qkn, s_gpre, s_ge, s_gl, s_g, s_gcm,
         s_gco, s_gexp, s_diff, s_dexp, s_dm, s_tk, s_tko, s_kk, s_L, s_dv, s_sb) = (
            sem("dn_" + n) for n in (
                "params", "levels", "level_steps", "taps_transposed", "taps", "conv", "silu", "squares", "norms",
                "norm_std", "qk_normed", "gate_sum", "gate_exp", "gate_ln", "gate", "cumulated", "cumulated_rows", "gate_exps",
                "differences", "decays", "decay_masks", "kv_transposed", "kv_rows", "grams", "lower",
                "steps", "beta"))
        with nc.Block() as block:
            @block.sync
            def _(sp):
                sp.dma_start(taps_rows, A["dn_conv_w"][0].rearrange("i (t c) -> (i t) c", c=P)).then_inc(s_par, 16)
                sp.dma_start(dn_par[:, 0:4], A["dn_a_log"].to_broadcast([P, 4])).then_inc(s_par, 16)
                sp.dma_start(dn_par[:, 4:8], A["dn_dt_bias"].to_broadcast([P, 4])).then_inc(s_par, 16)
                sp.dma_start(dn_gain, A["dn_out_gain"].to_broadcast([P, P])).then_inc(s_par, 16)

            def level_masks(pool, masks, levels, sem_steps, flip):
                step = Steps(pool, sem_steps)
                step(pool.memset(masks, 0.0))
                for i in range(levels):
                    s_ = 1 << i
                    v = masks[:, i, :].rearrange("p (b h r) -> p b h r", h=2, r=s_)[:, :, 1 if flip else 0, :]
                    step(pool.memset(v, 1.0))
                    lo = 0 if flip else s_
                    step(pool.affine_select(out=v, in_=v, compare_op=ALU.is_ge, fill=0.0, base=-lo,
                                            pattern=[[-2 * s_, P // (2 * s_)], [0, s_]], channel_multiplier=1))
                    step(pool.affine_select(out=v, in_=v, compare_op=ALU.is_ge, fill=0.0, base=lo + s_ - 1,
                                            pattern=[[2 * s_, P // (2 * s_)], [0, s_]], channel_multiplier=-1))

            @block.gpsimd
            def _(pool):
                level_masks(pool, lev, 7, s_lv, False)

            @block.scalar
            def _(act):
                act.wait_ge(s_par, 64)
                act.activation(beta_.rearrange("p (t h) -> p t h", h=HD), ab[:, :, 0, :], ACT.Sigmoid).then_inc(s_sb, 1)
                act.wait_ge(s_conv, 1)
                act.activation(conv, conv, ACT.Silu).then_inc(s_silu, 1)
                act.activation(zsil, zsil, ACT.Silu).then_inc(s_silu, 1)
                act.wait_ge(s_silu, 1)
                act.activation(at(O_H, 8 * S), conv[:, 0:8, :].rearrange("p a t -> p (a t)"), ACT.Square).then_inc(s_sq, 1)
                act.wait_ge(s_gpre, 1)
                act.activation(tmp_, tmp_, ACT.Exp, scale=-1.0).then_inc(s_ge, 1)
                act.activation(dn_par[:, 8:12], dn_par[:, 0:4], ACT.Exp).then_inc(s_ge, 1)
                act.wait_ge(s_ge, 1)
                act.activation(tmp_, tmp_, ACT.Ln, bias=1.0).then_inc(s_gl, 1)
                act.wait_ge(s_ssum, 1)
                act.activation(at(O_H, 8 * S), psf[:, 0:8 * S], ACT.Sqrt, bias=eps).then_inc(s_sstd, 1)
                act.wait_ge(s_gco, 1)
                act.activation(eg_, gc_, ACT.Exp).then_inc(s_gexp, 1)
                act.wait_ge(s_diff, 1)
                act.activation(qgT, gcB[:, HD:U, :], ACT.Exp).then_inc(s_gexp, 1)
                act.activation(egk_[:, 0:HD], egk_[:, 0:HD], ACT.Exp).then_inc(s_gexp, 1)
                act.activation(Dm, Dm, ACT.Exp).then_inc(s_dexp, 1)
                act.activation(DT, DT, ACT.Exp).then_inc(s_dexp, 1)

            @block.vector
            def _(dve):
                step = Steps(dve, s_dv)
                dve.wait_ge(s_par, 64)
                a_ = gc_.rearrange("p (t h) -> p t h", h=HD)
                for tt in range(TT):
                    one = dve.tensor_tensor(gc_[:, tt * HD:(tt + 1) * HD], ab[:, tt, 1, :], dn_par[:, 4:8], ALU.add)
                step(one)
                step(dve.tensor_scalar(tmp_, gc_, -1.0, None, ALU.mult))
                dve.tensor_tensor(tmp_, tmp_, gc_, ALU.max).then_inc(s_gpre, 1)
                dve.wait_ge(s_tap, 1)
                dve.tensor_copy(taps, ps[:, 7, 0:48]).then_inc(s_tapo, 1)
                dve.wait_ge(s_tapo, 1)
                for i in range(4):
                    for t in range(12):
                        src, w = conv_in[:, t, i:i + S], taps[:, i * 12 + t:i * 12 + t + 1]
                        if i == 0:
                            one = dve.tensor_scalar(conv[:, t, :], src, w, None, ALU.mult)
                        else:
                            one = dve.scalar_tensor_tensor(out=conv[:, t, :], in0=src, scalar=w, in1=conv[:, t, :],
                                                           op0=ALU.mult, op1=ALU.add)
                    if i < 3:
                        step(one)
                one.then_inc(s_conv, 1)
                dve.wait_ge(s_gl, 1)
                step(dve.scalar_tensor_tensor(out=tmp_, in0=gc_, scalar=0.0, in1=tmp_, op0=ALU.max, op1=ALU.add))
                for tt in range(TT):
                    one = dve.scalar_tensor_tensor(out=g_[:, tt * HD:(tt + 1) * HD], in0=tmp_[:, tt * HD:(tt + 1) * HD],
                                                   scalar=-1.0, in1=dn_par[:, 8:12], op0=ALU.mult, op1=ALU.mult)
                step(one)
                step(dve.tensor_scalar(g_, g_, -110.0, None, ALU.max))
                dve.tensor_copy(X, wide(g_, P)).then_inc(s_g, 1)
                dve.wait_ge(s_sstd, 1)
                step(dve.reciprocal(at(O_H, 8 * S), at(O_H, 8 * S)))
                rn = at(O_H, 8, S)
                dve.scalar_tensor_tensor(out=conv[:, 0:4, :], in0=conv[:, 0:4, :], scalar=P ** -0.5, in1=rn[:, 0:4, :],
                                         op0=ALU.mult, op1=ALU.mult)
                dve.tensor_tensor(conv[:, 4:8, :], conv[:, 4:8, :], rn[:, 4:8, :], ALU.mult).then_inc(s_qkn, 1)
                dve.wait_ge(s_gcm, 1)
                step(dve.tensor_copy(gcB, psf[:, 2048:3072].rearrange("p (u t) -> p u t", t=P)))
                dve.tensor_copy(gc_, ps[:, 6, 0:U]).then_inc(s_gco, 1)
                dve.wait_ge(s_gco, 1)
                step(dve.tensor_tensor(Dm, wide(gc_, P), gcB, ALU.subtract))
                step(dve.tensor_scalar(DT, Dm, -1.0, 0.0, ALU.mult, ALU.min))
                step(dve.tensor_scalar(Dm, Dm, 0.0, None, ALU.min))
                dve.tensor_tensor(egk_[:, 0:HD], gcB[:, 0:HD, P - 1], gc_[:, 0:HD], ALU.subtract).then_inc(s_diff, 1)
                dve.wait_ge(s_dexp, 2)
                dve.wait_ge(s_gexp, 3)
                dve.wait_ge(s_sb, 1)
                step(dve.tensor_tensor(Dm, Dm, strict_low.unsqueeze(1).to_broadcast([P, U, P]), ALU.mult))
                step(dve.tensor_tensor(Dm, Dm, wide(beta_, P), ALU.mult))
                step(dve.tensor_tensor(DT, DT, upper.unsqueeze(1).to_broadcast([P, U, P]), ALU.mult))
                step(dve.tensor_tensor(beg_, beta_, eg_, ALU.mult))
                dve.wait_ge(s_kk, 1)
                dve.tensor_tensor(L, psf[:, 0:1024].rearrange("p (u t) -> p u t", t=P), Dm, ALU.mult).then_inc(s_L, 1)
                dve.tensor_copy(T, ident.unsqueeze(1).to_broadcast([P, U, P])).then_inc(s_L, 1)
                dve.tensor_copy(TI, ident.unsqueeze(1).to_broadcast([P, U, P])).then_inc(s_L, 1)
                dve.tensor_tensor(AT, psf[:, 1024:2048].rearrange("p (u t) -> p u t", t=P), DT, ALU.mult).then_inc(s_L, 1)
                step(dve.tensor_tensor(qgT, qgT, conv[:, 0:4, P:S], ALU.mult))
                dve.wait_ge(s_tk, 1)
                kt = psf[:, 2048:3072].rearrange("p (u t) -> p u t", t=P)
                vt = psf[:, 3072:4096].rearrange("p (u t) -> p u t", t=P)
                dve.tensor_tensor(kbg, kt, wide(beg_, P), ALU.mult)
                dve.tensor_tensor(kdec, kt[:, 0:HD, :], wide(egk_[:, 0:HD], P), ALU.mult)
                dve.tensor_tensor(vb, vt, wide(beta_, P), ALU.mult).then_inc(s_tko, 1)

            @block.tensor
            def _(pe):
                pe.wait_ge(s_par, 64)
                transposes(pe, [(ps[:, 7, 0:48], taps_rows)]).then_inc(s_tap, 1)
                pe.wait_ge(s_sq, 1)
                for b in range(4):
                    mm = pe.matmul(ps[:, b, :], ones, at(O_H, 8 * S)[:, b * 512:(b + 1) * 512], start=True, stop=True)
                mm.then_inc(s_ssum, 1)
                pe.wait_ge(s_g, 1)
                pe.matmul(ps[:, 6, 0:U], upper, g_, start=True, stop=True)
                for u in range(U):
                    mm = pe.matmul(psf[:, 2048 + u * P:2048 + (u + 1) * P], X[:, u, :], upper, start=True, stop=True)
                mm.then_inc(s_gcm, 1)
                pe.wait_ge(s_qkn, 1)
                for b in range(2):
                    for u in range(U):
                        c, hd = divmod(u, HD)
                        q, k = conv[:, hd, c * P:(c + 1) * P], conv[:, 4 + hd, c * P:(c + 1) * P]
                        mm = pe.matmul(psf[:, b * 1024 + u * P:b * 1024 + (u + 1) * P], k, (k, q)[b], start=True, stop=True)
                mm.then_inc(s_kk, 1)
                pe.wait_ge(s_gco, 1)
                transposes(pe, [(psf[:, 2048 + w * 1024 + u * P:2048 + w * 1024 + (u + 1) * P],
                                 conv[:, 4 + 4 * w + u % HD, u // HD * P:(u // HD + 1) * P])
                                for w in range(2) for u in range(U)]).then_inc(s_tk, 1)

        s_C, s_xp, s_xe, s_y, s_T = (sem("inv_" + n) for n in (
            "level_part", "x_product", "x_copied", "update_product", "updated"))
        (s_u, s_ue, s_uT, s_w, s_wT, s_st, s_ste, s_wS, s_vn, s_o, s_oe, s_std, s_dv) = (sem("delta_" + n) for n in (
            "u", "u0_copied", "u1_copied", "w", "w_copied", "state", "state_copied", "w_state", "v_new", "out",
            "out_sums", "out_std", "steps"))
        with nc.Block() as block:
            @block.gpsimd
            def _(pool):
                for i in range(7):
                    if i >= 2:
                        pool.wait_ge(s_xp, 2 * (i - 1))
                    pool.tensor_tensor(Cm[i % 2], L, lev[:, i:i + 1, :].to_broadcast([P, U, P]), ALU.mult)\
                        .then_inc(s_C, 1)

            @block.tensor
            def _(pe):
                for i in range(7):
                    pe.wait_ge(s_C, i + 1)
                    for a in range(2):
                        if i:
                            pe.wait_ge(s_T, 2 * (i - 1) + a + 1)
                        for u in range(4 * a, 4 * a + 4):
                            mm = pe.matmul(psf[:, u * P:(u + 1) * P], Cm[i % 2][:, u, :], TI[:, u, :], start=True, stop=True)
                        mm.then_inc(s_xp, 1)
                    for a in range(2):
                        pe.wait_ge(s_xe, 2 * i + a + 1)
                        for u in range(4 * a, 4 * a + 4):
                            pe.matmul(psf[:, 1024 + u * P:1024 + (u + 1) * P], X[:, u, :], T[:, u, :], start=True, stop=True)
                            mm = pe.matmul(psf[:, 2048 + u * P:2048 + (u + 1) * P], T[:, u, :], X[:, u, :],
                                           start=True, stop=True)
                        mm.then_inc(s_y, 1)
                pe.wait_ge(s_T, 14)
                for u in range(U):
                    mm = pe.matmul(psf[:, u * P:(u + 1) * P], TI[:, u, :], vb[:, u, :], start=True, stop=True)
                mm.then_inc(s_u, 1)
                for hd in range(HD):
                    mm = pe.matmul(ps[:, 2, hd * P:(hd + 1) * P], kbg[:, HD + hd, :], TI[:, HD + hd, :], start=True, stop=True)
                mm.then_inc(s_w, 1)
                pe.wait_ge(s_ue, 1)
                for hd in range(HD):
                    mm = pe.matmul(ps[:, 3, hd * P:(hd + 1) * P], kdec[:, hd, :], vnew[:, hd, :], start=True, stop=True)
                mm.then_inc(s_st, 1)
                for hd in range(HD):
                    mm = pe.matmul(ps[:, 5, hd * P:(hd + 1) * P], AT[:, hd, :], vnew[:, hd, :], start=True, stop=True)
                mm.then_inc(s_o, 1)
                pe.wait_ge(s_wT, 1)
                pe.wait_ge(s_ste, 1)
                for hd in range(HD):
                    mm = pe.matmul(ps[:, 4, hd * P:(hd + 1) * P], wT[:, hd, :], state[:, hd, :], start=True, stop=True)
                mm.then_inc(s_wS, 1)
                pe.wait_ge(s_vn, 1)
                for hd in range(HD):
                    pe.matmul(ps[:, 6, hd * P:(hd + 1) * P], qgT[:, hd, :], state[:, hd, :], start=True, stop=False)
                    mm = pe.matmul(ps[:, 6, hd * P:(hd + 1) * P], AT[:, HD + hd, :], vnew[:, HD + hd, :],
                                   start=False, stop=True)
                mm.then_inc(s_o, 1)

            @block.scalar
            def _(act):
                for i in range(7):
                    for a in range(2):
                        act.wait_ge(s_xp, 2 * i + a + 1)
                        if i:
                            act.wait_ge(s_y, 2 * (i - 1) + a + 1)
                        act.copy(X[:, 4 * a:4 * a + 4, :], ps[:, a, :].rearrange("p (u t) -> p u t", t=P)).then_inc(s_xe, 1)
                act.wait_ge(s_w, 1)
                act.copy(wT, ps[:, 2, :].rearrange("p (u t) -> p u t", t=P)).then_inc(s_wT, 1)
                act.wait_ge(s_st, 1)
                act.copy(state, ps[:, 3, :].rearrange("p (u t) -> p u t", t=P)).then_inc(s_ste, 1)
                act.wait_ge(s_oe, 1)
                act.activation(tiny[:, 8:16], tiny[:, 0:8], ACT.Sqrt, bias=eps, scale=1.0 / P).then_inc(s_std, 1)

            @block.vector
            def _(dve):
                step = Steps(dve, s_dv)
                for i in range(7):
                    for a in range(2):
                        dve.wait_ge(s_y, 2 * i + a + 1)
                        if i:
                            dve.wait_ge(s_T, 2 * i)
                        half = slice(4 * a, 4 * a + 4)
                        dve.tensor_tensor(T[:, half, :], T[:, half, :],
                                          ps[:, 2 + a, :].rearrange("p (u t) -> p u t", t=P), ALU.subtract)
                        dve.tensor_tensor(TI[:, half, :], TI[:, half, :],
                                          ps[:, 4 + a, :].rearrange("p (u t) -> p u t", t=P), ALU.subtract).then_inc(s_T, 1)
                dve.wait_ge(s_u, 1)
                dve.tensor_copy(vnew[:, 0:HD, :], ps[:, 0, :].rearrange("p (u t) -> p u t", t=P)).then_inc(s_ue, 1)
                dve.tensor_copy(vnew[:, HD:U, :], ps[:, 1, :].rearrange("p (u t) -> p u t", t=P)).then_inc(s_uT, 1)
                dve.wait_ge(s_uT, 1)
                dve.wait_ge(s_wS, 1)
                dve.tensor_tensor(vnew[:, HD:U, :], vnew[:, HD:U, :], ps[:, 4, :].rearrange("p (u t) -> p u t", t=P),
                                  ALU.subtract).then_inc(s_vn, 1)
                dve.wait_ge(s_o, 2)
                o = mix[:, :, 512:1024]
                step(dve.tensor_copy(o, ps[:, 5:7, :]))
                sq = at(O_C, TT, 512)
                step(dve.tensor_tensor(sq, o, o, ALU.mult))
                dve.tensor_reduce(tiny[:, 0:8], sq.rearrange("p t (h d) -> p (t h) d", d=P), AX, ALU.add).then_inc(s_oe, 1)
                dve.wait_ge(s_std, 1)
                step(dve.reciprocal(tiny[:, 16:24], tiny[:, 8:16]))
                for tt in range(TT):
                    o3 = o[:, tt, :].rearrange("p (h d) -> p h d", d=P)
                    step(dve.tensor_tensor(o3, o3, wide(tiny[:, 16 + 4 * tt:20 + 4 * tt], P), ALU.mult))
                    step(dve.tensor_tensor(o3, o3, dn_gain.unsqueeze(1).to_broadcast([P, HD, P]), ALU.mult))
                    step(dve.tensor_tensor(o[:, tt, :], o[:, tt, :], zsil[:, tt, :], ALU.mult))

        def turn_stage(tag, rows):
            s_t, s_hi, s_lo = (sem(f"{tag}_{n}") for n in ("transposed", "hi", "lo"))
            with nc.Block() as block:
                @block.tensor
                def _(pe):
                    turn_rows(pe, rows, s_t)

                @block.scalar
                def _(act):
                    turned_hi(act, s_t, s_hi)

                @block.vector
                def _(dve):
                    turned_lo(dve, s_hi, s_lo)

        def rows_stage(tag, seg, chunks, upto, left, dve_part):
            s_steps = sem(f"{tag}_steps")
            n0, g0 = seg
            units = UPC * chunks
            with nc.Block() as block:
                @block.sync
                def _(sp):
                    st.issue(sp, upto)

                @block.tensor
                def _(pe):
                    for i in range(units):
                        await_unit(pe, g0 + i, 0)
                        k, c = divmod(i, 2)
                        for tt in range(TT):
                            mm = three(pe, ps[:, 2 * tt + c, :], [a[:, k, tt * P:(tt + 1) * P] for a in left],
                                       [w[(g0 + i) % BUFFERS] for w in (w_hi, w_lo)], k == 0, k == units // 2 - 1)
                        mm.then_inc(unit_used, 1)

                @block.scalar
                def _(act):
                    for i in range(units):
                        split_hi(act, n0 + i // UPC, g0 + i, i % UPC, 0)

                @block.vector
                def _(dve):
                    for i in range(units):
                        split_lo(dve, n0 + i // UPC, g0 + i, i % UPC, 0)
                    dve.wait_ge(unit_used, used_value(g0 + units - 1))
                    dve_part(dve, Steps(dve, s_steps))

        def product_rows(tt):
            return psf[:, tt * D:(tt + 1) * D]

        turn_stage("mix1", mix)
        O_TMP = O_C

        def add_mix(dve, step):
            for tt in range(TT):
                step(dve.tensor_tensor(at(O_TMP + tt * D, D), product_rows(tt), gate1, ALU.mult))
                step(dve.tensor_tensor(x[:, tt, :], x[:, tt, :], at(O_TMP + tt * D, D), ALU.add))
            step(dve.tensor_copy(gate2, mods[:, 5, :]))

        rows_stage("w_out", n_wout, 4, n_query[0] + SLOTS, (x_hi, x_lo), add_mix)

        s_x = sem("norm2_gain_loaded")
        s_sp = sem("x_stored")
        with nc.Block() as block:
            @block.sync
            def _(sp):
                sp.dma_start(x_spill, at(O_R, TT * D)).then_inc(s_sp, 16)
                sp.dma_start(gain, A["norm2_gain"].to_broadcast([P, D])).then_inc(s_x, 16)
                sp.wait_ge(s_sp, 16)
        norm_stage("norm2", h, x, s_x, 16, shift2, scale2)

        NH, KD, NK, TOP = 8, 256, 128, 16
        acts = at(O_R, P, S)
        CLEAR = 72
        O_Q = O_R + CLEAR * S
        qT = at(O_Q - 2 * NH * S, 2 * NH, S)
        qrows = at(O_Q, TT, NH * KD)
        score = at(O_Q, TT * 2 * NH, NK)
        O_K = O_Q + TT * NH * KD
        keys = at(O_K, 2, P)
        keysT = at(O_K + 256, 2, P)
        q_gain = at(O_K + 512, KD)
        O_V = O_K + 768
        best = at(O_V, TT * 2 * NH, TOP)
        best_at = at(O_V + 512, TT * 2 * NH, TOP)
        best_ix = at(O_V + 1024, TT * 2 * NH, TOP)
        picked = at(O_V + 1536, TT * NH, TOP)
        picked_at = at(O_V + 1792, TT * NH, TOP)
        O_M = O_V + 2048
        cand = at(O_M, TT * NH, TOP * TOP)
        part_of = at(O_M + 4096, 2, P)
        part_u = at(O_M + 4352, 2, P)
        assert O_M + 4608 <= O_R + P * S
        pickT = at(O_PICKS, 3, S)
        (s_ld, s_qa, s_qv, s_sq, s_std, s_qn, s_kt, s_kto, s_t, s_tv, s_ta, s_sc, s_scv, s_sca, s_dv) = (
            sem("query_" + n) for n in (
                "params", "rows_act", "rows_dve", "squares", "std", "normed", "keys_transposed", "keysT", "transposed",
                "qT_dve", "qT_act", "scores", "scores_dve", "scores_act", "steps"))
        with nc.Block() as block:
            @block.sync
            def _(sp):
                sp.dma_start(keys[:, 0, :], A["peer_sub_keys_1"][0]).then_inc(s_ld, 16)
                sp.dma_start(keys[:, 1, :], A["peer_sub_keys_2"][0]).then_inc(s_ld, 16)
                sp.dma_start(q_gain, A["peer_query_gain"].to_broadcast([P, KD])).then_inc(s_ld, 16)
                st.issue(sp, n_down[0] + SLOTS)

            @block.tensor
            def _(pe):
                for c in range(4):
                    if c >= 2:
                        pe.wait_ge(s_qv, c - 1)
                        pe.wait_ge(s_qa, c - 1)
                    product_group(pe, c, n_query[1] + KT * c, 0, "t", (x_hi, x_lo))
                pe.wait_ge(s_ld, 48)
                transposes(pe, [(ps[:, 6, i * P:(i + 1) * P], keys[:, i, :]) for i in range(2)]).then_inc(s_kt, 1)
                pe.wait_ge(s_kto, 1)
                pe.wait_ge(s_qa, 4)
                pe.wait_ge(s_qn, 1)
                for b in range(8):
                    transposes(pe, [(ps[:, b, (u % 2) * S + tt * P:(u % 2) * S + (tt + 1) * P],
                                     qrows[:, tt, u * P:(u + 1) * P])
                                    for u in (2 * b, 2 * b + 1) for tt in range(TT)]).then_inc(s_t, 1)
                for b in range(8):
                    if b == 0:
                        pe.wait_ge(s_tv, 4)
                        pe.wait_ge(s_ta, 4)
                    for j in range(4):
                        u = 4 * b + j
                        mm = pe.matmul(ps[:, b, j * P:(j + 1) * P], qT[:, u % 16, u // 16 * P:(u // 16 + 1) * P],
                                       keysT[:, u % 2, :], start=True, stop=True)
                    mm.then_inc(s_sc, 1)

            @block.vector
            def _(dve):
                step = Steps(dve, s_dv)
                lo_groups(dve, n_query, 4, lambda c: dve.tensor_copy(
                    qrows[:, 0, c * 512:(c + 1) * 512], ps[:, c % 2 * 4, :]).then_inc(s_qv, 1))
                dve.wait_ge(s_kt, 1)
                dve.tensor_copy(keysT, ps[:, 6, 0:256].rearrange("p (a n) -> p a n", n=P)).then_inc(s_kto, 1)
                dve.wait_ge(s_sq, 2)
                step(dve.tensor_reduce(tiny[:, 0:16], at(O_Q - 4096, TT * NH, KD), AX, ALU.add))
                dve.wait_ge(s_std, 1)
                step(dve.reciprocal(tiny[:, 32:48], tiny[:, 16:32]))
                for tt in range(TT):
                    for hd in range(NH):
                        v = qrows[:, tt, hd * KD:(hd + 1) * KD]
                        one = dve.scalar_tensor_tensor(out=v, in0=v, scalar=tiny[:, 32 + tt * NH + hd:33 + tt * NH + hd],
                                                       in1=q_gain, op0=ALU.mult, op1=ALU.mult)
                one.then_inc(s_qn, 1)
                for b in range(0, 8, 2):
                    dve.wait_ge(s_t, b + 1)
                    dve.tensor_copy(qT[:, 2 * b:2 * b + 2, :], ps[:, b, :].rearrange("p (a t) -> p a t", t=S)).then_inc(s_tv, 1)
                for b in range(0, 8, 2):
                    dve.wait_ge(s_sc, b + 1)
                    dve.tensor_copy(score[:, 4 * b:4 * b + 4, :], ps[:, b, :].rearrange("p (a t) -> p a t", t=P)).then_inc(s_scv, 1)

            @block.scalar
            def _(act):
                hi_groups(act, n_query, 4, lambda c: act.copy(
                    qrows[:, 1, c * 512:(c + 1) * 512], ps[:, c % 2 * 4 + 1, :]).then_inc(s_qa, 1))
                act.wait_ge(s_qa, 4)
                act.wait_ge(s_qv, 4)
                for tt in range(TT):
                    act.activation(at(O_Q - 4096 + tt * 2048, 2048), qrows[:, tt, :], ACT.Square).then_inc(s_sq, 1)
                act.wait_ge(s_dv, 1)
                act.activation(tiny[:, 16:32], tiny[:, 0:16], ACT.Sqrt, bias=eps, scale=1.0 / KD).then_inc(s_std, 1)
                for b in range(1, 8, 2):
                    act.wait_ge(s_t, b + 1)
                    act.copy(qT[:, 2 * b:2 * b + 2, :], ps[:, b, :].rearrange("p (a t) -> p a t", t=S)).then_inc(s_ta, 1)
                for b in range(1, 8, 2):
                    act.wait_ge(s_sc, b + 1)
                    act.copy(score[:, 4 * b:4 * b + 4, :], ps[:, b, :].rearrange("p (a t) -> p a t", t=P)).then_inc(s_sca, 1)

        NI = 2
        (s_E, s_L, s_M, s_G, s_route, s_dv) = (sem("experts_" + n) for n in (
            "hi", "lo", "product", "gelu", "routed", "steps"))
        n0 = n_down[0]
        ROUND = NI * SLOTS
        d_hi, d_lo = ([atr(o + i * D, D) for i in range(2)] for o in (O_W_HI, O_W_LO))

        with nc.Block() as block:
            @block.sync
            def _(sp):
                st.issue(sp, n_up[0] + SLOTS)

            @block.tensor
            def _(pe):
                pe.sem_inc(s_M, 2)

                def turn(i, rounds):
                    if i % NI == 0:
                        pe.wait_ge(landed[(n0 + i // NI) % SLOTS], rounds * 16 + st.landed_value(n0 + i // NI))
                    pe.wait_ge(s_L, rounds * ROUND + (i + 1))
                    w = st.words(n0 + i // NI, i % NI * D, D)
                    b = i % 2
                    transposes(pe, [(psf[:, b * 1024 + k * P:b * 1024 + (k + 1) * P], w[:, k * P:(k + 1) * P])
                                    for k in range(KT)]).then_inc(turned, 1)

                def product(i, rounds):
                    pe.wait_ge(s_L, rounds * ROUND + (i + 3))
                    if i % 2 == 0:
                        pe.wait_ge(s_G, rounds * (ROUND // 2) + (i // 2 + 1))
                    o = ps[:, 4 + i // 2 % 2, i % 2 * S:(i % 2 + 1) * S]
                    for k in range(KT):
                        ks = slice(k * P, (k + 1) * P)
                        mm = three(pe, o, [d_hi[i % 2][:, ks], d_lo[i % 2][:, ks]], [x_hi[:, k, :], x_lo[:, k, :]],
                                   k == 0, k == KT - 1)
                    mm.then_inc(s_M, 1)

                turn(0, 0)
                with pe.Fori(0, P // ROUND - 1) as r:
                    for i in range(ROUND):
                        turn(i + 1, r)
                        product(i, r)
                for i in range(P - ROUND, P):
                    if i + 1 < P:
                        turn(i + 1, 0)
                    product(i, 0)

            @block.scalar
            def _(act):
                act.sem_inc(s_G, 2)

                def hi(i, rounds):
                    act.wait_ge(s_M, rounds * ROUND + (i + 1))
                    act.wait_ge(turned, rounds * ROUND + (i + 1))
                    act.copy(d_hi[i % 2], psf[:, i % 2 * 1024:(i % 2 + 1) * 1024]).then_inc(s_E, 1)

                def gelu(p, rounds):
                    act.wait_ge(s_M, rounds * ROUND + (2 * p + 4))
                    act.wait_ge(s_const, 1)
                    act.activation(mem[:, bass.ds(rounds * (ROUND * S) + (O_R + 2 * p * S), 2 * S)],
                                   ps[:, 4 + p % 2, :], ACT.Gelu).then_inc(s_G, 1)

                def round_(rounds):
                    for i in range(1, ROUND + 1):
                        hi(i, rounds)
                        if i % 2 == 0:
                            gelu(i // 2 - 1, rounds)

                hi(0, 0)
                with act.Fori(0, CLEAR // ROUND) as r:
                    round_(r)
                act.wait_ge(s_route, 1)
                with act.Fori(CLEAR // ROUND, P // ROUND - 1) as r:
                    round_(r)
                for i in range(P - ROUND + 1, P):
                    hi(i, 0)
                    if i % 2 == 0:
                        gelu(i // 2 - 1, 0)
                gelu(P // 2 - 1, 0)

            @block.vector
            def _(dve):
                step = Steps(dve, s_dv)
                dve.sem_inc(s_L, 2)
                u32 = lambda ap: ap.bitcast(U32)

                def lo(i):
                    dve.wait_ge(s_E, i + 1)
                    dve.tensor_tensor(d_lo[i % 2], psf[:, i % 2 * 1024:(i % 2 + 1) * 1024], d_hi[i % 2].bitcast(F32),
                                      ALU.subtract).then_inc(s_L, 1)

                def top16(values, top, where, rows):
                    for r in rows:
                        one = dve.max(top[:, r, 0:8], values[:, r, :])
                        yield
                    step(one)
                    for r in rows:
                        one = dve.max_index(u32(where[:, r, 0:8]), top[:, r, 0:8], values[:, r, :])
                        yield
                    step(one)
                    for r in rows:
                        one = dve.match_replace(values[:, r, :], top[:, r, 0:8], values[:, r, :], -3.0e38)
                        yield
                    step(one)
                    for r in rows:
                        one = dve.max(top[:, r, 8:16], values[:, r, :])
                        yield
                    step(one)
                    for r in rows:
                        one = dve.max_index(u32(where[:, r, 8:16]), top[:, r, 8:16], values[:, r, :])
                        yield
                    step(one)

                def routing():
                    yield from top16(score, best, best_at, range(TT * 2 * NH))
                    step(dve.tensor_copy(best_ix, u32(best_at)))
                    yield
                    for tt in range(TT):
                        for hd in range(NH):
                            a = best[:, tt * 16 + 2 * hd, :]
                            b = best[:, tt * 16 + 2 * hd + 1, :]
                            one = dve.tensor_tensor(cand[:, tt * NH + hd, :].rearrange("p (a b) -> p a b", b=TOP), wide(a, TOP),
                                                    b.unsqueeze(1).to_broadcast([P, TOP, TOP]), ALU.add)
                            yield
                    step(one)
                    yield from top16(cand, picked, picked_at, range(TT * NH))
                    for tt in range(TT):
                        at_ = u32(at(O_V + 1792 + tt * P, P))
                        step(dve.tensor_scalar(u32(part_u[:, 0, :]), at_, 4, None, ALU.logical_shift_right))
                        step(dve.tensor_scalar(u32(part_u[:, 1, :]), at_, 15, None, ALU.bitwise_and))
                        step(dve.tensor_copy(part_of, u32(part_u)))
                        yield
                        eq = at(O_M, P, TOP)
                        for half in range(2):
                            step(dve.tensor_tensor(eq, wide(part_of[:, half, :], TOP),
                                                   iota[:, 0:TOP].unsqueeze(1).to_broadcast([P, P, TOP]), ALU.is_equal))
                            for _ in range(5):
                                yield
                            for hd in range(NH):
                                e3 = eq[:, hd * TOP:(hd + 1) * TOP, :]
                                ix = best_ix[:, tt * 16 + 2 * hd + half, :]
                                one = dve.tensor_tensor(e3, e3, ix.unsqueeze(1).to_broadcast([P, TOP, TOP]), ALU.mult)
                                yield
                            step(one)
                            step(dve.tensor_reduce(pickT[:, half, tt * P:(tt + 1) * P], eq, AX, ALU.add))
                            for _ in range(5):
                                yield
                        pk = picked[:, tt * NH:(tt + 1) * NH, :]
                        step(dve.tensor_tensor(pickT[:, 2, tt * P:(tt + 1) * P].rearrange("p (h j) -> p h j", j=TOP), pk,
                                               pk[:, :, 0:1].to_broadcast([P, NH, TOP]), ALU.subtract))
                    dve.drain().then_inc(s_route, 1)

                route = routing()
                for i in range(P):
                    lo(i)
                    for _ in range(5):
                        next(route, None)
                for _ in route:
                    pass

        GT = 4
        GB = 4
        one1 = at(O_W_HI, GB, GT * P)
        one2 = at(O_W_LO, GB, GT * P)
        gated = at(O_X_HI, GB, GT * P)
        (s_e, s_gn, s_t, s_pt, s_o2, s_gd, s_mm, s_w, s_dv) = (sem("gates_" + n) for n in (
            "exp", "normed", "transposed", "picksT", "onehots", "gated", "product", "applied", "steps"))
        NG_ = S // GT
        with nc.Block() as block:
            @block.scalar
            def _(act):
                act.activation(pickT[:, 2, :], pickT[:, 2, :], ACT.Exp).then_inc(s_e, 1)

            @block.tensor
            def _(pe):
                pe.wait_ge(s_gn, 1)
                transposes(pe, [(psf[:, (i * TT + tt) * P:(i * TT + tt + 1) * P], pickT[:, i, tt * P:(tt + 1) * P])
                                for i in range(3) for tt in range(TT)]).then_inc(s_t, 1)
                pe.wait_ge(s_pt, 1)
                with pe.Fori(0, NG_ // GB) as r:
                    for b in range(GB):
                        pe.wait_ge(s_gd, r * GB + (b + 1))
                        pe.wait_ge(s_w, r * GB + (b + 1))
                        for j in range(GT):
                            mm = pe.matmul(ps[:, 2 + b, j * P:(j + 1) * P], one1[:, b, j * P:(j + 1) * P],
                                           gated[:, b, j * P:(j + 1) * P], start=True, stop=True)
                        mm.then_inc(s_mm, 1)

            @block.gpsimd
            def _(pool):
                pool.wait_ge(s_pt, 1)
                with pool.Fori(0, NG_ // GB) as r:
                    for b in range(GB):
                        pool.wait_ge(s_o2, r * GB + (b + 1))
                        pool.wait_ge(s_const, 1)
                        pool.tensor_tensor(gated[:, b, :].rearrange("p (t i) -> p t i", i=P),
                                           one2[:, b, :].rearrange("p (t i) -> p t i", i=P),
                                           wide(mem[:, bass.ds(r * (GB * GT) + (O_PICKS + 2 * S + b * GT), GT)], P),
                                           ALU.mult).then_inc(s_gd, 1)

            @block.vector
            def _(dve):
                step = Steps(dve, s_dv)
                dve.wait_ge(s_e, 1)
                g3 = pickT[:, 2, :].rearrange("p (a j) -> p a j", j=TOP)
                step(dve.tensor_reduce(tiny[:, 0:16], g3, AX, ALU.add))
                step(dve.reciprocal(tiny[:, 16:32], tiny[:, 0:16]))
                dve.tensor_tensor(g3, g3, wide(tiny[:, 16:32], TOP), ALU.mult).then_inc(s_gn, 1)
                dve.wait_ge(s_t, 1)
                dve.tensor_copy(at(O_PICKS, 3 * S), psf[:, 0:3 * S]).then_inc(s_pt, 1)
                dve.sem_inc(s_mm, GB)
                dve.sem_inc(s_w, GB)
                dve.wait_ge(s_pt, 1)

                def onehots(j, r):
                    b, t0 = j % GB, r * (GB * GT) + j * GT
                    dve.wait_ge(s_mm, r * GB + (j + 1))
                    dve.tensor_tensor(one1[:, b, :].rearrange("p (t i) -> p t i", i=P),
                                      wide(mem[:, bass.ds(t0 + O_PICKS, GT)], P),
                                      iota.unsqueeze(1).to_broadcast([P, GT, P]), ALU.is_equal)
                    dve.tensor_tensor(one2[:, b, :].rearrange("p (t i) -> p t i", i=P),
                                      wide(mem[:, bass.ds(t0 + (O_PICKS + S), GT)], P),
                                      iota.unsqueeze(1).to_broadcast([P, GT, P]), ALU.is_equal).then_inc(s_o2, 1)

                def apply(j, r):
                    dve.wait_ge(s_mm, r * GB + (j + GB + 1))
                    a = acts[:, :, bass.ds(r * (GB * GT) + j * GT, GT)]
                    dve.tensor_tensor(a, a, ps[:, 2 + j % GB, :].rearrange("p (t i) -> p i t", i=P), ALU.mult)\
                        .then_inc(s_w, 1)

                onehots(0, 0)
                onehots(1, 0)
                with dve.Fori(0, NG_ // GB - 1) as r:
                    for j in range(GB):
                        onehots(j + 2, r)
                        apply(j, r)
                for j in range(NG_ - GB, NG_):
                    if j + 2 < NG_:
                        onehots(j + 2, 0)
                    apply(j, 0)

        n0, g0 = n_up
        (s_ld, s_ah, s_al, s_hi, s_lo, s_t, s_end, s_dv) = (sem("up_" + n) for n in (
            "x_loaded", "weights_hi", "weights_lo", "yT_act", "yT_dve", "transposed", "last_product", "steps"))
        x_back = at(O_R + TT * D, TT, D)
        yT = at(O_X_HI, KT, S)
        a_hi, a_lo = (lambda b: atr(O_X_HI + b * 1024, 1024)), (lambda b: atr(O_X_LO + b * 1024, 1024))
        with nc.Block() as block:
            @block.sync
            def _(sp):
                st.issue(sp, n_in2a[0] + SLOTS)
                sp.wait_ge(s_end, 1)
                sp.dma_start(at(O_R + TT * D, TT * D), x_spill).then_inc(s_ld, 16)

            @block.tensor
            def _(pe):
                for b in range(4):
                    pe.matmul(ps[:, b, :], zeros, at(O_CONST, 512), start=True, stop=False, skip_group_check=True)

                def units(i, rounds, last=False):
                    b = i // 4 % 2
                    if i % 4 == 0:
                        pe.wait_ge(s_al, rounds * 2 + (i // 4 + 1))
                    for u in range(2):
                        await_unit(pe, g0 + 2 * i + u, rounds)
                        w = (2 * i + u) % BUFFERS
                        for kk in range(4):
                            k, ks = 4 * u + kk, slice(kk * P, (kk + 1) * P)
                            mm = three(pe, ps[:, k // 2, k % 2 * S:(k % 2 + 1) * S], [w_hi[w][:, ks], w_lo[w][:, ks]],
                                       [v(b)[:, i % 4 * S:(i % 4 + 1) * S] for v in (a_hi, a_lo)], False, last)
                        mm.then_inc(unit_used, 1)
                with pe.Fori(0, P // 8 - 1) as r:
                    for i in range(8):
                        units(i, r)
                for i in range(P - 8, P):
                    units(i, 0, i == P - 1)
                pe.wait_ge(s_hi, 1)
                pe.wait_ge(s_lo, 1)
                transposes(pe, [(psf[:, 2048 + tt * D + k * P:2048 + tt * D + (k + 1) * P], yT[:, k, tt * P:(tt + 1) * P])
                                for tt in range(TT) for k in range(KT)]).then_inc(s_t, 1)

            @block.scalar
            def _(act):
                def weights_hi(q, r):
                    act.wait_ge(s_const, 1)
                    act.copy(a_hi(q % 2), mem[:, bass.ds(r * (8 * S) + (O_R + q * (4 * S)), 4 * S)]).then_inc(s_ah, 1)

                def round_(r, last=False):
                    for i in range(16):
                        j = i + (2 * P - 16 if last else 0)
                        split_hi(act, n0 + j // UPC, g0 + j, j % UPC, r)
                        if i % 8 == 3 and not (last and i > 8):
                            weights_hi(i // 8 + 1 + (2 * (P // 8 - 1) if last else 0), 0 if last else r)
                weights_hi(0, 0)
                with act.Fori(0, P // 8 - 1) as r:
                    round_(r)
                round_(0, last=True)
                act.wait_ge(unit_used, used_value(g0 + 2 * P - 1))
                act.copy(at(O_X_HI, 1024), psf[:, 0:1024]).then_inc(s_hi, 1)

            @block.gpsimd
            def _(pool):
                with pool.Fori(0, P // 8) as r:
                    for q in range(2):
                        pool.wait_ge(s_ah, r * 2 + (q + 1))
                        pool.wait_ge(s_const, 1)
                        pool.tensor_tensor(a_lo(q), mem[:, bass.ds(r * (8 * S) + (O_R + q * (4 * S)), 4 * S)],
                                           a_hi(q).bitcast(F32), ALU.subtract).then_inc(s_al, 1)

            @block.vector
            def _(dve):
                step = Steps(dve, s_dv)
                with dve.Fori(0, P // 8) as r:
                    for i in range(16):
                        split_lo(dve, n0 + i // UPC, g0 + i, i % UPC, r)
                dve.wait_ge(unit_used, used_value(g0 + 2 * P - 1))
                dve.tensor_copy(at(O_X_HI + 1024, 1024), psf[:, 1024:2048]).then_inc(s_lo, 1)
                dve.sem_inc(s_end, 1)
                dve.wait_ge(s_t, 1)
                dve.wait_ge(s_ld, 16)
                for tt in range(TT):
                    step(dve.tensor_tensor(x[:, tt, :], psf[:, 2048 + tt * D:2048 + (tt + 1) * D], gate2, ALU.mult))
                    step(dve.tensor_tensor(x[:, tt, :], x[:, tt, :], x_back[:, tt, :], ALU.add))

        renew_semaphores()

        O_F = O_R + TT * D
        qfT = at(O_F, 16, S)
        O_P2 = O_F + 16 * S
        N_P2 = 7 * D
        p2 = at(O_P2, TT, N_P2)
        O_W = O_P2 + TT * N_P2

        s_x = sem("norm1_2_gain_loaded")
        with nc.Block() as block:
            @block.sync
            def _(sp):
                sp.dma_start(gain, A["norm1_gain_2"].to_broadcast([P, D])).then_inc(s_x, 16)
        norm_stage("norm1_2", h, x, s_x, 16)

        HH = 8
        NB = HH * S
        cum = at(O_W, HH, S)
        Z = [at(o, HH, S) for o in (O_W + NB, O_W + 2 * NB, O_X_HI)]
        kx = at(O_W + 3 * NB, HH, S)
        sT = at(O_W + 4 * NB, 2 * HH, P)
        cross = at(O_W + 5 * NB, HH, P)
        lev = at(O_W + 5 * NB + HH * P, 7, P)
        logits = mem[0:16, O_W + 5 * NB + HH * P + 7 * P:O_W + 5 * NB + HH * P + 8 * P]
        O_L = O_W + 5 * NB + HH * P + 8 * P
        lbT = at(O_L, 6, HH)
        hg_gain = at(O_L + 48, D)
        assert O_L + 48 + D <= WORDS
        q3, f3 = qfT[:, 0:HH, :], qfT[:, HH:2 * HH, :]
        SD = 64
        qk = p2[:, :, 2 * D:4 * D]
        sb_gain = at(O_W + 4 * NB, 2, D)
        sq2 = at(O_W + NB, TT, 2 * D)
        std2 = tiny[:, 64:128]

        (s_bank_v, s_bank_a, s_par, s_lv, s_lt, s_lm, s_le, s_sg, s_f, s_ln, s_dv, s_sq, s_sum, s_std, s_rstd, s_pl) = (
            sem("proj2_" + n) for n in (
                "bank_out_dve", "bank_out_act", "params", "level_steps", "logits_transposed", "logits_shifted",
                "logits_exp", "sigmoids", "forget", "log_forget", "steps", "qk_squares", "qk_sums", "qk_std",
                "qk_inverse_std", "pool_steps"))
        with nc.Block() as block:
            @block.sync
            def _(sp):
                sp.dma_start(logits, A["lb_logits_2"].rearrange("l (k p) -> (l k) p", p=P)).then_inc(s_par, 16)
                sp.dma_start(hg_gain, A["hg_out_norm_2"].rearrange("l h d -> l (h d)").to_broadcast([P, D])).then_inc(s_par, 16)
                for i, name in enumerate(("sb_q_norm_2", "sb_k_norm_2")):
                    sp.dma_start(sb_gain[:, i, :], A[name].rearrange("l h d -> l (h d)").to_broadcast([P, D])).then_inc(s_par, 16)
                st.issue(sp, n_hgo[0] + SLOTS)

            @block.tensor
            def _(pe):
                for c in range(4):
                    if c >= 2:
                        pe.wait_ge(s_bank_v, c - 1)
                        pe.wait_ge(s_bank_a, c - 1)
                    product_group(pe, c, n_in2a[1] + KT * c, 0, "f", (x_hi, x_lo))
                pe.wait_ge(s_bank_v, 3)
                pe.wait_ge(s_bank_a, 3)
                pe.wait_ge(s_par, 64)
                transposes(pe, [(ps[:, 3, 0:16], logits)]).then_inc(s_lt, 1)
                with pe.Fori(0, 7) as r:
                    for c in range(2):
                        pe.wait_ge(s_bank_v, r * 2 + (c + 3))
                        pe.wait_ge(s_bank_a, r * 2 + (c + 3))
                        product_group(pe, c, n_in2b[1] + KT * c, r, "t", (x_hi, x_lo))

            def qf_out(b, c):
                t = c * 4 + b * 2
                return qfT[:, t:t + 2, :], ps[:, c % 2 * 4 + 2 * b:c % 2 * 4 + 2 * b + 2, 0:S]

            def loop_groups(eng, b, split, copy, s_bank, early, late):
                n0, g0 = n_in2b

                def empty(c, rounds):
                    eng.wait_ge(unit_used, rounds * 16 + used_value(g0 + KT * c + 7))
                    eng.wait_ge(s_const, 1)
                    copy(mem[:, bass.ds(rounds * 1024 + (O_P2 + b * N_P2 + c * 512), 512)],
                         ps[:, c % 2 * 4 + b, :]).then_inc(s_bank, 1)
                for u in range(16):
                    split(eng, n0 + u // UPC, g0 + u, u % UPC, 0)
                    if u == 11:
                        empty(0, 0)
                    early(u)
                with eng.Fori(0, 4) as r:
                    for u in range(16, 32):
                        split(eng, n0 + u // UPC, g0 + u, u % UPC, r)
                        if u % 8 == 3:
                            empty(u // 8 - 1, r)
                for v in (5, 6):
                    for u in range(16 * v, 16 * v + 16):
                        split(eng, n0 + u // UPC, g0 + u, u % UPC, 0)
                        if u % 8 == 3:
                            empty(u // 8 - 1, 0)
                        late(v, u % 16)
                empty(13, 0)

            @block.vector
            def _(dve):
                step = Steps(dve, s_dv)
                lo_groups(dve, n_in2a, 4, lambda c: dve.tensor_copy(*qf_out(0, c)).then_inc(s_bank_v, 1))

                def early(u):
                    if u == 1:
                        dve.wait_ge(s_lt, 1)
                        step(dve.tensor_copy(lbT[:, 0:2, :], ps[:, 3, 0:16].rearrange("p (l k) -> p l k", l=2)))
                        step(dve.tensor_tensor(lbT[:, 2, :], lbT[:, 0, :], lbT[:, 1, :], ALU.max))
                    elif u == 2:
                        step(dve.tensor_tensor(lbT[:, 0, :], lbT[:, 0, :], lbT[:, 2, :], ALU.subtract))
                        dve.tensor_tensor(lbT[:, 1, :], lbT[:, 1, :], lbT[:, 2, :], ALU.subtract).then_inc(s_lm, 1)
                    elif u == 7:
                        dve.wait_ge(s_le, 1)
                        step(dve.tensor_tensor(lbT[:, 2, :], lbT[:, 0, :], lbT[:, 1, :], ALU.add))
                        step(dve.reciprocal(lbT[:, 3, :], lbT[:, 2, :]))
                    elif u == 8:
                        step(dve.tensor_tensor(lbT[:, 4, :], lbT[:, 0, :], lbT[:, 3, :], ALU.mult))
                        step(dve.tensor_scalar(lbT[:, 5, :], lbT[:, 4, :], -1.0, 1.0, ALU.mult, ALU.add))
                    elif u in (9, 10):
                        dve.wait_ge(s_sg, 1)
                        for hd in range(4 * (u - 9), 4 * (u - 8)):
                            one = dve.tensor_scalar(f3[:, hd, :], f3[:, hd, :], lbT[:, 5, hd:hd + 1],
                                                    lbT[:, 4, hd:hd + 1], ALU.mult, ALU.add)
                        one.then_inc(s_f, 1)
                    elif u == 12:
                        dve.wait_ge(s_f, 2)
                        step(dve.tensor_scalar(kx, f3, -1.0, 1.0, ALU.mult, ALU.add))

                def late(v, u):
                    if v == 5 and u < 4:
                        tt, half = divmod(u, 2)
                        dve.wait_ge(s_sq, 1)
                        dve.tensor_reduce(tiny[:, 16 * u:16 * u + 16], sq2[:, tt, half * D:(half + 1) * D]
                                          .rearrange("p (h d) -> p h d", d=SD), AX, ALU.add).then_inc(s_sum, 1)
                    elif v == 5 and u < 12:
                        hd = u - 4
                        dve.wait_ge(s_ln, 1)
                        dve.tensor_tensor_scan(f3[:, hd, :], ones[:, 0:1].to_broadcast([P, S]), cum[:, hd, :], 0.0,
                                               ALU.mult, ALU.add)
                    elif v == 5 and u == 12:
                        dve.wait_ge(s_std, 1)
                        step(dve.reciprocal(std2, std2))
                        q_std = std2.rearrange("p (t h) -> p t h", t=TT)[:, :, 0:16]
                        dve.tensor_scalar(q_std, q_std, SD ** -0.5, None, ALU.mult).then_inc(s_rstd, 1)

                loop_groups(dve, 0, split_lo, dve.tensor_copy, s_bank_v, early, late)

            @block.scalar
            def _(act):
                hi_groups(act, n_in2a, 4, lambda c: act.copy(*qf_out(1, c)).then_inc(s_bank_a, 1))

                def early(u):
                    if u == 2:
                        act.wait_ge(s_bank_v, 4)
                        act.wait_ge(s_bank_a, 4)
                        act.activation(f3, f3, ACT.Sigmoid).then_inc(s_sg, 1)
                    elif u == 5:
                        act.wait_ge(s_lm, 1)
                        act.activation(lbT[:, 0:2, :], lbT[:, 0:2, :], ACT.Exp).then_inc(s_le, 1)
                    elif u == 13:
                        act.wait_ge(s_f, 2)
                        act.activation(cum, f3, ACT.Ln).then_inc(s_ln, 1)

                def late(v, u):
                    if v == 5 and u == 6:
                        act.wait_ge(s_sum, 4)
                        act.activation(std2, tiny[:, 0:64], ACT.Sqrt, bias=eps, scale=1.0 / SD).then_inc(s_std, 1)

                loop_groups(act, 1, split_hi, act.copy, s_bank_a, early, late)

            @block.gpsimd
            def _(pool):
                level_masks(pool, lev, 7, s_lv, True)
                step = Steps(pool, s_pl)
                pool.wait_ge(s_bank_v, 12)
                pool.wait_ge(s_bank_a, 12)
                pool.tensor_tensor(sq2, qk, qk, ALU.mult).then_inc(s_sq, 1)
                pool.wait_ge(s_rstd, 1)
                pool.wait_ge(s_par, 64)
                for tt in range(TT):
                    v = qk[:, tt, :].rearrange("p (h d) -> p h d", d=SD)
                    step(pool.tensor_tensor(v, v, wide(std2[:, 32 * tt:32 * tt + 32], SD), ALU.mult))
                    step(pool.tensor_tensor(qk[:, tt, :], qk[:, tt, :], sb_gain.rearrange("p a n -> p (a n)"), ALU.mult))

        (s_zero, s_sg, s_d, s_e, s_z, s_m, s_p, s_dv, s_o, s_ss, s_std) = (
            sem("hgrn_" + n) for n in (
                "scores_zero", "sigmoids", "exponents", "exps", "scaled", "level_product", "level_taken", "steps", "out",
                "out_squares", "out_std"))
        with nc.Block() as block:
            def halves(v, s_):
                return v.rearrange("p h (b f r) -> p (h b) f r", f=2, r=s_)

            def scale_level(pool, i):
                e, q, k = (halves(v, 1 << i) for v in (Z[i % 3], q3, kx))
                pool.tensor_tensor(e[:, :, 1, :], e[:, :, 1, :], q[:, :, 1, :], ALU.mult)
                return pool.tensor_tensor(e[:, :, 0, :], e[:, :, 0, :], k[:, :, 0, :], ALU.mult)

            @block.gpsimd
            def _(pool):
                pool.memset(sT, 0.0).then_inc(s_zero, 1)
                for i in range(8):
                    pool.wait_ge(s_e, i + 1)
                    scale_level(pool, i).then_inc(s_z, 1)

            @block.scalar
            def _(act):
                for i in range(8):
                    act.wait_ge(s_d, i + 1)
                    act.activation(Z[i % 3], Z[i % 3], ACT.Exp).then_inc(s_e, 1)
                act.activation(p2[:, :, D:2 * D], p2[:, :, D:2 * D], ACT.Sigmoid).then_inc(s_sg, 1)
                act.activation(p2[:, :, 5 * D:7 * D], p2[:, :, 5 * D:7 * D], ACT.Sigmoid).then_inc(s_sg, 1)
                act.wait_ge(s_ss, 1)
                act.activation(tiny[:, 16:32], tiny[:, 0:16], ACT.Sqrt, bias=eps, scale=1.0 / P).then_inc(s_std, 1)

            @block.vector
            def _(dve):
                step = Steps(dve, s_dv)
                def exponents(i):
                    if i >= 3:
                        dve.wait_ge(s_m, i - 1)
                    c, e = halves(f3, 1 << i), halves(Z[i % 3], 1 << i)
                    s_ = 1 << i
                    ref = c[:, :, 0, s_ - 1:s_].to_broadcast([P, NB // (2 * s_), s_])
                    dve.tensor_tensor(e[:, :, 1, :], c[:, :, 1, :], ref, ALU.subtract)
                    dve.tensor_tensor(e[:, :, 0, :], ref, c[:, :, 0, :], ALU.subtract).then_inc(s_d, 1)

                def take(i, mask):
                    dve.wait_ge(s_m, i + 1)
                    step(dve.copy_predicated(sT, mask.bitcast(U32).unsqueeze(1).to_broadcast([P, 2 * HH, P]),
                                             psf[:, i % 2 * 2048:(i % 2 + 1) * 2048].rearrange("p (u t) -> p u t", t=P)))
                    dve.drain().then_inc(s_p, 1)

                for i in range(3):
                    exponents(i)
                dve.wait_ge(s_zero, 1)
                take(0, ident)
                for i in range(7):
                    take(i + 1, lev[:, i, :])
                    if i + 3 < 8:
                        exponents(i + 3)
                dve.wait_ge(s_m, 9)
                dve.tensor_copy(cross, psf[:, 0:1024].rearrange("p (u t) -> p u t", t=P)).then_inc(s_p, 1)
                dve.wait_ge(s_o, 1)
                o = p2[:, :, 0:D]
                step(dve.tensor_copy(o, psf[:, 2048:4096].rearrange("p (t n) -> p t n", t=TT)))
                sq = at(O_W, TT, D)
                step(dve.tensor_tensor(sq, o, o, ALU.mult))
                dve.tensor_reduce(tiny[:, 0:16], sq.rearrange("p t (h d) -> p (t h) d", d=P), AX, ALU.add).then_inc(s_ss, 1)
                dve.wait_ge(s_std, 1)
                step(dve.reciprocal(tiny[:, 32:48], tiny[:, 16:32]))
                for tt in range(TT):
                    o3 = o[:, tt, :].rearrange("p (h d) -> p h d", d=P)
                    step(dve.tensor_tensor(o3, o3, wide(tiny[:, 32 + 8 * tt:40 + 8 * tt], P), ALU.mult))
                    step(dve.tensor_tensor(o[:, tt, :], o[:, tt, :], hg_gain, ALU.mult))
                    dve.wait_ge(s_sg, 2)
                    step(dve.tensor_tensor(o[:, tt, :], o[:, tt, :], p2[:, tt, D:2 * D], ALU.mult))

            @block.tensor
            def _(pe):
                for i in range(8):
                    if i >= 2:
                        pe.wait_ge(s_p, i - 1)
                    if i:
                        pe.wait_ge(s_z, i)
                    for u in range(2 * HH):
                        hd, tt = divmod(u, TT)
                        tok_ = slice(tt * P, (tt + 1) * P)
                        k = kx[:, hd, tok_] if i == 0 else Z[(i - 1) % 3][:, hd, tok_]
                        q = q3[:, hd, tok_] if i == 0 else k
                        mm = pe.matmul(psf[:, i % 2 * 2048 + u * P:i % 2 * 2048 + (u + 1) * P], k, q, start=True, stop=True)
                    mm.then_inc(s_m, 1)
                pe.wait_ge(s_p, 7)
                pe.wait_ge(s_z, 8)
                for hd in range(HH):
                    mm = pe.matmul(psf[:, hd * P:(hd + 1) * P], Z[7 % 3][:, hd, 0:P], Z[7 % 3][:, hd, P:S], start=True, stop=True)
                mm.then_inc(s_m, 1)
                pe.wait_ge(s_p, 9)
                for tt in range(TT):
                    for hd in range(HH):
                        o = psf[:, 2048 + tt * D + hd * P:2048 + tt * D + (hd + 1) * P]
                        v = [p2[:, j, hd * P:(hd + 1) * P] for j in range(TT)]
                        mm = pe.matmul(o, sT[:, hd * TT + tt, :], v[tt], start=True, stop=tt == 0)
                        if tt:
                            mm = pe.matmul(o, cross[:, hd, :], v[0], start=False, stop=True)
                mm.then_inc(s_o, 1)

        GH = 8
        qkT = at(O_W, 2 * GH, S)[0:SD]
        zT = at(O_W + 16 * S, GH, 384)
        spl = at(O_W + 16 * S + GH * 384, GH, 384)
        assert O_W + 16 * S + 2 * GH * 384 <= WORDS
        (s_tr, s_ev_v, s_ev_a, s_z, s_zc, s_abs, s_exp, s_ln, s_sp, s_r, s_df, s_w, s_wm, s_o, s_dv, s_oc) = (
            sem("stick_" + n) for n in (
                "transposed", "qkT_dve", "qkT_act", "scores", "scores_copied", "abs", "exp", "ln", "softplus", "sums_after",
                "log_weights", "weights", "weights_masked", "out", "group_steps", "out_copied"))

        def stick_group(g):
            with nc.Block() as block:
                @block.tensor
                def _(pe):
                    for b in range(8):
                        pairs = []
                        for u in (2 * b, 2 * b + 1):
                            col = (2 + u // GH) * D + (g * GH + u % GH) * SD
                            pairs += [(ps[0:SD, b, (u % 2) * S + tt * P:(u % 2) * S + (tt + 1) * P],
                                       p2[:, tt, col:col + SD]) for tt in range(TT)]
                        transposes(pe, pairs).then_inc(s_tr, 1)
                    pe.wait_ge(s_ev_v, 4 * g + 4)
                    pe.wait_ge(s_ev_a, 4 * g + 4)
                    for hd in range(GH):
                        q, k = qkT[:, hd, :], qkT[:, GH + hd, :]
                        pe.matmul(ps[:, hd, 0:S], k[:, 0:P], q, start=True, stop=True)
                        mm = pe.matmul(ps[:, hd, S:384], k[:, P:S], q[:, P:S], start=True, stop=True)
                        if hd % 4 == 3:
                            mm.then_inc(s_z, 1)
                    for half in range(2):
                        pe.wait_ge(s_sp, 2 * g + half + 1)
                        for hd in range(4 * half, 4 * half + 4):
                            pe.matmul(ps[:, hd, 0:S], low, spl[:, hd, 0:S], start=True, stop=False)
                            pe.matmul(ps[:, hd, P:S], ones, spl[:, hd, S:384], start=False, stop=True)
                            mm = pe.matmul(ps[:, hd, S:384], low, spl[:, hd, S:384], start=True, stop=True)
                        mm.then_inc(s_r, 1)
                    pe.wait_ge(s_wm, 2 * g + 2)
                    for tt in range(TT):
                        for hd in range(GH):
                            o = ps[:, tt, hd * SD:(hd + 1) * SD]
                            col = 4 * D + (g * GH + hd) * SD
                            for j in range(tt + 1):
                                c = S if j else tt * P
                                mm = pe.matmul(o, zT[:, hd, c:c + P], p2[:, j, col:col + SD], start=j == 0, stop=j == tt)
                    mm.then_inc(s_o, 1)

                @block.vector
                def _(dve):
                    step = Steps(dve, s_dv, g * 4)
                    for b in range(0, 8, 2):
                        dve.wait_ge(s_tr, 8 * g + b + 1)
                        dve.tensor_copy(qkT[:, 2 * b:2 * b + 2, :], ps[0:SD, b, :].rearrange("p (a t) -> p a t", t=S))\
                            .then_inc(s_ev_v, 1)
                    for half in range(2):
                        hs = slice(4 * half, 4 * half + 4)
                        dve.wait_ge(s_z, 2 * g + half + 1)
                        dve.tensor_copy(zT[:, hs, :], ps[:, hs, 0:384]).then_inc(s_zc, 1)
                    dve.wait_ge(s_zc, 2 * g + 2)
                    for half in range(2):
                        hs = slice(4 * half, 4 * half + 4)
                        dve.wait_ge(s_ln, 2 * g + half + 1)
                        step(dve.scalar_tensor_tensor(out=spl[:, hs, :], in0=zT[:, hs, :], scalar=0.0, in1=spl[:, hs, :],
                                                      op0=ALU.max, op1=ALU.add))
                        for c in (0, S):
                            one = dve.tensor_tensor(spl[:, hs, c:c + P], spl[:, hs, c:c + P],
                                                    strict_up.unsqueeze(1).to_broadcast([P, 4, P]), ALU.mult)
                        one.then_inc(s_sp, 1)
                    for half in range(2):
                        hs = slice(4 * half, 4 * half + 4)
                        dve.wait_ge(s_r, 2 * g + half + 1)
                        step(dve.tensor_tensor(zT[:, hs, :], zT[:, hs, :], ps[:, hs, 0:384], ALU.subtract))
                        dve.tensor_scalar(zT[:, hs, :], zT[:, hs, :], 0.0, None, ALU.min).then_inc(s_df, 1)
                    for half in range(2):
                        hs = slice(4 * half, 4 * half + 4)
                        dve.wait_ge(s_w, 2 * g + half + 1)
                        for c in (0, S):
                            one = dve.tensor_tensor(zT[:, hs, c:c + P], zT[:, hs, c:c + P],
                                                    strict_up.unsqueeze(1).to_broadcast([P, 4, P]), ALU.mult)
                        one.then_inc(s_wm, 1)
                    dve.wait_ge(s_o, g + 1)
                    dve.tensor_copy(p2[:, :, 2 * D + g * 512:2 * D + (g + 1) * 512], ps[:, 0:2, :]).then_inc(s_oc, 1)

                @block.scalar
                def _(act):
                    for b in range(1, 8, 2):
                        act.wait_ge(s_tr, 8 * g + b + 1)
                        act.copy(qkT[:, 2 * b:2 * b + 2, :], ps[0:SD, b, :].rearrange("p (a t) -> p a t", t=S))\
                            .then_inc(s_ev_a, 1)
                    for half in range(2):
                        hs = slice(4 * half, 4 * half + 4)
                        act.wait_ge(s_zc, 2 * g + half + 1)
                        act.activation(spl[:, hs, :], zT[:, hs, :], ACT.Abs).then_inc(s_abs, 1)
                        act.wait_ge(s_abs, 2 * g + half + 1)
                        act.activation(spl[:, hs, :], spl[:, hs, :], ACT.Exp, scale=-1.0).then_inc(s_exp, 1)
                        act.wait_ge(s_exp, 2 * g + half + 1)
                        act.activation(spl[:, hs, :], spl[:, hs, :], ACT.Ln, bias=1.0).then_inc(s_ln, 1)
                    for half in range(2):
                        act.wait_ge(s_df, 2 * g + half + 1)
                        act.activation(zT[:, 4 * half:4 * half + 4, :], zT[:, 4 * half:4 * half + 4, :], ACT.Exp)\
                            .then_inc(s_w, 1)

        for g in range(2):
            stick_group(g)

        turn_stage("hg_rows", p2[:, :, 0:D])
        mixed = at(O_W, TT, D)

        def add_hg(dve, step):
            for tt in range(TT):
                step(dve.tensor_tensor(mixed[:, tt, :], product_rows(tt), p2[:, tt, 5 * D:6 * D], ALU.mult))

        rows_stage("w_hg_out", n_hgo, 4, n_sbo[0] + SLOTS, (x_hi, x_lo), add_hg)
        turn_stage("sb_rows", p2[:, :, 2 * D:3 * D])

        def add_sb(dve, step):
            for tt in range(TT):
                step(dve.tensor_tensor(at(O_W + 2048, D), product_rows(tt), p2[:, tt, 6 * D:7 * D], ALU.mult))
                step(dve.tensor_tensor(mixed[:, tt, :], mixed[:, tt, :], at(O_W + 2048, D), ALU.add))

        rows_stage("w_sb_out", n_sbo, 4, n_wo[0] + SLOTS, (x_hi, x_lo), add_sb)
        turn_stage("mixed_rows", mixed)

        def add_wo(dve, step):
            for tt in range(TT):
                step(dve.tensor_tensor(x[:, tt, :], x[:, tt, :], product_rows(tt), ALU.add))

        rows_stage("w_o", n_wo, 4, n_ffi[0] + SLOTS, (x_hi, x_lo), add_wo)

        s_x = sem("norm2_2_gain_loaded")
        with nc.Block() as block:
            @block.sync
            def _(sp):
                sp.dma_start(gain, A["norm2_gain_2"].to_broadcast([P, D])).then_inc(s_x, 16)
        norm_stage("norm2_2", h, x, s_x, 16)

        ff = at(O_F, FT, S)
        ff_hi, ff_lo = (Pieces([atr(O_F + i * FT * S + t * S, min(t + 2, 4), S) for t in (0,) + tuple(range(2, FT, 4))])
                        for i in (1, 2))
        s_ga, s_up, s_prod, s_fh = sem("ff_gate"), sem("ff_up"), sem("ff_hidden"), sem("ff_hidden_hi")
        GA = FT // 4
        with nc.Block() as block:
            @block.sync
            def _(sp):
                st.issue(sp, n_ffo[0] + SLOTS)

            @block.tensor
            def _(pe):
                for c in range(2 * FT // 4):
                    if c >= 2:
                        if c - 2 <= GA:
                            pe.wait_ge(s_ga, c - 1)
                        if c - 2 >= GA:
                            pe.wait_ge(s_prod, c - 1 - GA)
                    product_group(pe, c, n_ffi[1] + KT * c, 0, "f", (x_hi, x_lo))

            @block.scalar
            def _(act):
                def evacuate(c):
                    if c <= GA:
                        n = 4 if c < GA else 2
                        act.activation(ff[:, 4 * c:4 * c + n, :], ps[:, c % 2 * 4:c % 2 * 4 + n, 0:S], ACT.Silu)\
                            .then_inc(s_ga, 1)
                    if c > GA:
                        high(c - 1)

                def high(c):
                    act.wait_ge(s_prod, c - GA + 1)
                    n, skip = (4, 0) if c > GA else (2, 2)
                    t = 4 * c + skip - FT
                    act.copy(ff_hi.piece(t), ff[:, t:t + n, :]).then_inc(s_fh, 1)

                hi_groups(act, n_ffi, 2 * FT // 4, evacuate)
                high(2 * FT // 4 - 1)

            @block.vector
            def _(dve):
                def tiles(c):
                    n, skip = (4, 0) if c > GA else (2, 2)
                    return 4 * c + skip - FT, n, skip

                def evacuate(c):
                    if c < GA:
                        return
                    t, n, skip = tiles(c)
                    dve.wait_ge(s_ga, GA + 1)
                    dve.tensor_tensor(ff[:, t:t + n, :], ff[:, t:t + n, :],
                                      ps[:, c % 2 * 4 + skip:c % 2 * 4 + skip + n, 0:S], ALU.mult).then_inc(s_prod, 1)
                    if c > GA:
                        low_part(c - 1)

                def low_part(c):
                    t, n, _ = tiles(c)
                    dve.wait_ge(s_fh, c - GA + 1)
                    dve.tensor_tensor(ff_lo.piece(t), ff[:, t:t + n, :], ff_hi.piece(t).bitcast(F32),
                                      ALU.subtract)

                lo_groups(dve, n_ffi, 2 * FT // 4, evacuate)
                low_part(2 * FT // 4 - 1)

        s_res, s_out = sem("result"), sem("stored")

        def add_ff(dve, step):
            for tt in range(TT):
                dve.tensor_tensor(x[:, tt, :], x[:, tt, :], product_rows(tt), ALU.add).then_inc(s_res, 1)

        rows_stage("w_ffn_out", n_ffo, 11, n_ffo[0] + 11, (ff_hi, ff_lo), add_ff)
        with nc.Block() as block:
            @block.sync
            def _(sp):
                sp.wait_ge(s_res, TT)
                sp.dma_start(out[0].rearrange("(t p) d -> p t d", p=P), x).then_inc(s_out, 16)
                sp.wait_ge(s_out, 16)


NAMES = ["x", "c", "w_ada", "b_ada", "norm1_gain", "w_in", "attn_q_gain", "attn_k_gain", "attn_rel_bias",
         "attn_out_gain", "dn_conv_w", "dn_a_log", "dn_dt_bias", "dn_out_gain", "w_out", "norm2_gain",
         "peer_w_query", "peer_query_gain", "peer_sub_keys_1", "peer_sub_keys_2", "peer_expert_down",
         "peer_expert_up", "norm1_gain_2", "w_in_2", "lb_logits_2", "hg_out_norm_2", "sb_q_norm_2",
         "sb_k_norm_2", "w_hg_out_2", "w_sb_out_2", "w_o_2", "norm2_gain_2", "w_ffn_in_2", "w_ffn_out_2"]


def kernel(**inputs):
    import numpy as np
    import concourse.bacc as bacc
    from concourse.bass_utils import run_bass_kernel_spmd

    nc = bacc.Bacc("TRN2", target_bir_lowering=False, num_devices=1)
    arrays, A = {}, {}
    for name in NAMES:
        a = np.ascontiguousarray(inputs[name])
        arrays[f"in_{name}"] = a
        A[name] = nc.dram_tensor(f"in_{name}", a.shape, mybir.dt.from_np(a.dtype), kind="ExternalInput").ap()
    out = nc.dram_tensor("out", (1, S, D), F32, kind="ExternalOutput").ap()
    build(nc, A, out)
    r = run_bass_kernel_spmd(nc, [arrays], core_ids=[0])
    return r.results[0]["out"]
```

```python
from contextlib import ExitStack

import concourse.bass as bass
from concourse import mybir

F32 = mybir.dt.float32
F32R = mybir.dt.float32r
U32 = mybir.dt.uint32
ALU = mybir.AluOpType
ACT = mybir.ActivationFunctionType
AX = mybir.AxisListType.X

P = 128
D = 1024
KT = D // P
S = 256
TT = S // P
EPS = 1e-6
NEG = -1e30
SLOTS = 4
SLOT = 2048
UNIT = 512
UPC = SLOT // UNIT
BUFFERS = 4

O_CONST = 0
O_GATE2 = 1536
O_X_HI = O_GATE2 + D
O_X_LO = O_X_HI + KT * S
O_W_HI = O_X_LO + KT * S
O_W_LO = O_W_HI + BUFFERS * UNIT
O_RING = O_W_LO + BUFFERS * UNIT
O_R = O_RING + SLOTS * SLOT
O_PICKS = O_R + P * S
WORDS = O_PICKS + 3 * S + 640


class Stream:

    def __init__(self, ring, landed, lo_ready, turned):
        self.ring, self.landed, self.lo_ready, self.turned = ring, landed, lo_ready, turned
        self.segments, self.count, self.issued, self.units = [], 0, 0, 0

    def add(self, count, source, cols, turned=False):
        unit0 = 0 if turned else self.units
        self.segments.append((self.count, count, source, cols, self.turned if turned else self.lo_ready,
                              2 if turned else UPC, unit0))
        self.count += count
        if not turned:
            self.units += UPC * count
        return self.count - count, unit0

    def words(self, n, first, count):
        o = (n % SLOTS) * SLOT + first
        return self.ring[:, o:o + count]

    def landed_value(self, n):
        return 16 * (n // SLOTS + 1)

    def load(self, sp, n, rounds, j, seg):
        start, _, source, cols, _, _, _ = seg
        if n >= SLOTS:
            for s0, count, _, _, used, per, unit0 in self.segments:
                if s0 <= n - SLOTS < s0 + count:
                    sp.wait_ge(used, rounds * (per * SLOTS) + (unit0 + per * (n - SLOTS - s0 + 1)))
        dst = self.ring[:, (n % SLOTS) * SLOT:(n % SLOTS + 1) * SLOT].rearrange("p (k n) -> p k n", n=cols)
        sp.dma_start(dst, source(rounds, j)).then_inc(self.landed[n % SLOTS], 16)

    def issue(self, sp, upto):
        for seg in self.segments:
            start, count = seg[0], seg[1]
            lo, hi = max(self.issued, start), min(upto, start + count)
            if lo >= hi:
                continue
            n = lo
            while n < hi and (n < start + SLOTS or (n - start) % SLOTS):
                self.load(sp, n, 0, n - start, seg)
                n += 1
            rounds = (hi - n) // SLOTS
            if rounds > 1:
                with sp.Fori(0, rounds) as r:
                    for j in range(SLOTS):
                        self.load(sp, n + j, r, n + j - start, seg)
                n += SLOTS * rounds
            for m in range(n, hi):
                self.load(sp, m, 0, m - start, seg)
            self.issued = hi


class Steps:

    def __init__(self, eng, sem, done=0):
        self.eng, self.sem, self.done = eng, sem, done

    def __call__(self, ins):
        self.done += 1
        ins.then_inc(self.sem, 1)
        self.eng.wait_ge(self.sem, self.done)


class Pieces:

    def __init__(self, pieces):
        self.pieces = pieces

    def piece(self, t):
        return self.pieces[(t + 2) // 4]

    def __getitem__(self, key):
        _, k, tokens = key
        return self.piece(k)[:, k if k < 2 else (k + 2) % 4, tokens]


def build(nc, A, out):
    with ExitStack() as ctx:
        mem = ctx.enter_context(nc.sbuf_tensor("mem", [P, WORDS], F32))
        mem_base = nc.sbuf_base - 4 * WORDS
        ps = ctx.enter_context(nc.psum_tensor("ps", [P, 8, 512], F32))
        psf = ps[:, :, :].rearrange("p b n -> p (b n)")
        ctx.enter_context(nc.allow_non_contiguous_dma(reason="short rows of small parameters"))
        x_spill = nc.dram_tensor("x_spill", (P, TT * D), F32, kind="Internal").ap()
        rel_ext = nc.dram_tensor("rel_ext", (8, 384), F32, kind="Internal").ap()

        stage_sems = []

        def lasting_sem(name):
            return ctx.enter_context(nc.semaphore(name))

        def sem(name):
            stage_sems.append(nc.alloc_semaphore(name))
            return stage_sems[-1]

        def renew_semaphores():
            with nc.Block() as block:
                @block.gpsimd
                def _(pool):
                    nc.clear_and_free_semaphores(stage_sems)
            stage_sems.clear()

        def at(off, *shape):
            n = 1
            for s in shape:
                n *= s
            v = mem[:, off:off + n]
            if len(shape) == 2:
                v = v.rearrange("p (a b) -> p a b", b=shape[1])
            elif len(shape) == 3:
                v = v.rearrange("p (a b c) -> p a b c", b=shape[1], c=shape[2])
            return v

        def wide(ap, n):
            return ap.unsqueeze(2).to_broadcast([ap.shape[0], ap.shape[1], n])

        ident = at(O_CONST, P)
        ones = at(O_CONST + 128, P)
        anti = at(O_CONST + 256, P)
        upper = at(O_CONST + 384, P)
        strict_low = at(O_CONST + 512, P)
        strict_up = at(O_CONST + 640, P)
        low = at(O_CONST + 768, P)
        iota = at(O_CONST + 896, P)
        zeros = at(O_CONST + 1024, P)
        eps = at(O_CONST + 1152, 1)
        tiny = at(O_CONST + 1160, 160)
        gate2 = at(O_GATE2, D)

        views = []

        def atr(off, *shape):
            n = shape[0] * (shape[1] if len(shape) > 1 else 1)
            for o, size, tensor in views:
                if o <= off and off + n <= o + size:
                    break
            else:
                o, tensor = off, nc.alloc_sbuf_tensor_at(f"parts{len(views)}", [P, n], F32R, offset=mem_base + 4 * off)
                views.append((off, n, tensor))
            v = tensor[:, off - o:off - o + n]
            return v.rearrange("p (a b) -> p a b", b=shape[1]) if len(shape) == 2 else v

        x_hi, x_lo = atr(O_X_HI, KT, S), atr(O_X_LO, KT, S)
        w_hi, w_lo = ([atr(o, BUFFERS, UNIT)[:, i, :] for i in range(BUFFERS)] for o in (O_W_HI, O_W_LO))

        landed = [lasting_sem(f"landed{i}") for i in range(SLOTS)]
        hi_ready, lo_ready = lasting_sem("hi_ready"), lasting_sem("lo_ready")
        unit_used, turned = lasting_sem("unit_used"), lasting_sem("down_turned")
        st = Stream(at(O_RING, SLOTS * SLOT), landed, lo_ready, turned)

        def column_chunks(w, first):
            v = w.rearrange("(k p) n -> p k n", p=P)
            return lambda r, j: v[:, j % 2 * 4:j % 2 * 4 + 4, bass.ds(r * 1024 + (first + j // 2 * 512), 512)]

        def row_chunks(w):
            v = w.rearrange("(k p) n -> p k n", p=P)
            return lambda r, j: v[:, bass.ds(r * 8 + j * 2, 2), :]

        def expert_chunks(w):
            v = w.rearrange("(a b) d -> a b d", a=P)
            return lambda r, j: v[:, bass.ds(r * 8 + j * 2, 2), :]

        w_in, w_in2 = A["w_in"][0], A["w_in_2"][0]
        FF = A["w_ffn_out_2"].shape[1]
        FT = FF // P
        n_ada = st.add(24, column_chunks(A["w_ada"][0], 0), 512)
        n_in = st.add(14, column_chunks(w_in, 0), 512)
        n_wout = st.add(4, row_chunks(A["w_out"][0]), D)
        n_query = st.add(8, column_chunks(A["peer_w_query"][0], 0), 512)
        n_down = st.add(64, expert_chunks(A["peer_expert_down"][0]), D, turned=True)
        n_up = st.add(64, expert_chunks(A["peer_expert_up"][0]), D)
        n_in2a = st.add(8, column_chunks(w_in2, 0), 512)
        n_in2b = st.add(28, column_chunks(w_in2, 4 * 512), 512)
        n_hgo = st.add(4, row_chunks(A["w_hg_out_2"][0]), D)
        n_sbo = st.add(4, row_chunks(A["w_sb_out_2"][0]), D)
        n_wo = st.add(4, row_chunks(A["w_o_2"][0]), D)
        n_ffi = st.add(22, column_chunks(A["w_ffn_in_2"][0], 0), 512)
        n_ffo = st.add(11, row_chunks(A["w_ffn_out_2"][0]), D)

        def split_hi(act, n, g, u, rounds):
            if u == 0:
                act.wait_ge(landed[n % SLOTS], rounds * 16 + st.landed_value(n))
            act.wait_ge(unit_used, rounds * (UPC * SLOTS) + (g + 1))
            act.copy(w_hi[g % BUFFERS], st.words(n, u * UNIT, UNIT)).then_inc(hi_ready, 1)

        def split_lo(dve, n, g, u, rounds):
            dve.wait_ge(hi_ready, rounds * (UPC * SLOTS) + (g + 1))
            dve.tensor_tensor(w_lo[g % BUFFERS], st.words(n, u * UNIT, UNIT), w_hi[g % BUFFERS].bitcast(F32),
                              ALU.subtract).then_inc(lo_ready, 1)

        def await_unit(pe, g, rounds):
            pe.wait_ge(lo_ready, rounds * (UPC * SLOTS) + (g + 1))

        def three(pe, o, lhs, rhs, start, stop, **kw):
            for i, (a, b) in enumerate(((0, 0), (0, 1), (1, 0))):
                mm = pe.matmul(o, lhs[a], rhs[b], start=start and i == 0, stop=stop and i == 2,
                               skip_group_check=True, **kw)
            return mm

        def product_group(pe, c, g, rounds, kind, left):
            for k in range(KT):
                await_unit(pe, g + k, rounds)
                parts = [w[(g + k) % BUFFERS] for w in (w_hi, w_lo)]
                if kind == "t":
                    for tt in range(TT):
                        ts = slice(tt * P, (tt + 1) * P)
                        mm = three(pe, ps[:, c % 2 * 4 + tt, :], [a[:, k, ts] for a in left], parts,
                                   k == 0, k == KT - 1)
                else:
                    for m in range(4):
                        ms = slice(m * P, (m + 1) * P)
                        mm = three(pe, ps[:, c % 2 * 4 + m, 0:S], [w[:, ms] for w in parts],
                                   [a[:, k, :] for a in left], k == 0, k == KT - 1)
                mm.then_inc(unit_used, 1)

        def split_groups(eng, split, at_unit, seg, groups, evacuate, beside=None):
            n0, g0 = seg
            for c in range(groups):
                for u in range(KT):
                    split(eng, n0 + 2 * c + u // UPC, g0 + KT * c + u, u % UPC, 0)
                    if u == at_unit and c:
                        eng.wait_ge(unit_used, used_value(g0 + KT * c - 1))
                        evacuate(c - 1)
                    if beside:
                        beside(c, u)
            eng.wait_ge(unit_used, used_value(g0 + KT * groups - 1))
            evacuate(groups - 1)

        def hi_groups(act, seg, groups, evacuate):
            split_groups(act, split_hi, 4, seg, groups, evacuate)

        def lo_groups(dve, seg, groups, evacuate):
            split_groups(dve, split_lo, 3, seg, groups, evacuate)

        def used_value(g):
            return g + 1 + BUFFERS

        def transposes(pe, pairs):
            for o, i in pairs:
                last = pe.transpose(o, i, ident[0:i.shape[0], 0:i.shape[0]])
            return last

        def turn_rows(pe, rows, s_t, b0=0):
            for q in range(4):
                transposes(pe, [(psf[:, b0 * 512 + (k * TT + tt) * P:b0 * 512 + (k * TT + tt + 1) * P],
                                 rows[:, tt, k * P:(k + 1) * P])
                                for k in (2 * q, 2 * q + 1) for tt in range(TT)]).then_inc(s_t, 1)

        def turned_hi(act, s_t, s_hi, b0=0, o_hi=O_X_HI):
            for q in range(4):
                act.wait_ge(s_t, b0 + q + 1)
                act.copy(atr(o_hi, KT * S)[:, q * 512:(q + 1) * 512], ps[:, b0 + q, :]).then_inc(s_hi, 1)

        def turned_lo(dve, s_hi, s_lo, b0=0, o_hi=O_X_HI, o_lo=O_X_LO):
            for q in range(4):
                dve.wait_ge(s_hi, b0 + q + 1)
                hi, lo = (atr(o, KT * S)[:, q * 512:(q + 1) * 512] for o in (o_hi, o_lo))
                dve.tensor_tensor(lo, ps[:, b0 + q, :], hi.bitcast(F32), ALU.subtract).then_inc(s_lo, 1)

        x = at(O_R, TT, D)
        O_MODS = O_R + TT * D
        mods = at(O_MODS, 6, D)
        shift1, scale1, gate1, shift2, scale2 = (mods[:, i, :] for i in range(5))
        O_S = O_MODS + 6 * D
        gain = at(O_S, D)
        h = at(O_S + D, TT, D)
        O_P1 = O_S + 3 * D
        N_P1 = 3 * 512 + 512
        p1 = at(O_P1, TT, N_P1)
        O_BA = O_P1 + TT * N_P1
        ba = at(O_BA, TT, 8)
        w_ba = at(O_BA + 16, KT, 8)
        O_CV = O_BA + 96
        LEAD = 3
        conv_in = at(O_CV, 12, S + LEAD)
        O_A = O_CV + 12 * (S + LEAD) + 4

        conv = at(O_S, 12, S)
        O_B = O_A + TT * D
        taps = at(O_B, 48)
        taps_rows = mem[0:48, O_B + 48:O_B + 48 + P]

        c_col = at(O_P1, KT)
        c_hi, c_lo = atr(O_X_HI, KT, P), atr(O_X_LO, KT, P)
        b_ada = mem[0:1, O_A:O_A + 6 * D]

        s_c, s_x, s_csil, s_crow, s_clo = sem("c_loaded"), sem("x_loaded"), sem("c_silu"), sem("c_hi"), sem("c_lo")
        s_ada, s_ada_out, s_const, s_pool = sem("ada_done"), sem("ada_bank_free"), lasting_sem("constants"), sem("pool_steps")
        with nc.Block() as block:
            @block.sync
            def _(sp):
                sp.dma_start(c_col, A["c"][0].rearrange("(k p) -> p k", p=P)).then_inc(s_c, 16)
                sp.dma_start(b_ada, A["b_ada"]).then_inc(s_c, 16)
                sp.dma_start(x, A["x"][0].rearrange("(t p) d -> p t d", p=P)).then_inc(s_x, 16)
                sp.dma_start(w_ba, w_in.rearrange("(k p) n -> p k n", p=P)[:, :, 3584:3592]).then_inc(s_x, 16)
                sp.dma_start(gain, A["norm1_gain"].to_broadcast([P, D])).then_inc(s_x, 16)
                st.issue(sp, n_in[0] + SLOTS)

            @block.gpsimd
            def _(pool):
                step = Steps(pool, s_pool)
                for m, v in ((ident, 0.0), (anti, 0.0), (ones, 1.0), (upper, 1.0), (strict_low, 1.0),
                             (strict_up, 1.0), (low, 1.0), (zeros, 0.0), (eps, EPS)):
                    step(pool.memset(m, v))
                for m, op, fill, base, pattern, mult in (
                        (ident, ALU.not_equal, 1.0, 0, -1, 1), (anti, ALU.not_equal, 1.0, -(P - 1), 1, 1),
                        (upper, ALU.is_ge, 0.0, 0, 1, -1), (strict_low, ALU.is_gt, 0.0, 0, -1, 1),
                        (strict_up, ALU.is_gt, 0.0, 0, 1, -1), (low, ALU.is_ge, 0.0, 0, -1, 1)):
                    step(pool.affine_select(out=m, in_=m, compare_op=op, fill=fill, base=base,
                                            pattern=[[pattern, P]], channel_multiplier=mult))
                pool.iota(iota, pattern=[[1, P]], base=0, channel_multiplier=0,
                          allow_small_or_imprecise_dtypes=True).then_inc(s_const, 1)

            n, g = n_ada

            @block.scalar
            def _(act):
                act.wait_ge(s_c, 32)
                act.activation(c_col, c_col, ACT.Silu).then_inc(s_csil, 1)
                act.wait_ge(s_csil, 1)
                act.copy(c_hi, wide(c_col, P)).then_inc(s_crow, 1)
                with act.Fori(0, 6) as r:
                    for u in range(16):
                        split_hi(act, n + u // UPC, g + u, u % UPC, r)

            @block.vector
            def _(dve):
                dve.wait_ge(s_crow, 1)
                dve.tensor_tensor(c_lo, wide(c_col, P), c_hi.bitcast(F32), ALU.subtract).then_inc(s_clo, 1)

                def out_row(c, rounds):
                    dve.wait_ge(s_ada, rounds * 2 + (c + 1))
                    dve.wait_ge(s_const, 1)
                    dve.tensor_copy(mem[:, bass.ds(rounds * 1024 + (O_MODS + 512 * c), 512)],
                                    ps[:, c % 2, :]).then_inc(s_ada_out, 1)
                for u in range(16):
                    split_lo(dve, n + u // UPC, g + u, u % UPC, 0)
                    if u == 11:
                        out_row(0, 0)
                with dve.Fori(0, 5) as r:
                    for u in range(16, 32):
                        split_lo(dve, n + u // UPC, g + u, u % UPC, r)
                        if u % 8 == 3:
                            out_row(u // 8 - 1, r)
                out_row(11, 0)

            @block.tensor
            def _(pe):
                pe.sem_inc(unit_used, BUFFERS)
                pe.sem_inc(s_ada_out, 2)
                pe.wait_ge(s_clo, 1)
                pe.wait_ge(s_const, 1)
                with pe.Fori(0, 6) as r:
                    for c in range(2):
                        pe.wait_ge(s_ada_out, r * 2 + (c + 1))
                        for k in range(KT):
                            await_unit(pe, g + KT * c + k, r)
                            three(pe, ps[:, c, :], [c_hi[:, k, :], c_lo[:, k, :]],
                                  [w[k % BUFFERS] for w in (w_hi, w_lo)], k == 0, False).then_inc(unit_used, 1)
                        pe.matmul(ps[:, c, :], ones[0:1, :],
                                  mem[0:1, bass.ds(r * 1024 + (O_A + 512 * c), 512)],
                                  start=False, stop=True, skip_group_check=True).then_inc(s_ada, 1)

        def norm_roots(act, rows, src, s_sq, s_src=None):
            for tt in range(TT):
                if s_src is not None:
                    act.wait_ge(s_src, tt + 1)
                act.activation(rows[:, tt, :], src[:, tt, :], ACT.Square, accum_out=tiny[:, tt:tt + 1]).then_inc(s_sq, 1)
            act.wait_ge(s_sq, TT)
            return act.activation(tiny[:, 2:4], tiny[:, 0:2], ACT.Sqrt, bias=eps, scale=1.0 / D)

        def norm_stage(tag, rows, src, s_gain, gain_value, shift=None, scale=None, beside=None, weight=None, roots=True):
            s_sq, s_std, s_h, s_t, s_hi, s_lo = (sem(f"{tag}_{n}") for n in (
                "squares", "std", "rows", "transposed", "hi", "lo"))
            s_v = sem(f"{tag}_steps")
            with nc.Block() as block:
                if beside:
                    @block.sync
                    def _(sp):
                        beside(sp)

                @block.scalar
                def _(act):
                    if roots:
                        norm_roots(act, rows, src, s_sq).then_inc(s_std, 1)
                    turned_hi(act, s_t, s_hi)

                @block.vector
                def _(dve):
                    step = Steps(dve, s_v)
                    if roots:
                        dve.wait_ge(s_std, 1)
                    step(dve.reciprocal(tiny[:, 4:6], tiny[:, 2:4]))
                    dve.wait_ge(s_gain, gain_value)
                    for tt in range(TT):
                        one = dve.scalar_tensor_tensor(out=rows[:, tt, :], in0=src[:, tt, :],
                                                       scalar=tiny[:, 4 + tt:5 + tt],
                                                       in1=gain if weight is None else weight,
                                                       op0=ALU.mult, op1=ALU.mult)
                        if scale is not None:
                            step(one)
                            step(dve.scalar_tensor_tensor(out=rows[:, tt, :], in0=scale, scalar=1.0,
                                                          in1=rows[:, tt, :], op0=ALU.add, op1=ALU.mult))
                        elif shift is not None:
                            step(one)
                        if shift is not None:
                            one = dve.tensor_tensor(rows[:, tt, :], rows[:, tt, :], shift, ALU.add)
                        one.then_inc(s_h, 1)
                    turned_lo(dve, s_hi, s_lo)

                @block.tensor
                def _(pe):
                    pe.wait_ge(s_h, TT)
                    turn_rows(pe, rows, s_t)

        norm_stage("norm1", h, x, s_x, 48, shift1, scale1)

        HA, DA = 8, 64
        mix = at(O_A, TT, D)
        qkT = at(O_B, 2 * HA, S)[0:DA]
        prob = at(O_B + 4096, HA, 384)
        probT = at(O_B + 4096 + 3072, 3 * HA, P)
        O_BT = O_B + 4096 + 6144
        bias_r = at(O_BT, HA, 2 * P)
        qk_gain = at(O_BT + 2048, 2, DA)
        att_gain = at(O_BT + 2048 + 128, 512)
        ext = mem[0:HA, O_B + 512:O_B + 512 + 384]
        squares = at(O_B + 4096, TT, D)
        NREL = A["attn_rel_bias"].shape[2]
        (s_par, s_ext, s_ext_out, s_bias, s_sq, s_sum, s_std, s_inv, s_pl) = (sem("att_" + n) for n in (
            "params", "rel_extended", "rel_stored", "bias_loaded", "qk_squares", "qk_sums", "qk_std", "qk_inverse_std",
            "pool_steps"))
        s_ba, s_bank_v, s_bank_a = sem("proj1_ba_done"), sem("proj1_bank_out_dve"), sem("proj1_bank_out_act")
        s_z3, s_bah, s_taps, s_tap, s_tapo, s_conv = (sem(n) for n in (
            "conv_lead_zero", "ba_hi", "taps_loaded", "taps_transposed", "taps_out", "conv_steps"))
        ba_hi, ba_lo = (atr(O_A + 64 * i, KT * 8).rearrange("p (k n) -> p k n", n=8) for i in range(2))

        with nc.Block() as block:
            n0, g0 = n_in

            @block.sync
            def _(sp):
                sp.dma_start(ext[:, 0:NREL], A["attn_rel_bias"][0]).then_inc(s_par, 16)
                sp.dma_start(qk_gain[:, 0, :], A["attn_q_gain"].to_broadcast([P, DA])).then_inc(s_par, 16)
                sp.dma_start(qk_gain[:, 1, :], A["attn_k_gain"].to_broadcast([P, DA])).then_inc(s_par, 16)
                sp.dma_start(att_gain, A["attn_out_gain"].to_broadcast([P, 512])).then_inc(s_par, 16)
                sp.dma_start(taps_rows, A["dn_conv_w"][0].rearrange("i (t c) -> (i t) c", c=P)).then_inc(s_taps, 16)
                st.issue(sp, n_wout[0] + SLOTS)

            @block.gpsimd
            def _(pool):
                step = Steps(pool, s_pl)
                pool.memset(conv_in[:, :, 0:LEAD], 0.0).then_inc(s_z3, 1)
                pool.wait_ge(s_ext, 1)
                pool.dma_start(rel_ext, ext).then_inc(s_ext_out, 16)
                pool.wait_ge(s_ext_out, 16)
                for blk in range(2):
                    src = bass.AP(rel_ext.tensor, 1 + P * blk, [[1, P], [384, HA], [1, P]])
                    pool.dma_start(bias_r[:, :, blk * P:(blk + 1) * P], src).then_inc(s_bias, 16)
                pool.wait_ge(s_bank_v, 2)
                pool.wait_ge(s_bank_a, 2)
                for tt in range(TT):
                    pool.tensor_tensor(squares[:, tt, :], p1[:, tt, 0:D], p1[:, tt, 0:D], ALU.mult).then_inc(s_sq, 1)
                pool.wait_ge(s_inv, 1)
                pool.wait_ge(s_par, 64)
                for tt in range(TT):
                    v = p1[:, tt, 0:D].rearrange("p (h d) -> p h d", d=DA)
                    step(pool.tensor_tensor(v, v, wide(tiny[:, 64 + 16 * tt:80 + 16 * tt], DA), ALU.mult))
                    for q in range(2):
                        w = v[:, q * HA:(q + 1) * HA, :]
                        pool.tensor_tensor(w, w, qk_gain[:, q:q + 1, :].to_broadcast([P, HA, DA]), ALU.mult)
                pool.wait_ge(s_bias, 32)
                pool.memset(bias_r[0:64, :, 0:64], NEG)

            @block.tensor
            def _(pe):
                for c in range(7):
                    if c == 1:
                        pe.wait_ge(s_taps, 16)
                        transposes(pe, [(ps[:, 4, 0:48], taps_rows)]).then_inc(s_tap, 1)
                        pe.wait_ge(s_tapo, 1)
                    if c >= 2:
                        pe.wait_ge(s_bank_v, c - 1)
                        pe.wait_ge(s_bank_a, c - 1)
                    product_group(pe, c, g0 + KT * c, 0, "f" if 3 <= c < 6 else "t", (x_hi, x_lo))
                for tt in range(TT):
                    for k in range(KT):
                        ts = slice(tt * P, (tt + 1) * P)
                        mm = three(pe, ps[:, 7, tt * 8:tt * 8 + 8], [x_hi[:, k, ts], x_lo[:, k, ts]],
                                   [ba_hi[:, k, :], ba_lo[:, k, :]], k == 0, k == KT - 1)
                mm.then_inc(s_ba, 1)

            def out_of(b, c):
                if 3 <= c < 6:
                    t = (c - 3) * 4 + b * 2
                    return conv_in[:, t:t + 2, LEAD:LEAD + S], ps[:, c % 2 * 4 + 2 * b:c % 2 * 4 + 2 * b + 2, 0:S]
                col = 512 * (c if c < 3 else 3)
                return p1[:, b, col:col + 512], ps[:, c % 2 * 4 + b, :]

            @block.vector
            def _(dve):
                dve.wait_ge(s_bah, 1)
                dve.tensor_tensor(ba_lo, w_ba, ba_hi.bitcast(F32), ALU.subtract)
                step = Steps(dve, s_conv)

                def beside(c, u):
                    if c == 0 and u == 5:
                        dve.wait_ge(s_par, 64)
                        dve.tensor_scalar(ext[:, NREL:384], ones[0:HA, 0:384 - NREL], ext[:, NREL - 1:NREL], None,
                                          ALU.mult).then_inc(s_ext, 1)
                    if c == 3 and u in (1, 2):
                        tt = u - 1
                        dve.wait_ge(s_sq, tt + 1)
                        dve.tensor_reduce(tiny[:, 16 * tt:16 * tt + 16], squares[:, tt, :].rearrange(
                            "p (h d) -> p h d", d=DA), AX, ALU.add).then_inc(s_sum, 1)
                    if c == 3 and u == 7:
                        dve.wait_ge(s_std, 1)
                        step(dve.reciprocal(tiny[:, 64:96], tiny[:, 32:64]))
                        q_inv = tiny[:, 64:96].rearrange("p (t h) -> p t h", t=TT)[:, :, 0:HA]
                        dve.tensor_scalar(q_inv, q_inv, DA ** -0.5, None, ALU.mult).then_inc(s_inv, 1)
                    if c == 0 and u == 7:
                        dve.wait_ge(s_tap, 1)
                        dve.tensor_copy(taps, ps[:, 4, 0:48]).then_inc(s_tapo, 1)
                    if c < 4 or u < 4:
                        return
                    i, t0 = u - 4, 4 * (c - 4)
                    if i == 0:
                        dve.wait_ge(s_z3, 1)
                        dve.wait_ge(s_tapo, 1)
                        dve.wait_ge(s_bank_a, c)
                        dve.wait_ge(s_bank_v, c)
                    for t in range(t0, t0 + 4):
                        src, w = conv_in[:, t, i:i + S], taps[:, i * 12 + t:i * 12 + t + 1]
                        if i == 0:
                            one = dve.tensor_scalar(conv[:, t, :], src, w, None, ALU.mult)
                        else:
                            one = dve.scalar_tensor_tensor(out=conv[:, t, :], in0=src, scalar=w, in1=conv[:, t, :],
                                                           op0=ALU.mult, op1=ALU.add)
                    step(one)

                split_groups(dve, split_lo, 3, n_in, 7, lambda c: dve.tensor_copy(*out_of(0, c)).then_inc(s_bank_v, 1),
                             beside)
                dve.wait_ge(s_ba, 1)
                dve.tensor_copy(ba, ps[:, 7, 0:16].rearrange("p (t n) -> p t n", n=8)).then_inc(s_bank_v, 1)

            @block.scalar
            def _(act):
                act.copy(ba_hi, w_ba).then_inc(s_bah, 1)

                def root(c, u):
                    if c == 3 and u == 4:
                        act.wait_ge(s_sum, 2)
                        act.activation(tiny[:, 32:64], tiny[:, 0:32], ACT.Sqrt, bias=eps, scale=1.0 / DA).then_inc(s_std, 1)

                split_groups(act, split_hi, 4, n_in, 7, lambda c: act.copy(*out_of(1, c)).then_inc(s_bank_a, 1), root)

        HD = 4
        U = TT * HD
        dn_norm = tiny[:, 128:128 + 2 * U]
        O_H = O_MODS
        zsil = p1[:, :, 3 * 512:4 * 512]
        dn_par = at(O_X_LO + 1024, 16)
        dn_gain = at(O_X_LO + 1040, P)
        s_par_dn, s_silu, s_sq, s_ssum = (sem("dn_" + n) for n in ("params", "silu", "squares", "norms"))
        s_tr, s_ev_v, s_ev_a, s_sc, s_diff, s_exp, s_pt, s_ptv, s_pta, s_o, s_on, s_osq, s_ostd, s_dv = (
            sem("att_" + n) for n in (
                "qk_transposed", "qkT_dve", "qkT_act", "scores", "shifted", "exp",
                "probs_transposed", "probT_dve", "probT_act", "heads", "out_rows", "out_squares", "out_std", "steps"))
        with nc.Block() as block:
            @block.sync
            def _(sp):
                sp.dma_start(dn_par[:, 0:4], A["dn_a_log"].to_broadcast([P, 4])).then_inc(s_par_dn, 16)
                sp.dma_start(dn_par[:, 4:8], A["dn_dt_bias"].to_broadcast([P, 4])).then_inc(s_par_dn, 16)
                sp.dma_start(dn_gain, A["dn_out_gain"].to_broadcast([P, P])).then_inc(s_par_dn, 16)
            @block.vector
            def _(dve):
                step = Steps(dve, s_dv)
                for b in range(0, 8, 2):
                    dve.wait_ge(s_tr, b + 1)
                    dve.tensor_copy(qkT[:, 2 * b:2 * b + 2, :], ps[0:DA, b, :].rearrange("p (a t) -> p a t", t=S))\
                        .then_inc(s_ev_v, 1)
                for half in range(2):
                    hs = slice(half * 4, half * 4 + 4)
                    dve.wait_ge(s_sc, half * 4 + 4)
                    for i, (a, b) in enumerate(((0, P), (P, 384))):
                        m = tiny[:, 96 + i * 8 + half * 4:100 + i * 8 + half * 4]
                        step(dve.tensor_reduce(m, ps[:, hs, a:b], AX, ALU.max))
                        ins = dve.tensor_tensor(prob[:, hs, a:b], ps[:, hs, a:b], wide(m, b - a), ALU.subtract)
                    ins.then_inc(s_diff, 1)
                for half in range(2):
                    hs = slice(half * 4, half * 4 + 4)
                    dve.wait_ge(s_exp, half + 1)
                    step(dve.tensor_reduce(tiny[:, 112 + half * 4:116 + half * 4], prob[:, hs, 0:P], AX, ALU.add))
                    step(dve.tensor_reduce(tiny[:, 120 + half * 4:124 + half * 4], prob[:, hs, P:384], AX, ALU.add))
                step(dve.reciprocal(tiny[:, 112:128], tiny[:, 112:128]))
                for b in range(0, 6, 2):
                    dve.wait_ge(s_pt, b + 1)
                    dve.tensor_copy(probT[:, 4 * b:4 * b + 4, :], ps[:, b, :].rearrange("p (a t) -> p a t", t=P))\
                        .then_inc(s_ptv, 1)
                dve.wait_ge(s_o, 1)
                for tt in range(TT):
                    dve.tensor_tensor(mix[:, tt, 0:512].rearrange("p (h d) -> p h d", d=DA),
                                      ps[:, 6 + tt, :].rearrange("p (h d) -> p h d", d=DA),
                                      wide(tiny[:, 112 + 8 * tt:120 + 8 * tt], DA), ALU.mult).then_inc(s_on, 1)
                dve.wait_ge(s_ostd, 1)
                step(dve.reciprocal(tiny[:, 4:6], tiny[:, 2:4]))
                for tt in range(TT):
                    step(dve.scalar_tensor_tensor(out=mix[:, tt, 0:512], in0=mix[:, tt, 0:512],
                                                  scalar=tiny[:, 4 + tt:5 + tt], in1=att_gain,
                                                  op0=ALU.mult, op1=ALU.mult))

            @block.scalar
            def _(act):
                act.activation(conv, conv, ACT.Silu).then_inc(s_silu, 1)
                for b in range(1, 8, 2):
                    act.wait_ge(s_tr, b + 1)
                    act.copy(qkT[:, 2 * b:2 * b + 2, :], ps[0:DA, b, :].rearrange("p (a t) -> p a t", t=S))\
                        .then_inc(s_ev_a, 1)
                act.wait_ge(s_silu, 1)
                act.activation(zsil, zsil, ACT.Silu)
                act.activation(at(O_H, 8 * S), conv[:, 0:8, :].rearrange("p a t -> p (a t)"), ACT.Square).then_inc(s_sq, 1)
                for half in range(2):
                    act.wait_ge(s_diff, half + 1)
                    act.activation(prob[:, half * 4:half * 4 + 4, :], prob[:, half * 4:half * 4 + 4, :], ACT.Exp)\
                        .then_inc(s_exp, 1)
                for b in range(1, 6, 2):
                    act.wait_ge(s_pt, b + 1)
                    act.copy(probT[:, 4 * b:4 * b + 4, :], ps[:, b, :].rearrange("p (a t) -> p a t", t=P))\
                        .then_inc(s_pta, 1)
                act.wait_ge(s_on, 2)
                act.wait_ge(s_pt, 6)
                for tt in range(TT):
                    act.activation(prob[:, 0:4, 0:P], mix[:, tt, 0:512].rearrange("p (a t) -> p a t", t=P), ACT.Square,
                                   accum_out=tiny[:, tt:tt + 1]).then_inc(s_osq, 1)
                    act.wait_ge(s_osq, tt + 1)
                act.activation(tiny[:, 2:4], tiny[:, 0:2], ACT.Sqrt, bias=eps, scale=1.0 / 512).then_inc(s_ostd, 1)
                act.wait_ge(s_ssum, 1)
                act.activation(dn_norm, ps[:, 0, 0:2 * U], ACT.Sqrt, bias=eps)

            @block.tensor
            def _(pe):
                for b in range(8):
                    transposes(pe, [(ps[0:DA, b, (u % 2) * S + tt * P:(u % 2) * S + (tt + 1) * P],
                                     p1[:, tt, u * DA:(u + 1) * DA])
                                    for u in (2 * b, 2 * b + 1) for tt in range(TT)]).then_inc(s_tr, 1)
                pe.wait_ge(s_ev_v, 4)
                pe.wait_ge(s_ev_a, 4)
                for hd in range(HA):
                    q, k = qkT[:, hd, :], qkT[:, HA + hd, :]
                    b0, b1 = bias_r[:, hd, 0:P], bias_r[:, hd, P:2 * P]
                    pe.matmul(ps[:, hd, 0:P], q[:, 0:P], k[:, 0:P], start=True, stop=False)
                    pe.matmul(ps[:, hd, 0:P], b0, anti, start=False, stop=True)
                    pe.matmul(ps[:, hd, P:384], q[:, P:S], k, start=True, stop=False)
                    pe.matmul(ps[:, hd, P:S], b1, anti, start=False, stop=False)
                    pe.matmul(ps[:, hd, S:384], b0, anti, start=False, stop=True).then_inc(s_sc, 1)
                for b in range(6):
                    pe.wait_ge(s_exp, 2 if b >= 3 else 1)
                    if b == 3:
                        pe.wait_ge(s_diff, 2)
                    transposes(pe, [(ps[:, b, j * P:(j + 1) * P],
                                     prob[:, (4 * b + j) // 3, (4 * b + j) % 3 * P:(4 * b + j) % 3 * P + P])
                                    for j in range(4)]).then_inc(s_pt, 1)
                pe.wait_ge(s_ptv, 3)
                pe.wait_ge(s_pta, 3)
                for tt in range(TT):
                    for hd in range(HA):
                        o = ps[:, 6 + tt, hd * DA:(hd + 1) * DA]
                        for j in range(tt + 1):
                            mm = pe.matmul(o, probT[:, 3 * hd + tt + j, :],
                                           p1[:, j, 2 * 512 + hd * DA:2 * 512 + (hd + 1) * DA],
                                           start=j == 0, stop=j == tt)
                mm.then_inc(s_o, 1)
                pe.wait_ge(s_sq, 1)
                for u in range(2 * U):
                    mm = pe.matmul(ps[:, 0, u:u + 1], at(O_H, 8 * S)[:, u * P:(u + 1) * P], ones[:, 0:1], start=True, stop=True)
                mm.then_inc(s_ssum, 1)

        gb = at(O_B + 320, 12, U)
        O_C = O_B + 512
        kbg, vb, T, TI, X, L = (at(O_C + i * 1024, U, P) for i in range(6))
        AT = at(O_C + 6 * 1024, U, P)
        vnew = at(O_C + 7 * 1024, U, P)
        wT = at(O_X_LO, HD, P)
        kdec = at(O_X_LO + 512, HD, P)
        assert O_C + 8 * 1024 <= WORDS
        Cm = [at(O_H + i * 1024, U, P) for i in range(2)]
        O_CI = O_CV
        Dm, DT, gcB = (at(O_CI + i * 1024, U, P) for i in range(3))
        state = at(O_X_HI, HD, P)
        qgT = at(O_X_HI + 512, HD, P)
        lev = at(O_P1, 7, P)
        g_, beta_, gc_, eg_, egk_, tmp_, beg_ = (gb[:, i, :] for i in range(7))
        ab = ba.rearrange("p t (b h) -> p t b h", b=2)
        inv_wide = at(O_H, 2 * U, P)
        (s_inv, s_invT, s_lv, s_qkn, s_gpre, s_ge, s_gl, s_g, s_gcm,
         s_gco, s_gexp, s_diff, s_dexp, s_tk, s_tko, s_kk, s_L, s_dv, s_sb) = (
            sem("dn_" + n) for n in (
                "inverse_norms", "inverse_norms_spread", "level_steps", "qk_normed", "gate_sum", "gate_exp", "gate_ln", "gate", "cumulated", "cumulated_rows", "gate_exps",
                "differences", "decays", "kv_transposed", "kv_rows", "grams", "lower",
                "steps", "beta"))
        with nc.Block() as block:
            def level_masks(pool, masks, levels, sem_steps, flip):
                step = Steps(pool, sem_steps)
                step(pool.memset(masks, 0.0))
                for i in range(levels):
                    s_ = 1 << i
                    v = masks[:, i, :].rearrange("p (b h r) -> p b h r", h=2, r=s_)[:, :, 1 if flip else 0, :]
                    step(pool.memset(v, 1.0))
                    lo = 0 if flip else s_
                    step(pool.affine_select(out=v, in_=v, compare_op=ALU.is_ge, fill=0.0, base=-lo,
                                            pattern=[[-2 * s_, P // (2 * s_)], [0, s_]], channel_multiplier=1))
                    step(pool.affine_select(out=v, in_=v, compare_op=ALU.is_ge, fill=0.0, base=lo + s_ - 1,
                                            pattern=[[2 * s_, P // (2 * s_)], [0, s_]], channel_multiplier=-1))

            @block.gpsimd
            def _(pool):
                level_masks(pool, lev, 7, s_lv, False)

            @block.scalar
            def _(act):
                act.activation(beta_.rearrange("p (t h) -> p t h", h=HD), ab[:, :, 0, :], ACT.Sigmoid).then_inc(s_sb, 1)
                act.wait_ge(s_gpre, 1)
                act.activation(tmp_, tmp_, ACT.Exp, scale=-1.0).then_inc(s_ge, 1)
                act.wait_ge(s_par_dn, 48)
                act.activation(dn_par[:, 8:12], dn_par[:, 0:4], ACT.Exp).then_inc(s_ge, 1)
                act.wait_ge(s_ge, 1)
                act.activation(tmp_, tmp_, ACT.Ln, bias=1.0).then_inc(s_gl, 1)
                act.wait_ge(s_gco, 1)
                act.activation(eg_, gc_, ACT.Exp).then_inc(s_gexp, 1)
                act.wait_ge(s_diff, 1)
                act.activation(qgT, gcB[:, HD:U, :], ACT.Exp).then_inc(s_gexp, 1)
                act.activation(egk_[:, 0:HD], egk_[:, 0:HD], ACT.Exp).then_inc(s_gexp, 1)
                act.activation(Dm, Dm, ACT.Exp).then_inc(s_dexp, 1)
                act.activation(DT, DT, ACT.Exp).then_inc(s_dexp, 1)

            @block.vector
            def _(dve):
                step = Steps(dve, s_dv)
                step(dve.reciprocal(dn_norm, dn_norm))
                step(dve.tensor_scalar(dn_norm[:, 0:U], dn_norm[:, 0:U], P ** -0.5, None, ALU.mult))
                dve.tensor_copy(inv_wide, wide(dn_norm, P)).then_inc(s_inv, 1)
                dve.wait_ge(s_par_dn, 48)
                for tt in range(TT):
                    one = dve.tensor_tensor(gc_[:, tt * HD:(tt + 1) * HD], ab[:, tt, 1, :], dn_par[:, 4:8], ALU.add)
                step(one)
                step(dve.tensor_scalar(tmp_, gc_, -1.0, None, ALU.mult))
                dve.tensor_tensor(tmp_, tmp_, gc_, ALU.max).then_inc(s_gpre, 1)
                dve.wait_ge(s_gl, 1)
                step(dve.scalar_tensor_tensor(out=tmp_, in0=gc_, scalar=0.0, in1=tmp_, op0=ALU.max, op1=ALU.add))
                for tt in range(TT):
                    one = dve.scalar_tensor_tensor(out=g_[:, tt * HD:(tt + 1) * HD], in0=tmp_[:, tt * HD:(tt + 1) * HD],
                                                   scalar=-1.0, in1=dn_par[:, 8:12], op0=ALU.mult, op1=ALU.mult)
                step(one)
                step(dve.tensor_scalar(g_, g_, -110.0, None, ALU.max))
                dve.tensor_copy(X, wide(g_, P)).then_inc(s_g, 1)
                dve.wait_ge(s_invT, 1)
                dve.tensor_tensor(conv[:, 0:8, :], conv[:, 0:8, :], psf[:, 0:2048].rearrange("p (a t) -> p a t", t=S),
                                  ALU.mult).then_inc(s_qkn, 1)
                dve.wait_ge(s_gcm, 1)
                step(dve.tensor_copy(gcB, psf[:, 2048:3072].rearrange("p (u t) -> p u t", t=P)))
                dve.tensor_copy(gc_, ps[:, 6, 0:U]).then_inc(s_gco, 1)
                dve.wait_ge(s_gco, 1)
                step(dve.tensor_tensor(Dm, wide(gc_, P), gcB, ALU.subtract))
                step(dve.tensor_scalar(DT, Dm, -1.0, 0.0, ALU.mult, ALU.min))
                step(dve.tensor_scalar(Dm, Dm, 0.0, None, ALU.min))
                dve.tensor_tensor(egk_[:, 0:HD], gcB[:, 0:HD, P - 1], gc_[:, 0:HD], ALU.subtract).then_inc(s_diff, 1)
                dve.tensor_copy(T, ident.unsqueeze(1).to_broadcast([P, U, P])).then_inc(s_L, 1)
                dve.tensor_copy(TI, ident.unsqueeze(1).to_broadcast([P, U, P])).then_inc(s_L, 1)
                dve.wait_ge(s_dexp, 2)
                dve.wait_ge(s_gexp, 3)
                dve.wait_ge(s_sb, 1)
                step(dve.tensor_tensor(Dm, Dm, strict_low.unsqueeze(1).to_broadcast([P, U, P]), ALU.mult))
                step(dve.tensor_tensor(Dm, Dm, wide(beta_, P), ALU.mult))
                step(dve.tensor_tensor(DT, DT, upper.unsqueeze(1).to_broadcast([P, U, P]), ALU.mult))
                step(dve.tensor_tensor(beg_, beta_, eg_, ALU.mult))
                dve.wait_ge(s_kk, 1)
                dve.tensor_tensor(L, psf[:, 0:1024].rearrange("p (u t) -> p u t", t=P), Dm, ALU.mult).then_inc(s_L, 1)
                dve.tensor_tensor(AT, psf[:, 1024:2048].rearrange("p (u t) -> p u t", t=P), DT, ALU.mult).then_inc(s_L, 1)
                step(dve.tensor_tensor(qgT, qgT, conv[:, 0:4, P:S], ALU.mult))
                dve.wait_ge(s_tk, 1)
                kt = psf[:, 2048:3072].rearrange("p (u t) -> p u t", t=P)
                vt = psf[:, 3072:4096].rearrange("p (u t) -> p u t", t=P)
                dve.tensor_tensor(kbg, kt, wide(beg_, P), ALU.mult)
                dve.tensor_tensor(kdec, kt[:, 0:HD, :], wide(egk_[:, 0:HD], P), ALU.mult)
                dve.tensor_tensor(vb, vt, wide(beta_, P), ALU.mult).then_inc(s_tko, 1)

            @block.tensor
            def _(pe):
                pe.wait_ge(s_inv, 1)
                for u in range(2 * U):
                    mm = pe.matmul(psf[:, u * P:(u + 1) * P], inv_wide[:, u, :], ident, start=True, stop=True)
                mm.then_inc(s_invT, 1)
                pe.wait_ge(s_g, 1)
                pe.matmul(ps[:, 6, 0:U], upper, g_, start=True, stop=True)
                for u in range(U):
                    mm = pe.matmul(psf[:, 2048 + u * P:2048 + (u + 1) * P], X[:, u, :], upper, start=True, stop=True)
                mm.then_inc(s_gcm, 1)
                pe.wait_ge(s_qkn, 1)
                for b in range(2):
                    for u in range(U):
                        c, hd = divmod(u, HD)
                        q, k = conv[:, hd, c * P:(c + 1) * P], conv[:, 4 + hd, c * P:(c + 1) * P]
                        mm = pe.matmul(psf[:, b * 1024 + u * P:b * 1024 + (u + 1) * P], k, (k, q)[b], start=True, stop=True)
                mm.then_inc(s_kk, 1)
                pe.wait_ge(s_gco, 1)
                transposes(pe, [(psf[:, 2048 + w * 1024 + u * P:2048 + w * 1024 + (u + 1) * P],
                                 conv[:, 4 + 4 * w + u % HD, u // HD * P:(u // HD + 1) * P])
                                for w in range(2) for u in range(U)]).then_inc(s_tk, 1)

        s_C, s_xp, s_xe, s_y, s_T, s_gz = (sem("inv_" + n) for n in (
            "level_part", "x_product", "x_copied", "update_product", "updated", "gain_gate"))
        (s_u, s_ue, s_uT, s_w, s_wT, s_st, s_ste, s_wS, s_vn, s_o, s_oe, s_std, s_dv) = (sem("delta_" + n) for n in (
            "u", "u0_copied", "u1_copied", "w", "w_copied", "state", "state_copied", "w_state", "v_new", "out",
            "out_sums", "out_std", "steps"))
        with nc.Block() as block:
            @block.gpsimd
            def _(pool):
                for i in range(7):
                    if i == 2:
                        pool.wait_ge(s_T, 2)
                    elif i > 2:
                        pool.wait_ge(s_xp, 2 * (i - 2))
                    pool.tensor_tensor(Cm[i % 2], L, lev[:, i:i + 1, :].to_broadcast([P, U, P]), ALU.mult)\
                        .then_inc(s_C, 1)
                for tt in range(TT):
                    z3 = zsil[:, tt, :].rearrange("p (h d) -> p h d", d=P)
                    one = pool.tensor_tensor(z3, z3, dn_gain.unsqueeze(1).to_broadcast([P, HD, P]), ALU.mult)
                one.then_inc(s_gz, 1)

            @block.tensor
            def _(pe):
                pe.wait_ge(s_C, 1)
                for a in range(2):
                    transposes(pe, [(psf[:, 2048 + u * P:2048 + (u + 1) * P], Cm[0][:, u, :])
                                    for u in range(4 * a, 4 * a + 4)]).then_inc(s_y, 1)
                for i in range(1, 7):
                    pe.wait_ge(s_C, i + 1)
                    for a in range(2):
                        pe.wait_ge(s_T, 2 * (i - 1) + a + 1)
                        for u in range(4 * a, 4 * a + 4):
                            mm = pe.matmul(psf[:, u * P:(u + 1) * P], Cm[i % 2][:, u, :], TI[:, u, :], start=True, stop=True)
                        mm.then_inc(s_xp, 1)
                    for a in range(2):
                        pe.wait_ge(s_xe, 2 * (i - 1) + a + 1)
                        for u in range(4 * a, 4 * a + 4):
                            pe.matmul(psf[:, 1024 + u * P:1024 + (u + 1) * P], X[:, u, :], T[:, u, :], start=True, stop=True)
                            mm = pe.matmul(psf[:, 2048 + u * P:2048 + (u + 1) * P], T[:, u, :], X[:, u, :],
                                           start=True, stop=True)
                        mm.then_inc(s_y, 1)
                pe.wait_ge(s_T, 14)
                for u in range(U):
                    mm = pe.matmul(psf[:, u * P:(u + 1) * P], TI[:, u, :], vb[:, u, :], start=True, stop=True)
                mm.then_inc(s_u, 1)
                for hd in range(HD):
                    mm = pe.matmul(ps[:, 2, hd * P:(hd + 1) * P], kbg[:, HD + hd, :], TI[:, HD + hd, :], start=True, stop=True)
                mm.then_inc(s_w, 1)
                pe.wait_ge(s_ue, 1)
                for hd in range(HD):
                    mm = pe.matmul(ps[:, 3, hd * P:(hd + 1) * P], kdec[:, hd, :], vnew[:, hd, :], start=True, stop=True)
                mm.then_inc(s_st, 1)
                for hd in range(HD):
                    mm = pe.matmul(ps[:, 5, hd * P:(hd + 1) * P], AT[:, hd, :], vnew[:, hd, :], start=True, stop=True)
                mm.then_inc(s_o, 1)
                pe.wait_ge(s_wT, 1)
                pe.wait_ge(s_ste, 1)
                for hd in range(HD):
                    mm = pe.matmul(ps[:, 4, hd * P:(hd + 1) * P], wT[:, hd, :], state[:, hd, :], start=True, stop=True)
                mm.then_inc(s_wS, 1)
                pe.wait_ge(s_vn, 1)
                for hd in range(HD):
                    pe.matmul(ps[:, 6, hd * P:(hd + 1) * P], qgT[:, hd, :], state[:, hd, :], start=True, stop=False)
                    mm = pe.matmul(ps[:, 6, hd * P:(hd + 1) * P], AT[:, HD + hd, :], vnew[:, HD + hd, :],
                                   start=False, stop=True)
                mm.then_inc(s_o, 1)

            @block.scalar
            def _(act):
                for i in range(1, 7):
                    for a in range(2):
                        act.wait_ge(s_xp, 2 * (i - 1) + a + 1)
                        if i > 1:
                            act.wait_ge(s_y, 2 * (i - 1) + a + 1)
                        act.copy(X[:, 4 * a:4 * a + 4, :], ps[:, a, :].rearrange("p (u t) -> p u t", t=P)).then_inc(s_xe, 1)
                act.wait_ge(s_w, 1)
                act.copy(wT, ps[:, 2, :].rearrange("p (u t) -> p u t", t=P)).then_inc(s_wT, 1)
                act.wait_ge(s_st, 1)
                act.copy(state, ps[:, 3, :].rearrange("p (u t) -> p u t", t=P)).then_inc(s_ste, 1)
                act.wait_ge(s_oe, 1)
                act.activation(tiny[:, 8:16], tiny[:, 0:8], ACT.Sqrt, bias=eps, scale=1.0 / P).then_inc(s_std, 1)

            @block.vector
            def _(dve):
                step = Steps(dve, s_dv)
                for i in range(7):
                    for a in range(2):
                        dve.wait_ge(s_y, 2 * i + a + 1)
                        if i:
                            dve.wait_ge(s_T, 2 * i)
                        half = slice(4 * a, 4 * a + 4)
                        dve.tensor_tensor(T[:, half, :], T[:, half, :], Cm[0][:, half, :] if i == 0 else
                                          ps[:, 2 + a, :].rearrange("p (u t) -> p u t", t=P), ALU.subtract)
                        dve.tensor_tensor(TI[:, half, :], TI[:, half, :],
                                          ps[:, 4 + a, :].rearrange("p (u t) -> p u t", t=P), ALU.subtract).then_inc(s_T, 1)
                dve.wait_ge(s_u, 1)
                dve.tensor_copy(vnew[:, 0:HD, :], ps[:, 0, :].rearrange("p (u t) -> p u t", t=P)).then_inc(s_ue, 1)
                dve.tensor_copy(vnew[:, HD:U, :], ps[:, 1, :].rearrange("p (u t) -> p u t", t=P)).then_inc(s_uT, 1)
                dve.wait_ge(s_uT, 1)
                dve.wait_ge(s_wS, 1)
                dve.tensor_tensor(vnew[:, HD:U, :], vnew[:, HD:U, :], ps[:, 4, :].rearrange("p (u t) -> p u t", t=P),
                                  ALU.subtract).then_inc(s_vn, 1)
                dve.wait_ge(s_o, 2)
                o = mix[:, :, 512:1024]
                step(dve.tensor_copy(o, ps[:, 5:7, :]))
                sq = at(O_C, TT, 512)
                step(dve.tensor_tensor(sq, o, o, ALU.mult))
                dve.tensor_reduce(tiny[:, 0:8], sq.rearrange("p t (h d) -> p (t h) d", d=P), AX, ALU.add).then_inc(s_oe, 1)
                dve.wait_ge(s_std, 1)
                step(dve.reciprocal(tiny[:, 16:24], tiny[:, 8:16]))
                dve.wait_ge(s_gz, 1)
                for tt in range(TT):
                    o3 = o[:, tt, :].rearrange("p (h d) -> p h d", d=P)
                    step(dve.tensor_tensor(o3, o3, wide(tiny[:, 16 + 4 * tt:20 + 4 * tt], P), ALU.mult))
                    step(dve.tensor_tensor(o[:, tt, :], o[:, tt, :], zsil[:, tt, :], ALU.mult))

        def turn_stage(tag, rows, second=None, second_at=(0, 0)):
            s_t, s_hi, s_lo = (sem(f"{tag}_{n}") for n in ("transposed", "hi", "lo"))
            with nc.Block() as block:
                @block.tensor
                def _(pe):
                    turn_rows(pe, rows, s_t)
                    if second is not None:
                        turn_rows(pe, second, s_t, 4)

                @block.scalar
                def _(act):
                    turned_hi(act, s_t, s_hi)
                    if second is not None:
                        turned_hi(act, s_t, s_hi, 4, second_at[0])

                @block.vector
                def _(dve):
                    turned_lo(dve, s_hi, s_lo)
                    if second is not None:
                        turned_lo(dve, s_hi, s_lo, 4, *second_at)

        def rows_stage(tag, segs, chunks, upto, lefts, dve_parts, beside=None, act_after=None,
                       pool_part=None):
            s_steps = sem(f"{tag}_steps")
            units = UPC * chunks
            with nc.Block() as block:
                @block.sync
                def _(sp):
                    if beside:
                        beside(sp)
                    st.issue(sp, upto)

                @block.tensor
                def _(pe):
                    for j, (_n0, g0) in enumerate(segs):
                        for i in range(units):
                            await_unit(pe, g0 + i, 0)
                            k, c = divmod(i, 2)
                            for tt in range(TT):
                                mm = three(pe, ps[:, 4 * j + 2 * tt + c, :],
                                           [a[:, k, tt * P:(tt + 1) * P] for a in lefts[j]],
                                           [w[(g0 + i) % BUFFERS] for w in (w_hi, w_lo)], k == 0, k == units // 2 - 1)
                            mm.then_inc(unit_used, 1)

                @block.scalar
                def _(act):
                    for n0, g0 in segs:
                        for i in range(units):
                            split_hi(act, n0 + i // UPC, g0 + i, i % UPC, 0)
                    if act_after:
                        act_after(act)

                if pool_part:
                    @block.gpsimd
                    def _(pool):
                        pool_part(pool)

                @block.vector
                def _(dve):
                    step = Steps(dve, s_steps)
                    for j, (n0, g0) in enumerate(segs):
                        for i in range(units):
                            split_lo(dve, n0 + i // UPC, g0 + i, i % UPC, 0)
                            if j and i == 3:
                                dve.wait_ge(unit_used, used_value(segs[j - 1][1] + units - 1))
                                dve_parts[j - 1](dve, step)
                    dve.wait_ge(unit_used, used_value(segs[-1][1] + units - 1))
                    dve_parts[-1](dve, step)

        def product_rows(tt, j=0):
            return psf[:, j * 2048 + tt * D:j * 2048 + (tt + 1) * D]

        turn_stage("mix1", mix)
        O_TMP = O_C

        s_xsum, s_xsq, s_wt = sem("x1_rows"), sem("x1_squares"), sem("norm2_weight")

        def norm2_weight(pool):
            pool.wait_ge(s_gain, 16)
            pool.tensor_tensor(scale2, scale2, gain, ALU.mult).then_inc(s_wt, 1)
            pool.wait_ge(s_wt, 1)
            pool.tensor_tensor(scale2, scale2, gain, ALU.add)
            pool.tensor_copy(gate2, mods[:, 5, :])

        def add_mix(dve, step):
            for tt in range(TT):
                step(dve.tensor_tensor(at(O_TMP + tt * D, D), product_rows(tt), gate1, ALU.mult))
                dve.tensor_tensor(x[:, tt, :], x[:, tt, :], at(O_TMP + tt * D, D), ALU.add).then_inc(s_xsum, 1)

        s_gain = lasting_sem("gain_loaded")
        s_sp = sem("x_stored")

        def load_gain(name):
            return lambda sp: sp.dma_start(gain, A[name].to_broadcast([P, D])).then_inc(s_gain, 16)

        rows_stage("w_out", [n_wout], 4, n_query[0] + SLOTS, [(x_hi, x_lo)], [add_mix], load_gain("norm2_gain"),
                   lambda act: norm_roots(act, h, x, s_xsq, s_xsum), norm2_weight)

        def store_x(sp):
            sp.dma_start(x_spill, at(O_R, TT * D)).then_inc(s_sp, 16)
            sp.wait_ge(s_sp, 16)

        norm_stage("norm2", h, x, s_gain, 16, shift2, beside=store_x, weight=scale2, roots=False)

        NH, KD, NK, TOP = 8, 256, 128, 16
        acts = at(O_R, P, S)
        CLEAR = 72
        O_Q = O_R + CLEAR * S
        qT = at(O_Q - 2 * NH * S, 2 * NH, S)
        qrows = at(O_Q, TT, NH * KD)
        score = at(O_Q, TT * 2 * NH, NK)
        O_K = O_Q + TT * NH * KD
        keys = at(O_K, 2, P)
        keysT = at(O_K + 256, 2, P)
        q_gain = at(O_K + 512, KD)
        O_V = O_K + 768
        best = at(O_V, TT * 2 * NH, TOP)
        best_at = at(O_V + 512, TT * 2 * NH, TOP)
        best_ix = at(O_V + 1024, TT * 2 * NH, TOP)
        picked = at(O_V + 1536, TT * NH, TOP)
        picked_at = at(O_V + 1792, TT * NH, TOP)
        O_M = O_V + 2048
        cand = at(O_M, TT * NH, TOP * TOP)
        part_of = at(O_M + 4096, 2, P)
        part_u = at(O_M + 4352, 2, P)
        assert O_M + 4608 <= O_R + P * S
        pickT = at(O_PICKS, 3, S)
        (s_ld, s_qa, s_qv, s_sq, s_std, s_qn, s_kt, s_kto, s_t, s_tv, s_ta, s_sc, s_scv, s_sca, s_dv) = (
            sem("query_" + n) for n in (
                "params", "rows_act", "rows_dve", "squares", "std", "normed", "keys_transposed", "keysT", "transposed",
                "qT_dve", "qT_act", "scores", "scores_dve", "scores_act", "steps"))
        with nc.Block() as block:
            @block.sync
            def _(sp):
                sp.dma_start(keys[:, 0, :], A["peer_sub_keys_1"][0]).then_inc(s_ld, 16)
                sp.dma_start(keys[:, 1, :], A["peer_sub_keys_2"][0]).then_inc(s_ld, 16)
                sp.dma_start(q_gain, A["peer_query_gain"].to_broadcast([P, KD])).then_inc(s_ld, 16)
                st.issue(sp, n_down[0] + SLOTS)

            @block.tensor
            def _(pe):
                for c in range(4):
                    if c >= 2:
                        pe.wait_ge(s_qv, c - 1)
                        pe.wait_ge(s_qa, c - 1)
                    product_group(pe, c, n_query[1] + KT * c, 0, "t", (x_hi, x_lo))
                pe.wait_ge(s_ld, 48)
                transposes(pe, [(ps[:, 6, i * P:(i + 1) * P], keys[:, i, :]) for i in range(2)]).then_inc(s_kt, 1)
                pe.wait_ge(s_qv, 3)
                pe.wait_ge(s_qa, 3)
                for b in range(8):
                    if b % 2 == 0:
                        pe.wait_ge(s_qn, b // 2 + 1)
                    if b == 4:
                        pe.wait_ge(s_qv, 4)
                        pe.wait_ge(s_qa, 4)
                    if b == 6:
                        pe.wait_ge(s_kto, 1)
                    transposes(pe, [(ps[:, b, (u % 2) * S + tt * P:(u % 2) * S + (tt + 1) * P],
                                     qrows[:, tt, u * P:(u + 1) * P])
                                    for u in (2 * b, 2 * b + 1) for tt in range(TT)]).then_inc(s_t, 1)
                for b in range(8):
                    if b == 0:
                        pe.wait_ge(s_tv, 4)
                        pe.wait_ge(s_ta, 4)
                    for j in range(4):
                        u = 4 * b + j
                        mm = pe.matmul(ps[:, b, j * P:(j + 1) * P], qT[:, u % 16, u // 16 * P:(u // 16 + 1) * P],
                                       keysT[:, u % 2, :], start=True, stop=True)
                    mm.then_inc(s_sc, 1)

            @block.vector
            def _(dve):
                step = Steps(dve, s_dv)

                def scale(c):
                    dve.wait_ge(s_std, c + 1)
                    inv = tiny[:, 64 + 4 * c:68 + 4 * c]
                    step(dve.reciprocal(inv, tiny[:, 32 + 4 * c:36 + 4 * c]))
                    for i in range(4):
                        tt, hd = i // 2, 2 * c + i % 2
                        v = qrows[:, tt, hd * KD:(hd + 1) * KD]
                        one = dve.scalar_tensor_tensor(out=v, in0=v, scalar=inv[:, i:i + 1], in1=q_gain,
                                                       op0=ALU.mult, op1=ALU.mult)
                    one.then_inc(s_qn, 1)

                def beside(c, u):
                    if c == 1 and u == 6:
                        dve.wait_ge(s_ld, 48)
                    if c and u == 7:
                        scale(c - 1)

                split_groups(dve, split_lo, 3, n_query, 4, lambda c: dve.tensor_copy(
                    qrows[:, 0, c * 512:(c + 1) * 512], ps[:, c % 2 * 4, :]).then_inc(s_qv, 1), beside)
                dve.wait_ge(s_kt, 1)
                dve.tensor_copy(keysT, ps[:, 6, 0:256].rearrange("p (a n) -> p a n", n=P)).then_inc(s_kto, 1)
                scale(3)
                for b in range(0, 8, 2):
                    dve.wait_ge(s_t, b + 1)
                    dve.tensor_copy(qT[:, 2 * b:2 * b + 2, :], ps[:, b, :].rearrange("p (a t) -> p a t", t=S)).then_inc(s_tv, 1)
                for b in range(0, 8, 2):
                    dve.wait_ge(s_sc, b + 1)
                    dve.tensor_copy(score[:, 4 * b:4 * b + 4, :], ps[:, b, :].rearrange("p (a t) -> p a t", t=P)).then_inc(s_scv, 1)

            @block.scalar
            def _(act):
                def roots(c):
                    act.wait_ge(s_qa, c + 1)
                    act.wait_ge(s_qv, c + 1)
                    for i in range(4):
                        tt, hd, n = i // 2, 2 * c + i % 2, 4 * c + i
                        act.activation(at(O_Q - 4096 + n * KD, KD), qrows[:, tt, hd * KD:(hd + 1) * KD], ACT.Square,
                                       accum_out=tiny[:, n:n + 1]).then_inc(s_sq, 1)
                    act.wait_ge(s_sq, 4 * c + 4)
                    act.activation(tiny[:, 32 + 4 * c:36 + 4 * c], tiny[:, 4 * c:4 * c + 4], ACT.Sqrt, bias=eps,
                                   scale=1.0 / KD).then_inc(s_std, 1)

                def beside(c, u):
                    if c and u == 6:
                        roots(c - 1)

                split_groups(act, split_hi, 4, n_query, 4, lambda c: act.copy(
                    qrows[:, 1, c * 512:(c + 1) * 512], ps[:, c % 2 * 4 + 1, :]).then_inc(s_qa, 1), beside)
                roots(3)
                for b in range(1, 8, 2):
                    act.wait_ge(s_t, b + 1)
                    act.copy(qT[:, 2 * b:2 * b + 2, :], ps[:, b, :].rearrange("p (a t) -> p a t", t=S)).then_inc(s_ta, 1)
                for b in range(1, 8, 2):
                    act.wait_ge(s_sc, b + 1)
                    act.copy(score[:, 4 * b:4 * b + 4, :], ps[:, b, :].rearrange("p (a t) -> p a t", t=P)).then_inc(s_sca, 1)

        NI = 2
        (s_E, s_L, s_M, s_G, s_route, s_dv) = (sem("experts_" + n) for n in (
            "hi", "lo", "product", "gelu", "routed", "steps"))
        n0 = n_down[0]
        ROUND = NI * SLOTS
        d_hi, d_lo = ([atr(o + i * D, D) for i in range(2)] for o in (O_W_HI, O_W_LO))

        with nc.Block() as block:
            @block.sync
            def _(sp):
                st.issue(sp, n_up[0] + SLOTS)

            @block.tensor
            def _(pe):
                pe.sem_inc(s_M, 2)

                def turn(i, rounds):
                    if i % NI == 0:
                        pe.wait_ge(landed[(n0 + i // NI) % SLOTS], rounds * 16 + st.landed_value(n0 + i // NI))
                    pe.wait_ge(s_L, rounds * ROUND + (i + 1))
                    w = st.words(n0 + i // NI, i % NI * D, D)
                    b = i % 2
                    transposes(pe, [(psf[:, b * 1024 + k * P:b * 1024 + (k + 1) * P], w[:, k * P:(k + 1) * P])
                                    for k in range(KT)]).then_inc(turned, 1)

                def product(i, rounds):
                    pe.wait_ge(s_L, rounds * ROUND + (i + 3))
                    if i % 2 == 0:
                        pe.wait_ge(s_G, rounds * (ROUND // 2) + (i // 2 + 1))
                    o = ps[:, 4 + i // 2 % 2, i % 2 * S:(i % 2 + 1) * S]
                    for k in range(KT):
                        ks = slice(k * P, (k + 1) * P)
                        mm = three(pe, o, [d_hi[i % 2][:, ks], d_lo[i % 2][:, ks]], [x_hi[:, k, :], x_lo[:, k, :]],
                                   k == 0, k == KT - 1)
                    mm.then_inc(s_M, 1)

                turn(0, 0)
                with pe.Fori(0, P // ROUND - 1) as r:
                    for i in range(ROUND):
                        turn(i + 1, r)
                        product(i, r)
                for i in range(P - ROUND, P):
                    if i + 1 < P:
                        turn(i + 1, 0)
                    product(i, 0)

            @block.scalar
            def _(act):
                act.sem_inc(s_G, 2)

                def hi(i, rounds):
                    act.wait_ge(s_M, rounds * ROUND + (i + 1))
                    act.wait_ge(turned, rounds * ROUND + (i + 1))
                    act.copy(d_hi[i % 2], psf[:, i % 2 * 1024:(i % 2 + 1) * 1024]).then_inc(s_E, 1)

                def gelu(p, rounds):
                    act.wait_ge(s_M, rounds * ROUND + (2 * p + 4))
                    act.wait_ge(s_const, 1)
                    act.activation(mem[:, bass.ds(rounds * (ROUND * S) + (O_R + 2 * p * S), 2 * S)],
                                   ps[:, 4 + p % 2, :], ACT.Gelu).then_inc(s_G, 1)

                def round_(rounds):
                    for i in range(1, ROUND + 1):
                        hi(i, rounds)
                        if i % 2 == 0:
                            gelu(i // 2 - 1, rounds)

                hi(0, 0)
                with act.Fori(0, CLEAR // ROUND) as r:
                    round_(r)
                act.wait_ge(s_route, 1)
                with act.Fori(CLEAR // ROUND, P // ROUND - 1) as r:
                    round_(r)
                for i in range(P - ROUND + 1, P):
                    hi(i, 0)
                    if i % 2 == 0:
                        gelu(i // 2 - 1, 0)
                gelu(P // 2 - 1, 0)

            @block.vector
            def _(dve):
                step = Steps(dve, s_dv)
                dve.sem_inc(s_L, 2)
                u32 = lambda ap: ap.bitcast(U32)

                def lo(i):
                    dve.wait_ge(s_E, i + 1)
                    dve.tensor_tensor(d_lo[i % 2], psf[:, i % 2 * 1024:(i % 2 + 1) * 1024], d_hi[i % 2].bitcast(F32),
                                      ALU.subtract).then_inc(s_L, 1)

                def top16(values, top, where, rows):
                    for r in rows:
                        one = dve.max(top[:, r, 0:8], values[:, r, :])
                        yield
                    step(one)
                    for r in rows:
                        one = dve.max_index(u32(where[:, r, 0:8]), top[:, r, 0:8], values[:, r, :])
                        yield
                    step(one)
                    for r in rows:
                        one = dve.match_replace(values[:, r, :], top[:, r, 0:8], values[:, r, :], -3.0e38)
                        yield
                    step(one)
                    for r in rows:
                        one = dve.max(top[:, r, 8:16], values[:, r, :])
                        yield
                    step(one)
                    for r in rows:
                        one = dve.max_index(u32(where[:, r, 8:16]), top[:, r, 8:16], values[:, r, :])
                        yield
                    step(one)

                def routing():
                    yield from top16(score, best, best_at, range(TT * 2 * NH))
                    step(dve.tensor_copy(best_ix, u32(best_at)))
                    yield
                    for tt in range(TT):
                        for hd in range(NH):
                            a = best[:, tt * 16 + 2 * hd, :]
                            b = best[:, tt * 16 + 2 * hd + 1, :]
                            one = dve.tensor_tensor(cand[:, tt * NH + hd, :].rearrange("p (a b) -> p a b", b=TOP), wide(a, TOP),
                                                    b.unsqueeze(1).to_broadcast([P, TOP, TOP]), ALU.add)
                            yield
                    step(one)
                    yield from top16(cand, picked, picked_at, range(TT * NH))
                    for tt in range(TT):
                        at_ = u32(at(O_V + 1792 + tt * P, P))
                        step(dve.tensor_scalar(u32(part_u[:, 0, :]), at_, 4, None, ALU.logical_shift_right))
                        step(dve.tensor_scalar(u32(part_u[:, 1, :]), at_, 15, None, ALU.bitwise_and))
                        step(dve.tensor_copy(part_of, u32(part_u)))
                        yield
                        eq = at(O_M, P, TOP)
                        for half in range(2):
                            step(dve.tensor_tensor(eq, wide(part_of[:, half, :], TOP),
                                                   iota[:, 0:TOP].unsqueeze(1).to_broadcast([P, P, TOP]), ALU.is_equal))
                            for _ in range(5):
                                yield
                            for hd in range(NH):
                                e3 = eq[:, hd * TOP:(hd + 1) * TOP, :]
                                ix = best_ix[:, tt * 16 + 2 * hd + half, :]
                                one = dve.tensor_tensor(e3, e3, ix.unsqueeze(1).to_broadcast([P, TOP, TOP]), ALU.mult)
                                yield
                            step(one)
                            step(dve.tensor_reduce(pickT[:, half, tt * P:(tt + 1) * P], eq, AX, ALU.add))
                            for _ in range(5):
                                yield
                        pk = picked[:, tt * NH:(tt + 1) * NH, :]
                        step(dve.tensor_tensor(pickT[:, 2, tt * P:(tt + 1) * P].rearrange("p (h j) -> p h j", j=TOP), pk,
                                               pk[:, :, 0:1].to_broadcast([P, NH, TOP]), ALU.subtract))
                    dve.drain().then_inc(s_route, 1)

                route = routing()
                for i in range(P):
                    lo(i)
                    for _ in range(5):
                        next(route, None)
                for _ in route:
                    pass

        GT = 4
        GB = 4
        one1 = at(O_W_HI, GB, GT * P)
        one2 = at(O_W_LO, GB, GT * P)
        gated = at(O_X_HI, GB, GT * P)
        (s_e, s_gn, s_t, s_pt, s_o2, s_gd, s_mm, s_w, s_dv) = (sem("gates_" + n) for n in (
            "exp", "normed", "transposed", "picksT", "onehots", "gated", "product", "applied", "steps"))
        NG_ = S // GT
        with nc.Block() as block:
            @block.scalar
            def _(act):
                act.activation(pickT[:, 2, :], pickT[:, 2, :], ACT.Exp).then_inc(s_e, 1)

            @block.tensor
            def _(pe):
                pe.wait_ge(s_gn, 1)
                transposes(pe, [(psf[:, (i * TT + tt) * P:(i * TT + tt + 1) * P], pickT[:, i, tt * P:(tt + 1) * P])
                                for i in range(3) for tt in range(TT)]).then_inc(s_t, 1)
                pe.wait_ge(s_pt, 1)
                with pe.Fori(0, NG_ // GB) as r:
                    for b in range(GB):
                        pe.wait_ge(s_gd, r * GB + (b + 1))
                        pe.wait_ge(s_w, r * GB + (b + 1))
                        for j in range(GT):
                            mm = pe.matmul(ps[:, 2 + b, j * P:(j + 1) * P], one1[:, b, j * P:(j + 1) * P],
                                           gated[:, b, j * P:(j + 1) * P], start=True, stop=True)
                        mm.then_inc(s_mm, 1)

            @block.gpsimd
            def _(pool):
                pool.wait_ge(s_pt, 1)
                with pool.Fori(0, NG_ // GB) as r:
                    for b in range(GB):
                        pool.wait_ge(s_o2, r * GB + (b + 1))
                        pool.wait_ge(s_const, 1)
                        pool.tensor_tensor(gated[:, b, :].rearrange("p (t i) -> p t i", i=P),
                                           one2[:, b, :].rearrange("p (t i) -> p t i", i=P),
                                           wide(mem[:, bass.ds(r * (GB * GT) + (O_PICKS + 2 * S + b * GT), GT)], P),
                                           ALU.mult).then_inc(s_gd, 1)

            @block.vector
            def _(dve):
                step = Steps(dve, s_dv)
                dve.wait_ge(s_e, 1)
                g3 = pickT[:, 2, :].rearrange("p (a j) -> p a j", j=TOP)
                step(dve.tensor_reduce(tiny[:, 0:16], g3, AX, ALU.add))
                step(dve.reciprocal(tiny[:, 16:32], tiny[:, 0:16]))
                dve.tensor_tensor(g3, g3, wide(tiny[:, 16:32], TOP), ALU.mult).then_inc(s_gn, 1)
                dve.wait_ge(s_t, 1)
                dve.tensor_copy(at(O_PICKS, 3 * S), psf[:, 0:3 * S]).then_inc(s_pt, 1)
                dve.sem_inc(s_mm, GB)
                dve.sem_inc(s_w, GB)
                dve.wait_ge(s_pt, 1)

                def onehots(j, r):
                    b, t0 = j % GB, r * (GB * GT) + j * GT
                    dve.wait_ge(s_mm, r * GB + (j + 1))
                    dve.tensor_tensor(one1[:, b, :].rearrange("p (t i) -> p t i", i=P),
                                      wide(mem[:, bass.ds(t0 + O_PICKS, GT)], P),
                                      iota.unsqueeze(1).to_broadcast([P, GT, P]), ALU.is_equal)
                    dve.tensor_tensor(one2[:, b, :].rearrange("p (t i) -> p t i", i=P),
                                      wide(mem[:, bass.ds(t0 + (O_PICKS + S), GT)], P),
                                      iota.unsqueeze(1).to_broadcast([P, GT, P]), ALU.is_equal).then_inc(s_o2, 1)

                def apply(j, r):
                    dve.wait_ge(s_mm, r * GB + (j + GB + 1))
                    a = acts[:, :, bass.ds(r * (GB * GT) + j * GT, GT)]
                    dve.tensor_tensor(a, a, ps[:, 2 + j % GB, :].rearrange("p (t i) -> p i t", i=P), ALU.mult)\
                        .then_inc(s_w, 1)

                onehots(0, 0)
                onehots(1, 0)
                with dve.Fori(0, NG_ // GB - 1) as r:
                    for j in range(GB):
                        onehots(j + 2, r)
                        apply(j, r)
                for j in range(NG_ - GB, NG_):
                    if j + 2 < NG_:
                        onehots(j + 2, 0)
                    apply(j, 0)

        n0, g0 = n_up
        (s_xsum, s_xsq, s_ld, s_ah, s_al, s_hi, s_lo, s_t, s_end, s_dv) = (sem("up_" + n) for n in (
            "x_rows", "x_squares",
            "x_loaded", "weights_hi", "weights_lo", "yT_act", "yT_dve", "transposed", "last_product", "steps"))
        x_back = at(O_R + TT * D, TT, D)
        yT = at(O_X_HI, KT, S)
        a_hi, a_lo = (lambda b: atr(O_X_HI + b * 1024, 1024)), (lambda b: atr(O_X_LO + b * 1024, 1024))
        with nc.Block() as block:
            @block.sync
            def _(sp):
                st.issue(sp, n_in2a[0] + SLOTS)
                sp.wait_ge(s_end, 1)
                sp.dma_start(at(O_R + TT * D, TT * D), x_spill).then_inc(s_ld, 16)
                load_gain("norm1_gain_2")(sp)

            @block.tensor
            def _(pe):
                for b in range(4):
                    pe.matmul(ps[:, b, :], zeros, at(O_CONST, 512), start=True, stop=False, skip_group_check=True)

                def units(i, rounds, last=False):
                    b = i // 4 % 2
                    if i % 4 == 0:
                        pe.wait_ge(s_al, rounds * 2 + (i // 4 + 1))
                    for u in range(2):
                        await_unit(pe, g0 + 2 * i + u, rounds)
                        w = (2 * i + u) % BUFFERS
                        for kk in range(4):
                            k, ks = 4 * u + kk, slice(kk * P, (kk + 1) * P)
                            mm = three(pe, ps[:, k // 2, k % 2 * S:(k % 2 + 1) * S], [w_hi[w][:, ks], w_lo[w][:, ks]],
                                       [v(b)[:, i % 4 * S:(i % 4 + 1) * S] for v in (a_hi, a_lo)], False, last)
                        mm.then_inc(unit_used, 1)
                with pe.Fori(0, P // 8 - 1) as r:
                    for i in range(8):
                        units(i, r)
                for i in range(P - 8, P):
                    units(i, 0, i == P - 1)
                pe.wait_ge(s_hi, 1)
                pe.wait_ge(s_lo, 1)
                transposes(pe, [(psf[:, 2048 + tt * D + k * P:2048 + tt * D + (k + 1) * P], yT[:, k, tt * P:(tt + 1) * P])
                                for tt in range(TT) for k in range(KT)]).then_inc(s_t, 1)

            @block.scalar
            def _(act):
                def weights_hi(q, r):
                    act.wait_ge(s_const, 1)
                    act.copy(a_hi(q % 2), mem[:, bass.ds(r * (8 * S) + (O_R + q * (4 * S)), 4 * S)]).then_inc(s_ah, 1)

                def round_(r, last=False):
                    for i in range(16):
                        j = i + (2 * P - 16 if last else 0)
                        split_hi(act, n0 + j // UPC, g0 + j, j % UPC, r)
                        if i % 8 == 3 and not (last and i > 8):
                            weights_hi(i // 8 + 1 + (2 * (P // 8 - 1) if last else 0), 0 if last else r)
                weights_hi(0, 0)
                with act.Fori(0, P // 8 - 1) as r:
                    round_(r)
                round_(0, last=True)
                act.wait_ge(unit_used, used_value(g0 + 2 * P - 1))
                act.copy(at(O_X_HI, 1024), psf[:, 0:1024]).then_inc(s_hi, 1)
                norm_roots(act, h, x, s_xsq, s_xsum)

            @block.gpsimd
            def _(pool):
                with pool.Fori(0, P // 8) as r:
                    for q in range(2):
                        pool.wait_ge(s_ah, r * 2 + (q + 1))
                        pool.wait_ge(s_const, 1)
                        pool.tensor_tensor(a_lo(q), mem[:, bass.ds(r * (8 * S) + (O_R + q * (4 * S)), 4 * S)],
                                           a_hi(q).bitcast(F32), ALU.subtract).then_inc(s_al, 1)

            @block.vector
            def _(dve):
                step = Steps(dve, s_dv)
                with dve.Fori(0, P // 8) as r:
                    for i in range(16):
                        split_lo(dve, n0 + i // UPC, g0 + i, i % UPC, r)
                dve.wait_ge(unit_used, used_value(g0 + 2 * P - 1))
                dve.tensor_copy(at(O_X_HI + 1024, 1024), psf[:, 1024:2048]).then_inc(s_lo, 1)
                dve.sem_inc(s_end, 1)
                dve.wait_ge(s_t, 1)
                dve.wait_ge(s_ld, 16)
                for tt in range(TT):
                    step(dve.tensor_tensor(x[:, tt, :], psf[:, 2048 + tt * D:2048 + (tt + 1) * D], gate2, ALU.mult))
                    dve.tensor_tensor(x[:, tt, :], x[:, tt, :], x_back[:, tt, :], ALU.add).then_inc(s_xsum, 1)

        renew_semaphores()

        O_F = O_R + TT * D
        qfT = at(O_F, 16, S)
        O_P2 = O_F + 16 * S
        N_P2 = 7 * D
        p2 = at(O_P2, TT, N_P2)
        O_W = O_P2 + TT * N_P2

        norm_stage("norm1_2", h, x, s_gain, 32, roots=False)

        HH = 8
        NB = HH * S
        cum = at(O_W, HH, S)
        Z = [at(o, HH, S) for o in (O_W + NB, O_W + 2 * NB, O_X_HI, O_X_LO)]
        ZB = len(Z)
        kx = at(O_W + 3 * NB, HH, S)
        sT = at(O_W + 4 * NB, 2 * HH, P)
        cross = at(O_W + 5 * NB, HH, P)
        lev = at(O_W + 5 * NB + HH * P, 7, P)
        logits = mem[0:16, O_W + 5 * NB + HH * P + 7 * P:O_W + 5 * NB + HH * P + 8 * P]
        O_L = O_W + 5 * NB + HH * P + 8 * P
        lbT = at(O_L, 6, HH)
        hg_gain = at(O_L + 48, D)
        assert O_L + 48 + D <= WORDS
        q3, f3 = qfT[:, 0:HH, :], qfT[:, HH:2 * HH, :]
        SD = 64
        qk = p2[:, :, 2 * D:4 * D]
        sb_gain = at(O_W + 4 * NB, 2, D)
        sq2 = at(O_W + NB, TT, 2 * D)
        std2 = tiny[:, 64:128]

        (s_bank_v, s_bank_a, s_par, s_lv, s_lt, s_lm, s_le, s_sg, s_f, s_ln, s_dv, s_sq, s_sum, s_std, s_rstd, s_pl) = (
            sem("proj2_" + n) for n in (
                "bank_out_dve", "bank_out_act", "params", "level_steps", "logits_transposed", "logits_shifted",
                "logits_exp", "sigmoids", "forget", "log_forget", "steps", "qk_squares", "qk_sums", "qk_std",
                "qk_inverse_std", "pool_steps"))
        with nc.Block() as block:
            @block.sync
            def _(sp):
                sp.dma_start(logits, A["lb_logits_2"].rearrange("l (k p) -> (l k) p", p=P)).then_inc(s_par, 16)
                sp.dma_start(hg_gain, A["hg_out_norm_2"].rearrange("l h d -> l (h d)").to_broadcast([P, D])).then_inc(s_par, 16)
                for i, name in enumerate(("sb_q_norm_2", "sb_k_norm_2")):
                    sp.dma_start(sb_gain[:, i, :], A[name].rearrange("l h d -> l (h d)").to_broadcast([P, D])).then_inc(s_par, 16)
                st.issue(sp, n_hgo[0] + SLOTS)

            @block.tensor
            def _(pe):
                for c in range(4):
                    if c >= 2:
                        pe.wait_ge(s_bank_v, c - 1)
                        pe.wait_ge(s_bank_a, c - 1)
                    product_group(pe, c, n_in2a[1] + KT * c, 0, "f", (x_hi, x_lo))
                pe.wait_ge(s_bank_v, 3)
                pe.wait_ge(s_bank_a, 3)
                pe.wait_ge(s_par, 64)
                transposes(pe, [(ps[:, 3, 0:16], logits)]).then_inc(s_lt, 1)
                with pe.Fori(0, 7) as r:
                    for c in range(2):
                        pe.wait_ge(s_bank_v, r * 2 + (c + 3))
                        pe.wait_ge(s_bank_a, r * 2 + (c + 3))
                        product_group(pe, c, n_in2b[1] + KT * c, r, "t", (x_hi, x_lo))

            def qf_out(b, c):
                t = c * 4 + b * 2
                return qfT[:, t:t + 2, :], ps[:, c % 2 * 4 + 2 * b:c % 2 * 4 + 2 * b + 2, 0:S]

            def loop_groups(eng, b, split, copy, s_bank, early, late):
                n0, g0 = n_in2b

                def empty(c, rounds):
                    eng.wait_ge(unit_used, rounds * 16 + used_value(g0 + KT * c + 7))
                    eng.wait_ge(s_const, 1)
                    copy(mem[:, bass.ds(rounds * 1024 + (O_P2 + b * N_P2 + c * 512), 512)],
                         ps[:, c % 2 * 4 + b, :]).then_inc(s_bank, 1)
                for u in range(16):
                    split(eng, n0 + u // UPC, g0 + u, u % UPC, 0)
                    if u == 11:
                        empty(0, 0)
                    early(u)
                with eng.Fori(0, 4) as r:
                    for u in range(16, 32):
                        split(eng, n0 + u // UPC, g0 + u, u % UPC, r)
                        if u % 8 == 3:
                            empty(u // 8 - 1, r)
                for v in (5, 6):
                    for u in range(16 * v, 16 * v + 16):
                        split(eng, n0 + u // UPC, g0 + u, u % UPC, 0)
                        if u % 8 == 3:
                            empty(u // 8 - 1, 0)
                        late(v, u % 16)
                empty(13, 0)

            @block.vector
            def _(dve):
                step = Steps(dve, s_dv)
                lo_groups(dve, n_in2a, 4, lambda c: dve.tensor_copy(*qf_out(0, c)).then_inc(s_bank_v, 1))

                def early(u):
                    if u == 1:
                        dve.wait_ge(s_lt, 1)
                        step(dve.tensor_copy(lbT[:, 0:2, :], ps[:, 3, 0:16].rearrange("p (l k) -> p l k", l=2)))
                        step(dve.tensor_tensor(lbT[:, 2, :], lbT[:, 0, :], lbT[:, 1, :], ALU.max))
                    elif u == 2:
                        step(dve.tensor_tensor(lbT[:, 0, :], lbT[:, 0, :], lbT[:, 2, :], ALU.subtract))
                        dve.tensor_tensor(lbT[:, 1, :], lbT[:, 1, :], lbT[:, 2, :], ALU.subtract).then_inc(s_lm, 1)
                    elif u == 7:
                        dve.wait_ge(s_le, 1)
                        step(dve.tensor_tensor(lbT[:, 2, :], lbT[:, 0, :], lbT[:, 1, :], ALU.add))
                        step(dve.reciprocal(lbT[:, 3, :], lbT[:, 2, :]))
                    elif u == 8:
                        step(dve.tensor_tensor(lbT[:, 4, :], lbT[:, 0, :], lbT[:, 3, :], ALU.mult))
                        step(dve.tensor_scalar(lbT[:, 5, :], lbT[:, 4, :], -1.0, 1.0, ALU.mult, ALU.add))
                    elif u in (9, 10):
                        dve.wait_ge(s_sg, 1)
                        for hd in range(4 * (u - 9), 4 * (u - 8)):
                            one = dve.tensor_scalar(f3[:, hd, :], f3[:, hd, :], lbT[:, 5, hd:hd + 1],
                                                    lbT[:, 4, hd:hd + 1], ALU.mult, ALU.add)
                        one.then_inc(s_f, 1)
                    elif u == 12:
                        dve.wait_ge(s_f, 2)
                        step(dve.tensor_scalar(kx, f3, -1.0, 1.0, ALU.mult, ALU.add))

                def late(v, u):
                    if v == 5 and u < 4:
                        tt, half = divmod(u, 2)
                        dve.wait_ge(s_sq, 1)
                        dve.tensor_reduce(tiny[:, 16 * u:16 * u + 16], sq2[:, tt, half * D:(half + 1) * D]
                                          .rearrange("p (h d) -> p h d", d=SD), AX, ALU.add).then_inc(s_sum, 1)
                    elif v == 5 and u < 12:
                        hd = u - 4
                        dve.wait_ge(s_ln, 1)
                        dve.tensor_tensor_scan(f3[:, hd, :], ones[:, 0:1].to_broadcast([P, S]), cum[:, hd, :], 0.0,
                                               ALU.mult, ALU.add)
                    elif v == 5 and u == 12:
                        dve.wait_ge(s_std, 1)
                        step(dve.reciprocal(std2, std2))
                        q_std = std2.rearrange("p (t h) -> p t h", t=TT)[:, :, 0:16]
                        dve.tensor_scalar(q_std, q_std, SD ** -0.5, None, ALU.mult).then_inc(s_rstd, 1)

                loop_groups(dve, 0, split_lo, dve.tensor_copy, s_bank_v, early, late)

            @block.scalar
            def _(act):
                hi_groups(act, n_in2a, 4, lambda c: act.copy(*qf_out(1, c)).then_inc(s_bank_a, 1))

                def early(u):
                    if u == 2:
                        act.wait_ge(s_bank_v, 4)
                        act.wait_ge(s_bank_a, 4)
                        act.activation(f3, f3, ACT.Sigmoid).then_inc(s_sg, 1)
                    elif u == 5:
                        act.wait_ge(s_lm, 1)
                        act.activation(lbT[:, 0:2, :], lbT[:, 0:2, :], ACT.Exp).then_inc(s_le, 1)
                    elif u == 13:
                        act.wait_ge(s_f, 2)
                        act.activation(cum, f3, ACT.Ln).then_inc(s_ln, 1)

                def late(v, u):
                    if v == 5 and u == 6:
                        act.wait_ge(s_sum, 4)
                        act.activation(std2, tiny[:, 0:64], ACT.Sqrt, bias=eps, scale=1.0 / SD).then_inc(s_std, 1)

                loop_groups(act, 1, split_hi, act.copy, s_bank_a, early, late)

            @block.gpsimd
            def _(pool):
                level_masks(pool, lev, 7, s_lv, True)
                step = Steps(pool, s_pl)
                pool.wait_ge(s_bank_v, 12)
                pool.wait_ge(s_bank_a, 12)
                pool.tensor_tensor(sq2, qk, qk, ALU.mult).then_inc(s_sq, 1)
                pool.wait_ge(s_rstd, 1)
                pool.wait_ge(s_par, 64)
                for tt in range(TT):
                    v = qk[:, tt, :].rearrange("p (h d) -> p h d", d=SD)
                    step(pool.tensor_tensor(v, v, wide(std2[:, 32 * tt:32 * tt + 32], SD), ALU.mult))
                    step(pool.tensor_tensor(qk[:, tt, :], qk[:, tt, :], sb_gain.rearrange("p a n -> p (a n)"), ALU.mult))

        s_zero, s_d, s_e, s_z, s_m, s_p, s_dv, s_o = (
            sem("hgrn_" + n) for n in (
                "scores_zero", "exponents", "exps", "scaled", "level_product", "level_taken", "steps", "out"))
        with nc.Block() as block:
            def halves(v, s_):
                return v.rearrange("p h (b f r) -> p (h b) f r", f=2, r=s_)

            def scale_level(pool, i):
                e, q, k = (halves(v, 1 << i) for v in (Z[i % ZB], q3, kx))
                pool.tensor_tensor(e[:, :, 1, :], e[:, :, 1, :], q[:, :, 1, :], ALU.mult)
                return pool.tensor_tensor(e[:, :, 0, :], e[:, :, 0, :], k[:, :, 0, :], ALU.mult)

            @block.gpsimd
            def _(pool):
                pool.memset(sT, 0.0).then_inc(s_zero, 1)
                for i in range(8):
                    pool.wait_ge(s_e, i + 1)
                    scale_level(pool, i).then_inc(s_z, 1)

            @block.scalar
            def _(act):
                for i in range(8):
                    act.wait_ge(s_d, i + 1)
                    act.activation(Z[i % ZB], Z[i % ZB], ACT.Exp).then_inc(s_e, 1)
                act.activation(p2[:, :, D:2 * D], p2[:, :, D:2 * D], ACT.Sigmoid)
                act.activation(p2[:, :, 5 * D:7 * D], p2[:, :, 5 * D:7 * D], ACT.Sigmoid)
                act.wait_ge(s_o, 1)
                act.copy(p2[:, 1, 0:D], psf[:, 3072:4096])

            @block.vector
            def _(dve):
                step = Steps(dve, s_dv)
                def exponents(i):
                    if i >= ZB:
                        dve.wait_ge(s_m, i - ZB + 2)
                    c, e = halves(f3, 1 << i), halves(Z[i % ZB], 1 << i)
                    s_ = 1 << i
                    ref = c[:, :, 0, s_ - 1:s_].to_broadcast([P, NB // (2 * s_), s_])
                    dve.tensor_tensor(e[:, :, 1, :], c[:, :, 1, :], ref, ALU.subtract)
                    dve.tensor_tensor(e[:, :, 0, :], ref, c[:, :, 0, :], ALU.subtract).then_inc(s_d, 1)

                def take(i, mask):
                    dve.wait_ge(s_m, i + 1)
                    step(dve.copy_predicated(sT, mask.bitcast(U32).unsqueeze(1).to_broadcast([P, 2 * HH, P]),
                                             psf[:, i % 2 * 2048:(i % 2 + 1) * 2048].rearrange("p (u t) -> p u t", t=P)))
                    dve.drain().then_inc(s_p, 1)

                for i in range(ZB):
                    exponents(i)
                dve.wait_ge(s_zero, 1)
                take(0, ident)
                for i in range(7):
                    take(i + 1, lev[:, i, :])
                    if i + ZB < 8:
                        exponents(i + ZB)
                dve.wait_ge(s_m, 9)
                dve.tensor_copy(cross, psf[:, 0:1024].rearrange("p (u t) -> p u t", t=P)).then_inc(s_p, 1)
                dve.wait_ge(s_o, 1)
                dve.tensor_copy(p2[:, 0, 0:D], psf[:, 2048:3072])

            @block.tensor
            def _(pe):
                for i in range(8):
                    if i >= 2:
                        pe.wait_ge(s_p, i - 1)
                    if i:
                        pe.wait_ge(s_z, i)
                    for u in range(2 * HH):
                        hd, tt = divmod(u, TT)
                        tok_ = slice(tt * P, (tt + 1) * P)
                        k = kx[:, hd, tok_] if i == 0 else Z[(i - 1) % ZB][:, hd, tok_]
                        q = q3[:, hd, tok_] if i == 0 else k
                        mm = pe.matmul(psf[:, i % 2 * 2048 + u * P:i % 2 * 2048 + (u + 1) * P], k, q, start=True, stop=True)
                    mm.then_inc(s_m, 1)
                pe.wait_ge(s_p, 7)
                pe.wait_ge(s_z, 8)
                for hd in range(HH):
                    mm = pe.matmul(psf[:, hd * P:(hd + 1) * P], Z[7 % ZB][:, hd, 0:P], Z[7 % ZB][:, hd, P:S], start=True, stop=True)
                mm.then_inc(s_m, 1)
                pe.wait_ge(s_p, 9)
                for tt in range(TT):
                    for hd in range(HH):
                        o = psf[:, 2048 + tt * D + hd * P:2048 + tt * D + (hd + 1) * P]
                        v = [p2[:, j, hd * P:(hd + 1) * P] for j in range(TT)]
                        mm = pe.matmul(o, sT[:, hd * TT + tt, :], v[tt], start=True, stop=tt == 0)
                        if tt:
                            mm = pe.matmul(o, cross[:, hd, :], v[0], start=False, stop=True)
                mm.then_inc(s_o, 1)

        GH = 4
        GROUPS = D // SD // GH
        GW = GH * SD
        O_ZT = O_W + 2 * 2 * GH * S
        qkT = [at(O_W + i * 2 * GH * S, 2 * GH, S)[0:SD] for i in range(2)]
        zT, spl = ([at(O_ZT + (2 * n + i) * GH * 384, GH, 384) for i in range(2)] for n in range(2))
        O_OSQ = O_ZT + 4 * GH * 384
        o_sq = at(O_OSQ, TT, D)
        assert O_OSQ + TT * D <= O_L + 48
        s_osq, s_osum, s_ostd, s_oinv, s_pl = (sem("hgrn_out_" + n) for n in ("squares", "sums", "std", "inverse", "steps"))
        (s_tr, s_ev_v, s_ev_a, s_z, s_zc, s_abs, s_exp, s_ln, s_sp, s_r, s_df, s_w, s_wm, s_o, s_dv, s_oc) = (
            sem("stick_" + n) for n in (
                "transposed", "qkT_dve", "qkT_act", "scores", "scores_copied", "abs", "exp", "ln", "softplus", "sums_after",
                "log_weights", "weights", "weights_masked", "out", "steps", "out_copied"))

        with nc.Block() as block:
            @block.tensor
            def _(pe):
                def turn(j):
                    if j >= 2:
                        pe.wait_ge(s_oc, j - 1)
                    for b in range(4):
                        pairs = []
                        for u in (2 * b, 2 * b + 1):
                            col = (2 + u // GH) * D + j * GW + u % GH * SD
                            pairs += [(ps[0:SD, j % 2 * 4 + b, (u % 2) * S + tt * P:(u % 2) * S + (tt + 1) * P],
                                       p2[:, tt, col:col + SD]) for tt in range(TT)]
                        transposes(pe, pairs).then_inc(s_tr, 1)

                def scores(j):
                    pe.wait_ge(s_ev_v, 2 * j + 2)
                    pe.wait_ge(s_ev_a, 2 * j + 2)
                    for hd in range(GH):
                        b, q, k = j % 2 * 4 + hd, qkT[j % 2][:, hd, :], qkT[j % 2][:, GH + hd, :]
                        pe.matmul(ps[:, b, 0:S], k[:, 0:P], q, start=True, stop=True)
                        mm = pe.matmul(ps[:, b, S:384], k[:, P:S], q[:, P:S], start=True, stop=True)
                    mm.then_inc(s_z, 1)

                def sums(j):
                    pe.wait_ge(s_sp, j + 1)
                    for hd in range(GH):
                        b, v = j % 2 * 4 + hd, spl[j % 2]
                        pe.matmul(ps[:, b, 0:S], low, v[:, hd, 0:S], start=True, stop=False)
                        pe.matmul(ps[:, b, P:S], ones, v[:, hd, S:384], start=False, stop=True)
                        mm = pe.matmul(ps[:, b, S:384], low, v[:, hd, S:384], start=True, stop=True)
                    mm.then_inc(s_r, 1)

                def heads(j):
                    pe.wait_ge(s_wm, j + 1)
                    for tt in range(TT):
                        for hd in range(GH):
                            o = ps[:, j % 2 * 4, tt * GW + hd * SD:tt * GW + (hd + 1) * SD]
                            col = 4 * D + j * GW + hd * SD
                            for i in range(tt + 1):
                                c = S if i else tt * P
                                mm = pe.matmul(o, zT[j % 2][:, hd, c:c + P], p2[:, i, col:col + SD], start=i == 0, stop=i == tt)
                    mm.then_inc(s_o, 1)

                for j in range(2):
                    turn(j)
                    scores(j)
                for a in range(0, GROUPS, 2):
                    sums(a)
                    sums(a + 1)
                    for j in (a, a + 1):
                        heads(j)
                        if j + 2 < GROUPS:
                            turn(j + 2)
                            scores(j + 2)

            @block.vector
            def _(dve):
                step = Steps(dve, s_dv)

                def take_qk(j):
                    for b in (0, 2):
                        dve.wait_ge(s_tr, 4 * j + b + 1)
                        dve.tensor_copy(qkT[j % 2][:, 2 * b:2 * b + 2, :],
                                        ps[0:SD, j % 2 * 4 + b, :].rearrange("p (a t) -> p a t", t=S)).then_inc(s_ev_v, 1)

                def take_scores(j):
                    dve.wait_ge(s_z, j + 1)
                    dve.tensor_copy(zT[j % 2], ps[:, j % 2 * 4:j % 2 * 4 + 4, 0:384]).then_inc(s_zc, 1)

                def softplus(j):
                    dve.wait_ge(s_ln, j + 1)
                    v = spl[j % 2]
                    step(dve.scalar_tensor_tensor(out=v, in0=zT[j % 2], scalar=0.0, in1=v, op0=ALU.max, op1=ALU.add))
                    for c in (0, S):
                        one = dve.tensor_tensor(v[:, :, c:c + P], v[:, :, c:c + P],
                                                strict_up.unsqueeze(1).to_broadcast([P, GH, P]), ALU.mult)
                    one.then_inc(s_sp, 1)

                def log_weights(j):
                    dve.wait_ge(s_r, j + 1)
                    v = zT[j % 2]
                    step(dve.tensor_tensor(v, v, ps[:, j % 2 * 4:j % 2 * 4 + 4, 0:384], ALU.subtract))
                    dve.tensor_scalar(v, v, 0.0, None, ALU.min).then_inc(s_df, 1)

                def mask(j):
                    dve.wait_ge(s_w, j + 1)
                    for c in (0, S):
                        v = zT[j % 2][:, :, c:c + P]
                        one = dve.tensor_tensor(v, v, strict_up.unsqueeze(1).to_broadcast([P, GH, P]), ALU.mult)
                    one.then_inc(s_wm, 1)

                def take_heads(j):
                    dve.wait_ge(s_o, j + 1)
                    dve.tensor_copy(p2[:, :, 2 * D + j * GW:2 * D + (j + 1) * GW],
                                    ps[:, j % 2 * 4, :].rearrange("p (t n) -> p t n", t=TT)).then_inc(s_oc, 1)

                for j in range(2):
                    take_qk(j)
                    take_scores(j)
                for a in range(0, GROUPS, 2):
                    if a == 2:
                        dve.wait_ge(s_ostd, 1)
                        dve.reciprocal(tiny[:, 32:48], tiny[:, 16:32]).then_inc(s_oinv, 1)
                    for part in (softplus, log_weights, mask):
                        part(a)
                        part(a + 1)
                    if a == 0:
                        dve.wait_ge(s_osq, 1)
                        dve.tensor_reduce(tiny[:, 0:16], o_sq.rearrange("p t (h d) -> p (t h) d", d=P), AX, ALU.add)\
                            .then_inc(s_osum, 1)
                    for j in (a, a + 1):
                        take_heads(j)
                        if j + 2 < GROUPS:
                            take_qk(j + 2)
                            take_scores(j + 2)

            @block.scalar
            def _(act):
                def take_qk(j):
                    for b in (1, 3):
                        act.wait_ge(s_tr, 4 * j + b + 1)
                        act.copy(qkT[j % 2][:, 2 * b:2 * b + 2, :],
                                 ps[0:SD, j % 2 * 4 + b, :].rearrange("p (a t) -> p a t", t=S)).then_inc(s_ev_a, 1)

                def exp_part(j):
                    v = spl[j % 2]
                    act.wait_ge(s_zc, j + 1)
                    act.activation(v, zT[j % 2], ACT.Abs).then_inc(s_abs, 1)
                    act.wait_ge(s_abs, j + 1)
                    act.activation(v, v, ACT.Exp, scale=-1.0).then_inc(s_exp, 1)

                def log_part(j):
                    v = spl[j % 2]
                    act.wait_ge(s_exp, j + 1)
                    act.activation(v, v, ACT.Ln, bias=1.0).then_inc(s_ln, 1)

                def weights(j):
                    act.wait_ge(s_df, j + 1)
                    act.activation(zT[j % 2], zT[j % 2], ACT.Exp).then_inc(s_w, 1)

                for a in range(0, GROUPS, 2):
                    take_qk(a)
                    if a == 0:
                        take_qk(1)
                    exp_part(a)
                    if a > 0:
                        take_qk(a + 1)
                    exp_part(a + 1)
                    for part in (log_part, weights):
                        part(a)
                        part(a + 1)
                    if a == 0:
                        act.wait_ge(s_osum, 1)
                        act.activation(tiny[:, 16:32], tiny[:, 0:16], ACT.Sqrt, bias=eps, scale=1.0 / P).then_inc(s_ostd, 1)

            @block.gpsimd
            def _(pool):
                step = Steps(pool, s_pl)
                o = p2[:, :, 0:D]
                pool.tensor_tensor(o_sq, o, o, ALU.mult).then_inc(s_osq, 1)
                pool.wait_ge(s_osq, 1)
                for tt in range(TT):
                    step(pool.tensor_tensor(p2[:, tt, D:2 * D], hg_gain, p2[:, tt, D:2 * D], ALU.mult))
                    step(pool.tensor_tensor(o[:, tt, :], o[:, tt, :], p2[:, tt, D:2 * D], ALU.mult))
                pool.wait_ge(s_oinv, 1)
                for tt in range(TT):
                    o3 = o[:, tt, :].rearrange("p (h d) -> p h d", d=P)
                    step(pool.tensor_tensor(o3, o3, wide(tiny[:, 32 + 8 * tt:40 + 8 * tt], P), ALU.mult))

        mixed = at(O_W, TT, D)
        O_SB = O_W + 3 * D
        turn_stage("heads", p2[:, :, 0:D], p2[:, :, 2 * D:3 * D], (O_SB, O_SB + KT * S))

        def add_hg(dve, step):
            for tt in range(TT):
                step(dve.tensor_tensor(mixed[:, tt, :], product_rows(tt), p2[:, tt, 5 * D:6 * D], ALU.mult))

        def add_sb(dve, step):
            for tt in range(TT):
                step(dve.tensor_tensor(at(O_W + 2048, D), product_rows(tt, 1), p2[:, tt, 6 * D:7 * D], ALU.mult))
                step(dve.tensor_tensor(mixed[:, tt, :], mixed[:, tt, :], at(O_W + 2048, D), ALU.add))

        rows_stage("w_hg_sb", [n_hgo, n_sbo], 4, n_wo[0] + SLOTS,
                   [(x_hi, x_lo), [atr(o, KT, S) for o in (O_SB, O_SB + KT * S)]], [add_hg, add_sb])
        turn_stage("mixed_rows", mixed)

        s_xsum, s_xsq = sem("x3_rows"), sem("x3_squares")

        def add_wo(dve, step):
            for tt in range(TT):
                dve.tensor_tensor(x[:, tt, :], x[:, tt, :], product_rows(tt), ALU.add).then_inc(s_xsum, 1)

        rows_stage("w_o", [n_wo], 4, n_ffi[0] + SLOTS, [(x_hi, x_lo)], [add_wo], load_gain("norm2_gain_2"),
                   lambda act: norm_roots(act, h, x, s_xsq, s_xsum))

        norm_stage("norm2_2", h, x, s_gain, 48, roots=False)

        ff = at(O_F, FT, S)
        ff_hi, ff_lo = (Pieces([atr(O_F + i * FT * S + t * S, min(t + 2, 4), S) for t in (0,) + tuple(range(2, FT, 4))])
                        for i in (1, 2))
        s_ga, s_prod, s_fh = sem("ff_gate"), sem("ff_hidden"), sem("ff_hidden_hi")
        GA = FT // 4
        with nc.Block() as block:
            @block.sync
            def _(sp):
                st.issue(sp, n_ffo[0] + SLOTS)

            @block.tensor
            def _(pe):
                for c in range(2 * FT // 4):
                    if c >= 2:
                        if c - 2 <= GA:
                            pe.wait_ge(s_ga, c - 1)
                        if c - 2 >= GA:
                            pe.wait_ge(s_prod, c - 1 - GA)
                    product_group(pe, c, n_ffi[1] + KT * c, 0, "f", (x_hi, x_lo))

            @block.scalar
            def _(act):
                def evacuate(c):
                    if c <= GA:
                        n = 4 if c < GA else 2
                        act.activation(ff[:, 4 * c:4 * c + n, :], ps[:, c % 2 * 4:c % 2 * 4 + n, 0:S], ACT.Silu)\
                            .then_inc(s_ga, 1)
                    if c > GA:
                        high(c - 1)

                def high(c):
                    act.wait_ge(s_prod, c - GA + 1)
                    n, skip = (4, 0) if c > GA else (2, 2)
                    t = 4 * c + skip - FT
                    act.copy(ff_hi.piece(t), ff[:, t:t + n, :]).then_inc(s_fh, 1)

                hi_groups(act, n_ffi, 2 * FT // 4, evacuate)
                high(2 * FT // 4 - 1)

            @block.vector
            def _(dve):
                def tiles(c):
                    n, skip = (4, 0) if c > GA else (2, 2)
                    return 4 * c + skip - FT, n, skip

                def evacuate(c):
                    if c < GA:
                        return
                    t, n, skip = tiles(c)
                    dve.wait_ge(s_ga, GA + 1)
                    dve.tensor_tensor(ff[:, t:t + n, :], ff[:, t:t + n, :],
                                      ps[:, c % 2 * 4 + skip:c % 2 * 4 + skip + n, 0:S], ALU.mult).then_inc(s_prod, 1)
                    if c > GA:
                        low_part(c - 1)

                def low_part(c):
                    t, n, _ = tiles(c)
                    dve.wait_ge(s_fh, c - GA + 1)
                    dve.tensor_tensor(ff_lo.piece(t), ff[:, t:t + n, :], ff_hi.piece(t).bitcast(F32),
                                      ALU.subtract)

                lo_groups(dve, n_ffi, 2 * FT // 4, evacuate)
                low_part(2 * FT // 4 - 1)

        s_res, s_out = sem("result"), sem("stored")

        def add_ff(dve, step):
            for tt in range(TT):
                dve.tensor_tensor(x[:, tt, :], x[:, tt, :], product_rows(tt), ALU.add).then_inc(s_res, 1)

        rows_stage("w_ffn_out", [n_ffo], 11, n_ffo[0] + 11, [(ff_hi, ff_lo)], [add_ff])
        with nc.Block() as block:
            @block.sync
            def _(sp):
                sp.wait_ge(s_res, TT)
                sp.dma_start(out[0].rearrange("(t p) d -> p t d", p=P), x).then_inc(s_out, 16)
                sp.wait_ge(s_out, 16)


NAMES = ["x", "c", "w_ada", "b_ada", "norm1_gain", "w_in", "attn_q_gain", "attn_k_gain", "attn_rel_bias",
         "attn_out_gain", "dn_conv_w", "dn_a_log", "dn_dt_bias", "dn_out_gain", "w_out", "norm2_gain",
         "peer_w_query", "peer_query_gain", "peer_sub_keys_1", "peer_sub_keys_2", "peer_expert_down",
         "peer_expert_up", "norm1_gain_2", "w_in_2", "lb_logits_2", "hg_out_norm_2", "sb_q_norm_2",
         "sb_k_norm_2", "w_hg_out_2", "w_sb_out_2", "w_o_2", "norm2_gain_2", "w_ffn_in_2", "w_ffn_out_2"]


def kernel(**inputs):
    import numpy as np
    import concourse.bacc as bacc
    from concourse.bass_utils import run_bass_kernel_spmd

    nc = bacc.Bacc("TRN2", target_bir_lowering=False, num_devices=1)
    arrays, A = {}, {}
    for name in NAMES:
        a = np.ascontiguousarray(inputs[name])
        arrays[f"in_{name}"] = a
        A[name] = nc.dram_tensor(f"in_{name}", a.shape, mybir.dt.from_np(a.dtype), kind="ExternalInput").ap()
    out = nc.dram_tensor("out", (1, S, D), F32, kind="ExternalOutput").ap()
    build(nc, A, out)
    r = run_bass_kernel_spmd(nc, [arrays], core_ids=[0])
    return r.results[0]["out"]
```
